# Optimizing a Trainium2 kernel written in Bass

```python
import jax
import jax.numpy as jnp
from jax import lax
import numpy as np

D_MODEL = 1024
BATCH = 1
SEQ = 512
DEPTH = 1

ATT_HEADS = 8
ATT_KV_HEADS = 2
ATT_HEAD_DIM = 64
ATT_GROUP = ATT_HEADS // ATT_KV_HEADS
ATT_WIDTH = ATT_HEADS * ATT_HEAD_DIM
ATT_KV_WIDTH = ATT_KV_HEADS * ATT_HEAD_DIM
WINDOW = 128
ATT_BLOCK = 128
DN_HEADS = 4
DN_HEAD_DIM = 128
DN_WIDTH = DN_HEADS * DN_HEAD_DIM
CONV_WIDTH = 4
DN_CHUNK = 64
D_MIX = ATT_WIDTH + DN_WIDTH
IN_SPLITS = (ATT_WIDTH, ATT_KV_WIDTH, ATT_KV_WIDTH, 3 * DN_WIDTH, DN_HEADS, DN_HEADS, DN_WIDTH)
D_IN_PROJ = ATT_WIDTH + 2 * ATT_KV_WIDTH + 4 * DN_WIDTH + 2 * DN_HEADS
PEER_HEADS = 8
N_KEYS = 128
N_EXPERTS = N_KEYS * N_KEYS
PEER_QDIM = 128
PEER_HALF = PEER_QDIM // 2
PEER_TOPK = 16
PEER_TOKEN_BLOCK = 128
EPS = 1e-6

kernel_name = "hybrid_swa_sink_gdn_peer_block"

def rms_norm(x, g):
    xf = x.astype(jnp.float32)
    y = xf * lax.rsqrt(jnp.mean(xf * xf, axis=-1, keepdims=True) + EPS)
    return (y * g.astype(jnp.float32)).astype(x.dtype)

def l2norm(x):
    return x * lax.rsqrt(jnp.sum(x * x, axis=-1, keepdims=True) + EPS)

def sliding_window_sink_attention(q, k, v, sinks):
    B, S = q.shape[0], q.shape[1]
    nb = S // ATT_BLOCK
    f32 = jnp.float32
    qb = q.reshape(B, nb, ATT_BLOCK, ATT_KV_HEADS, ATT_GROUP, ATT_HEAD_DIM).astype(f32)

    def band(t):
        tb = t.reshape(B, nb, ATT_BLOCK, ATT_KV_HEADS, ATT_HEAD_DIM).astype(f32)
        prev = jnp.pad(tb[:, :-1], ((0, 0), (1, 0), (0, 0), (0, 0), (0, 0)))
        return jnp.concatenate([prev, tb], axis=2)

    kb, vb = band(k), band(v)
    s = jnp.einsum('bnqhgd,bnkhd->bnhgqk', qb, kb) * (ATT_HEAD_DIM ** -0.5)
    qi = jnp.arange(ATT_BLOCK)[:, None]
    kj = jnp.arange(2 * ATT_BLOCK)[None, :]
    rel = qi + ATT_BLOCK - kj
    in_window = (rel >= 0) & (rel < WINDOW)
    key_exists = (jnp.arange(nb)[:, None, None] > 0) | (kj[None] >= ATT_BLOCK)
    mask = in_window[None] & key_exists
    s = jnp.where(mask[None, :, None, None], s, -jnp.inf)
    sink = sinks.astype(f32).reshape(ATT_KV_HEADS, ATT_GROUP)[None, None, :, :, None, None]
    m = jnp.maximum(jnp.max(s, axis=-1, keepdims=True), sink)
    p = jnp.exp(s - m)
    denom = jnp.sum(p, axis=-1, keepdims=True) + jnp.exp(sink - m)
    o = jnp.einsum('bnhgqk,bnkhd->bnqhgd', p / denom, vb)
    return o.reshape(B, S, ATT_WIDTH)

def causal_conv_silu(x, w):
    S = x.shape[1]
    xp = jnp.pad(x, ((0, 0), (CONV_WIDTH - 1, 0), (0, 0)))
    y = sum(xp[:, j:j + S] * w[j] for j in range(CONV_WIDTH))
    return jax.nn.silu(y)

def gated_delta_rule(q, k, v, g, beta):
    B, S, H, D = q.shape
    C = DN_CHUNK
    nc = S // C
    f32 = jnp.float32

    def chunks(t):
        return t.reshape(B, nc, C, H, D).transpose(0, 3, 1, 2, 4)

    q, k, v = chunks(q), chunks(k), chunks(v)
    g = g.reshape(B, nc, C, H).transpose(0, 3, 1, 2)
    beta = beta.reshape(B, nc, C, H).transpose(0, 3, 1, 2)
    gc = jnp.cumsum(g, axis=-1)
    causal = jnp.tril(jnp.ones((C, C), dtype=bool))
    strict = jnp.tril(jnp.ones((C, C), dtype=bool), k=-1)
    diff = gc[..., :, None] - gc[..., None, :]
    decay_mat = jnp.where(causal, jnp.exp(jnp.where(causal, diff, 0.0)), 0.0)
    kb = k * beta[..., None]
    m_low = jnp.where(strict, jnp.einsum('bhncd,bhnjd->bhncj', kb, k) * decay_mat, 0.0)
    a_mat = m_low + jnp.eye(C, dtype=f32)
    rhs = jnp.concatenate([v * beta[..., None], kb * jnp.exp(gc)[..., None]], axis=-1)
    sol = lax.linalg.triangular_solve(a_mat, rhs, left_side=True, lower=True, unit_diagonal=True)
    u, w = sol[..., :D], sol[..., D:]
    qk = jnp.where(causal, jnp.einsum('bhncd,bhnjd->bhncj', q, k) * decay_mat, 0.0)
    q_dec = q * jnp.exp(gc)[..., None]
    k_dec = k * jnp.exp(gc[..., -1:] - gc)[..., None]
    chunk_decay = jnp.exp(gc[..., -1])

    def step(state, inp):
        u_c, w_c, qk_c, qd_c, kd_c, cd_c = inp
        v_new = u_c - jnp.einsum('bhcd,bhde->bhce', w_c, state)
        o_c = jnp.einsum('bhcd,bhde->bhce', qd_c, state) + jnp.einsum('bhcj,bhje->bhce', qk_c, v_new)
        state = state * cd_c[..., None, None] + jnp.einsum('bhcd,bhce->bhde', kd_c, v_new)
        return state, o_c

    xs = tuple(jnp.moveaxis(t, 2, 0) for t in (u, w, qk, q_dec, k_dec, chunk_decay))
    init = jnp.zeros((B, H, D, D), dtype=f32)
    _, o = lax.scan(step, init, xs)
    return o.transpose(1, 0, 3, 2, 4).reshape(B, S, H, D)

def peer(xn, w_q, sub_keys, u_tab, v_tab):
    B, S, D = xn.shape
    T = B * S
    xt = xn.reshape(T, D)
    q = (xt @ w_q).reshape(T, PEER_HEADS, 2, PEER_HALF)
    s = jnp.einsum('thpc,hpnc->thpn', q, sub_keys)
    s_top, i_top = lax.top_k(s, PEER_TOPK)
    cand_s = (s_top[:, :, 0, :, None] + s_top[:, :, 1, None, :]).reshape(T, PEER_HEADS, PEER_TOPK * PEER_TOPK)
    cand_i = (i_top[:, :, 0, :, None] * N_KEYS + i_top[:, :, 1, None, :]).reshape(T, PEER_HEADS, PEER_TOPK * PEER_TOPK)
    best_s, pos = lax.top_k(cand_s, PEER_TOPK)
    idx = jnp.take_along_axis(cand_i, pos, axis=-1)
    gate = jax.nn.softmax(best_s.astype(jnp.float32), axis=-1).astype(xn.dtype)
    nblk = T // PEER_TOKEN_BLOCK
    hk = PEER_HEADS * PEER_TOPK

    def block(args):
        xb, ib, gb = args
        act = jax.nn.gelu(jnp.einsum('tkd,td->tk', u_tab[ib], xb), approximate=False)
        return jnp.einsum('tk,tkd->td', act * gb, v_tab[ib])

    out = lax.map(block, (xt.reshape(nblk, PEER_TOKEN_BLOCK, D),
                          idx.reshape(nblk, PEER_TOKEN_BLOCK, hk),
                          gate.reshape(nblk, PEER_TOKEN_BLOCK, hk)))
    return out.reshape(B, S, D)

def hybrid_layer(h, norm_mix_g, w_in, att_q_norm_g, att_k_norm_g, att_sinks, att_out_norm_g,
                 dn_conv_w, dn_a_log, dn_dt_bias, dn_out_norm_g, w_out, norm_ffn_g,
                 peer_w_q, peer_sub_keys, peer_u, peer_v):
    B, S, _ = h.shape
    f32 = jnp.float32
    xn = rms_norm(h, norm_mix_g)
    proj = xn @ w_in
    offs = []
    acc = 0
    for width in IN_SPLITS[:-1]:
        acc += width
        offs.append(acc)
    q_a, k_a, v_a, qkv_d, a_d, b_d, z_d = jnp.split(proj, offs, axis=-1)

    q_a = rms_norm(q_a.reshape(B, S, ATT_HEADS, ATT_HEAD_DIM), att_q_norm_g)
    k_a = rms_norm(k_a.reshape(B, S, ATT_KV_HEADS, ATT_HEAD_DIM), att_k_norm_g)
    v_a = v_a.reshape(B, S, ATT_KV_HEADS, ATT_HEAD_DIM)
    att = sliding_window_sink_attention(q_a, k_a, v_a, att_sinks).astype(h.dtype)
    att = rms_norm(att, att_out_norm_g)

    qkv = causal_conv_silu(qkv_d.astype(f32), dn_conv_w.astype(f32))
    q_d, k_d, v_d = jnp.split(qkv, 3, axis=-1)
    shp = (B, S, DN_HEADS, DN_HEAD_DIM)
    q_d = l2norm(q_d.reshape(shp)) * (DN_HEAD_DIM ** -0.5)
    k_d = l2norm(k_d.reshape(shp))
    v_d = v_d.reshape(shp)
    g = -jnp.exp(dn_a_log.astype(f32)) * jax.nn.softplus(a_d.astype(f32) + dn_dt_bias.astype(f32))
    beta = jax.nn.sigmoid(b_d.astype(f32))
    o = gated_delta_rule(q_d, k_d, v_d, g, beta)
    o = rms_norm(o, dn_out_norm_g) * jax.nn.silu(z_d.astype(f32).reshape(shp))
    dn = o.reshape(B, S, DN_WIDTH).astype(h.dtype)

    h = h + jnp.concatenate([att, dn], axis=-1) @ w_out
    h = h + peer(rms_norm(h, norm_ffn_g), peer_w_q, peer_sub_keys, peer_u, peer_v)
    return h

def setup_inputs(seed: int = 0) -> dict:
    key = jax.random.key(seed)
    ks = jax.random.split(key, 20)
    L = DEPTH
    nrm = jax.random.normal
    dt = jnp.exp(jax.random.uniform(ks[9], (L, DN_HEADS), minval=jnp.log(1e-3), maxval=jnp.log(1e-1)))
    return {
        "x": nrm(ks[0], (BATCH, SEQ, D_MODEL), jnp.float32),
        "norm_mix_g": 1.0 + 0.02 * nrm(ks[1], (L, D_MODEL), jnp.float32),
        "w_in": nrm(ks[2], (L, D_MODEL, D_IN_PROJ), jnp.float32) * D_MODEL ** -0.5,
        "att_q_norm_g": 1.0 + 0.02 * nrm(ks[3], (L, ATT_HEAD_DIM), jnp.float32),
        "att_k_norm_g": 1.0 + 0.02 * nrm(ks[4], (L, ATT_HEAD_DIM), jnp.float32),
        "att_sinks": nrm(ks[5], (L, ATT_HEADS), jnp.float32),
        "att_out_norm_g": 1.0 + 0.02 * nrm(ks[6], (L, ATT_WIDTH), jnp.float32),
        "dn_conv_w": nrm(ks[7], (L, CONV_WIDTH, 3 * DN_WIDTH), jnp.float32) * CONV_WIDTH ** -0.5,
        "dn_a_log": jnp.log(jax.random.uniform(ks[8], (L, DN_HEADS), minval=1.0, maxval=16.0)),
        "dn_dt_bias": dt + jnp.log(-jnp.expm1(-dt)),
        "dn_out_norm_g": 1.0 + 0.02 * nrm(ks[10], (L, DN_HEAD_DIM), jnp.float32),
        "w_out": nrm(ks[11], (L, D_MIX, D_MODEL), jnp.float32) * D_MIX ** -0.5,
        "norm_ffn_g": 1.0 + 0.02 * nrm(ks[12], (L, D_MODEL), jnp.float32),
        "peer_w_q": nrm(ks[13], (L, D_MODEL, PEER_HEADS * PEER_QDIM), jnp.float32) * D_MODEL ** -0.5,
        "peer_sub_keys": nrm(ks[14], (L, PEER_HEADS, 2, N_KEYS, PEER_HALF), jnp.float32) * PEER_HALF ** -0.5,
        "peer_u": nrm(ks[15], (L, N_EXPERTS, D_MODEL), jnp.float32) * D_MODEL ** -0.5,
        "peer_v": nrm(ks[16], (L, N_EXPERTS, D_MODEL), jnp.float32) * D_MODEL ** -0.5,
    }

def reference(x, norm_mix_g, w_in, att_q_norm_g, att_k_norm_g, att_sinks, att_out_norm_g,
              dn_conv_w, dn_a_log, dn_dt_bias, dn_out_norm_g, w_out, norm_ffn_g,
              peer_w_q, peer_sub_keys, peer_u, peer_v):
    h = x
    for l in range(DEPTH):
        h = hybrid_layer(h, norm_mix_g[l], w_in[l], att_q_norm_g[l], att_k_norm_g[l], att_sinks[l],
                         att_out_norm_g[l], dn_conv_w[l], dn_a_log[l], dn_dt_bias[l], dn_out_norm_g[l],
                         w_out[l], norm_ffn_g[l], peer_w_q[l], peer_sub_keys[l], peer_u[l], peer_v[l])
    return h


_drawn_inputs = setup_inputs


def setup_inputs(seed=0):
    import zlib

    import numpy as np

    out = dict(_drawn_inputs(seed))
    spreads = {}
    factors = {'att_q_norm_g': 4.441,
     'att_k_norm_g': 5.587,
     'att_sinks': 3.416,
     'att_out_norm_g': 4.938,
     'dn_out_norm_g': 7.314,
     'norm_ffn_g': 8.0,
     'peer_w_q': 4.865,
     'peer_sub_keys': 4.872,
     'peer_u': 5.362,
     'peer_v': 4.868}
    for name, (base, spread) in spreads.items():
        noise = np.random.default_rng([zlib.crc32(name.encode()), seed]).standard_normal(out[name].shape)
        drawn = base * np.exp(spread * noise) if base else spread * noise
        out[name] = jnp.asarray(drawn.astype(out[name].dtype))
    for name, factor in factors.items():
        out[name] = (out[name] * factor).astype(out[name].dtype)
    return out
```

```python
from contextlib import ExitStack

import concourse.bass as bass
from concourse import mybir

P = 128
T = 512
TB = T // P
D = 1024
KD = D // P
EPS = 1e-6

HD = 64
NH = 8
NKV = 2
GRP = NH // NKV
ATT = NH * HD
KVW = NKV * HD

DH = 128
DN = 4
DNW = DN * DH
TAPS = 4
CH = 64
CT = 3 * DN

W_TOK = ATT + 2 * KVW
W_CONV0 = W_TOK
W_AB0 = W_CONV0 + 3 * DNW
W_Z0 = W_AB0 + 2 * DN
W_END = W_Z0 + DNW

PH = 8
NK = 128
HALF = 64
TOPK = 16
HA = PH * TOPK
PAIRS = [(0, 1, 16), (1, 1, 8), (2, 1, 5), (3, 1, 4), (4, 1, 3), (5, 3, 2), (8, 8, 1)]
NPAIR = sum(r * w for _, r, w in PAIRS)

GT = 4
NG = NK // GT
BIG = 3.0e38

F32 = mybir.dt.float32
F32R = mybir.dt.float32r
U32 = mybir.dt.uint32
ALU = mybir.AluOpType
ACT = mybir.ActivationFunctionType
AX = mybir.AxisListType.X


def chain(eng, sem, count):
    def link(ins):
        count[0] += 1
        ins.then_inc(sem, 1)
        eng.wait_ge(sem, count[0])
    return link


class Banks:

    def __init__(self, banks, done, taken):
        self.banks, self.done, self.taken = banks, done, taken
        self.names, self.consumer = [], []

    def add(self, name, consumer):
        self.names.append(name)
        self.consumer.append(consumer)

    def n(self, name):
        return self.names.index(name)

    def bank(self, name):
        return self.banks[self.n(name) % len(self.banks)]

    def rank(self, n):
        return self.consumer[:n + 1].count(self.consumer[n])

    def wait_free(self, pe, name):
        n = self.n(name) - len(self.banks)
        if n >= 0:
            pe.wait_ge(self.taken[self.consumer[n]], self.rank(n))

    def wait_full(self, eng, name):
        eng.wait_ge(self.done, self.n(name) + 1)

    def wait_taken(self, eng, name):
        n = self.n(name)
        eng.wait_ge(self.taken[self.consumer[n]], self.rank(n))


class Tensors:
    pass


class Memory:

    def __init__(self, nc):
        self.nc, self.live = nc, {}

    def take(self, name, shape, dt=F32):
        size = 4
        for n in shape[1:]:
            size *= n
        size = -(-size // 64) * 64
        at = -(-self.nc.sbuf_base // 64) * 64
        for a, b in sorted(self.live.values()):
            if a - at >= size:
                break
            at = max(at, b)
        assert at + size <= self.nc.sbuf_usable_end, (name, at, size, self.live)
        self.live[name] = (at, at + size)
        return self.nc.alloc_sbuf_tensor_at(name, shape, dt, offset=at)

    def drop(self, *names):
        for name in names:
            del self.live[name]

    def local(self, ctx):
        def sb(name, shape, dt=F32):
            t = self.take(name, shape, dt)
            ctx.callback(self.drop, name)
            return t
        return sb


def constants(nc, m, sem):
    made = sem("masks_made")
    with nc.Block() as block:
        @block.gpsimd
        def _(pool):
            link = chain(pool, made, [0])
            nc.gpsimd.memset(m.ident[:], 0.0)
            nc.gpsimd.memset(m.upper[:], 0.0)
            nc.gpsimd.memset(m.lower[:], 0.0)
            nc.gpsimd.memset(m.chunk_ones[:], 0.0)
            nc.gpsimd.memset(m.convin[:, :, 0:TAPS - 1], 0.0)
            nc.gpsimd.memset(m.neg_half[:], -0.5)
            nc.gpsimd.memset(m.att_mask[:], 0.0)
            link(nc.gpsimd.memset(m.blockdiag[:], 1.0))
            for q in range(P // CH):
                a = slice(q * CH, (q + 1) * CH)
                nc.gpsimd.memset(m.upper[a, a], 1.0)
                nc.gpsimd.memset(m.lower[a, a], 1.0)
                link(nc.gpsimd.memset(m.chunk_ones[a, a], 1.0))
            nc.gpsimd.affine_select(out=m.ident[:], in_=m.ident[:], compare_op=ALU.not_equal, fill=1.0,
                                    base=0, pattern=[[-1, P]], channel_multiplier=1)
            nc.gpsimd.affine_select(out=m.upper[:], in_=m.upper[:], compare_op=ALU.is_ge, fill=0.0,
                                    base=0, pattern=[[1, P]], channel_multiplier=-1)
            nc.gpsimd.affine_select(out=m.lower[:], in_=m.lower[:], compare_op=ALU.is_gt, fill=0.0,
                                    base=0, pattern=[[-1, P]], channel_multiplier=1)
            nc.gpsimd.affine_select(out=m.att_mask[:, 0:P], in_=m.att_mask[:, 0:P], compare_op=ALU.is_gt,
                                    fill=-1e30, base=0, pattern=[[1, P]], channel_multiplier=-1)
            nc.gpsimd.affine_select(out=m.att_mask[:, P:2 * P], in_=m.att_mask[:, P:2 * P],
                                    compare_op=ALU.is_ge, fill=-1e30, base=0, pattern=[[-1, P]],
                                    channel_multiplier=1)
            for l in range(6):
                s = 1 << l
                v = m.blockdiag[:, l, :].rearrange("p (b r) -> p b r", r=s)
                link(nc.gpsimd.affine_select(out=v, in_=v, compare_op=ALU.is_ge, fill=0.0, base=0,
                                             pattern=[[-s, P // s], [0, s]], channel_multiplier=1))
                link(nc.gpsimd.affine_select(out=v, in_=v, compare_op=ALU.is_ge, fill=0.0, base=s - 1,
                                             pattern=[[s, P // s], [0, s]], channel_multiplier=-1))
            for l in range(6):
                above = m.blockdiag[:, l + 1, :] if l < 5 else m.chunk_ones[:]
                nc.gpsimd.tensor_tensor(m.levels[:, l, :], above, m.blockdiag[:, l, :], ALU.subtract)


def input_projection(nc, m, ps, sem, x, norm_mix_g, w_in):
    x_in = [sem(f"x_in{b}") for b in range(TB)]
    g_in = sem("mix_gain_in")
    w_cols = [(W_CONV0 + 512 * c, 512) for c in range(3)] + [(0, 512), (512, W_TOK - 512),
                                                            (W_AB0, W_END - W_AB0)]
    w_ld = [sem(f"w_in{i}") for i in range(len(w_cols))]
    squares, scale, normed, done = sem("x_squares"), sem("x_scale"), sem("x_normed"), sem("proj_done")
    plink, vlink = sem("proj_pool"), sem("proj_dve")
    banks = Banks(ps, done, {"act": sem("proj_act"), "dve": sem("proj_vec")})
    for b in range(TB):
        for half in range(2):
            banks.add(("xT", b, half), "act")
    for c in range(3):
        for i in range(4):
            banks.add(("conv", c, i), "dve" if i % 2 else "act")
    for b in range(TB):
        banks.add(("tok0", b), "act")
    for b in range(TB):
        banks.add(("tok1", b), "dve")
    for b in range(TB):
        banks.add(("ab", b), "act")
        banks.add(("z", b), "dve")
    wview = w_in[0].rearrange("(k p) n -> p k n", p=P)
    last = [("conv", c, 3) for c in range(3)] + [("tok0", TB - 1), ("tok1", TB - 1), ("z", TB - 1)]

    with ExitStack() as ctx:
        sb = m.mem.local(ctx)
        gain = sb("mix_gain", [P, D])
        xn = sb("xn", [P, 2, D])
        junk = sb("x_junk", [P, D])
        xnT = sb("xnT", [P, KD, T])
        wbuf = sb("wbuf", [P, 3, KD, 520])
        ss = sb("x_ss", [P, TB])
        with nc.Block() as block:
            @block.sync
            def _(sp):
                xv = x[0].rearrange("(b p) d -> b p d", p=P)
                for b in range(TB):
                    sp.dma_start(m.acc[:, b, :], xv[b]).then_inc(x_in[b], 16)
                sp.dma_start(gain[:], norm_mix_g[0:1, :].broadcast_to([P, D])).then_inc(g_in, 16)
                for i, (c0, n) in enumerate(w_cols):
                    if i >= 3:
                        sp.wait_ge(done, banks.n(last[i - 3]) + 1)
                    sp.dma_start(wbuf[:, i % 3, :, 0:n], wview[:, :, c0:c0 + n]).then_inc(w_ld[i], 16)

            @block.gpsimd
            def _(pool):
                link = chain(pool, plink, [0])
                for b in range(TB):
                    pool.wait_ge(squares, b + 1)
                    link(nc.gpsimd.tensor_scalar(ss[:, b:b + 1], ss[:, b:b + 1], 1.0 / D, EPS, ALU.mult, ALU.add))
                    nc.gpsimd.tensor_tensor(ss[:, b:b + 1], ss[:, b:b + 1], m.neg_half[:, 0:1],
                                            ALU.pow).then_inc(scale, 1)

            @block.scalar
            def _(act):
                for b in range(TB):
                    act.wait_ge(x_in[b], 16)
                    if b:
                        act.wait_ge(squares, b)
                    nc.scalar.activation(junk[:], m.acc[:, b, :], ACT.Square,
                                         accum_out=ss[:, b:b + 1]).then_inc(squares, 1)
                for b in range(TB):
                    for half in range(2):
                        g = ("xT", b, half)
                        banks.wait_full(act, g)
                        nc.scalar.activation(xnT[:, 4 * half:4 * half + 4, b * P:(b + 1) * P],
                                             banks.bank(g)[:].rearrange("p (k t) -> p k t", k=4),
                                             ACT.Copy).then_inc(banks.taken["act"], 1)
                for c in range(3):
                    for i in (0, 2):
                        g = ("conv", c, i)
                        banks.wait_full(act, g)
                        nc.scalar.activation(m.convin[:, 4 * c + i, TAPS - 1:], banks.bank(g)[:],
                                             ACT.Copy).then_inc(banks.taken["act"], 1)
                for b in range(TB):
                    banks.wait_full(act, ("tok0", b))
                    nc.scalar.activation(m.qa[:, b, :], banks.bank(("tok0", b))[:],
                                         ACT.Copy).then_inc(banks.taken["act"], 1)
                for b in range(TB):
                    banks.wait_full(act, ("ab", b))
                    nc.scalar.activation(m.ab[:, b, :], banks.bank(("ab", b))[:, 0:2 * DN],
                                         ACT.Copy).then_inc(banks.taken["act"], 1)

            @block.vector
            def _(dve):
                dve.wait_ge(g_in, 16)
                for b in range(TB):
                    dve.wait_ge(scale, b + 1)
                    if b >= 2:
                        dve.wait_ge(done, 2 * (b - 1))
                    nc.vector.scalar_tensor_tensor(xn[:, b % 2, :], m.acc[:, b, :], ss[:, b:b + 1], gain[:],
                                                   ALU.mult, ALU.mult).then_inc(normed, 1)
                for c in range(3):
                    for i in (1, 3):
                        g = ("conv", c, i)
                        banks.wait_full(dve, g)
                        nc.vector.tensor_copy(m.convin[:, 4 * c + i, TAPS - 1:],
                                              banks.bank(g)[:]).then_inc(banks.taken["dve"], 1)
                for b in range(TB):
                    banks.wait_full(dve, ("tok1", b))
                    nc.vector.tensor_copy(m.kva[:, b, :], banks.bank(("tok1", b))[:, 0:2 * KVW]
                                          ).then_inc(banks.taken["dve"], 1)
                for b in range(TB):
                    banks.wait_full(dve, ("z", b))
                    nc.vector.tensor_copy(m.z[:, b, :], banks.bank(("z", b))[:]).then_inc(banks.taken["dve"], 1)

            @block.tensor
            def _(pe):
                for b in range(TB):
                    pe.wait_ge(normed, b + 1)
                    for half in range(2):
                        g = ("xT", b, half)
                        for k in range(4):
                            kk = 4 * half + k
                            t = nc.tensor.transpose(banks.bank(g)[:, k * P:(k + 1) * P],
                                                    xn[:, b % 2, kk * P:(kk + 1) * P], m.ident[:])
                        t.then_inc(done, 1)
                banks.wait_taken(pe, ("xT", TB - 1, 1))
                for c in range(3):
                    pe.wait_ge(w_ld[c], 16)
                    for i in range(4):
                        g = ("conv", c, i)
                        banks.wait_free(pe, g)
                        for k in range(KD):
                            t = nc.tensor.matmul(banks.bank(g)[:], wbuf[:, c, k, i * P:(i + 1) * P], xnT[:, k, :],
                                                 start=(k == 0), stop=(k == KD - 1))
                        t.then_inc(done, 1)

                def by_token(g, b, slot, c0, n):
                    banks.wait_free(pe, g)
                    for k in range(KD):
                        t = nc.tensor.matmul(banks.bank(g)[:, 0:n], xnT[:, k, b * P:(b + 1) * P],
                                             wbuf[:, slot, k, c0:c0 + n], start=(k == 0), stop=(k == KD - 1))
                    t.then_inc(done, 1)

                pe.wait_ge(w_ld[3], 16)
                for b in range(TB):
                    by_token(("tok0", b), b, 0, 0, 512)
                pe.wait_ge(w_ld[4], 16)
                for b in range(TB):
                    by_token(("tok1", b), b, 1, 0, W_TOK - 512)
                pe.wait_ge(w_ld[5], 16)
                for b in range(TB):
                    by_token(("ab", b), b, 2, 0, 2 * DN)
                    by_token(("z", b), b, 2, 2 * DN, DNW)


def conv_and_norms(nc, m, ps, sem, conv_w, a_log, dt_bias, q_norm_g, k_norm_g):
    small_in = [sem(f"small_in{i}") for i in range(5)]
    convd, silud, done = sem("conv_done"), sem("silu_done"), sem("norms_done")
    squared, summed, scaled = sem("qk_squared"), sem("qk_summed"), sem("qk_scaled")
    unit, att_sq, att_pow, att_unit = sem("qk_unit"), sem("att_squares"), sem("att_pow"), sem("att_unit")
    z1, z2, z3, b2 = sem("gate_z"), sem("gate_softplus"), sem("gate_alog"), sem("gate_beta")
    plink, vlink, alink = sem("norms_pool"), sem("norms_dve"), sem("norms_act")
    banks = Banks(ps, done, {"act": sem("norms_by_act"), "dve": sem("norms_by_dve")})
    for c in range(CT):
        banks.add(("tok", c), "act")
    for b in range(TB):
        banks.add(("attq", b), "dve")
        banks.add(("attk", b), "dve")
    for c in range(2 * DN):
        banks.add(("unitT", c), "act")

    with ExitStack() as ctx:
        sb = m.mem.local(ctx)
        wconv = sb("wconv", [P, TAPS, CT])
        convT = sb("convT", [P, CT, T])
        sq = sb("qk_sq", [P, 2 * DN, T])
        ssd = sb("qk_ss", [P, 2 * DN, TB])
        att_sqr = sb("att_sqr", [P, TB, ATT + KVW])
        ssa = sb("att_ss", [P, TB, NH + NKV])
        qg = sb("att_qg", [P, HD])
        kg = sb("att_kg", [P, HD])
        alog = sb("alog", [P, DN])
        dtb = sb("dtb", [P, DN])
        zz = sb("gate_zz", [P, TB, DN])
        za = sb("gate_za", [P, TB, DN])
        eb = sb("gate_eb", [P, TB, DN])
        qn = sb("att_qn", [P, TB, ATT])
        kn = sb("att_kn", [P, TB, KVW])
        with nc.Block() as block:
            @block.sync
            def _(sp):
                sp.dma_start(wconv[:].rearrange("p j c -> p (j c)"), conv_w).then_inc(small_in[0], 16)
                sp.dma_start(alog[:], a_log[0:1, :].broadcast_to([P, DN])).then_inc(small_in[1], 16)
                sp.dma_start(dtb[:], dt_bias[0:1, :].broadcast_to([P, DN])).then_inc(small_in[2], 16)
                sp.dma_start(qg[:], q_norm_g[0:1, :].broadcast_to([P, HD])).then_inc(small_in[3], 16)
                sp.dma_start(kg[:], k_norm_g[0:1, :].broadcast_to([P, HD])).then_inc(small_in[4], 16)

            @block.vector
            def _(dve):
                link = chain(dve, vlink, [0])
                dve.wait_ge(small_in[2], 16)
                nc.vector.tensor_tensor(zz[:], m.ab[:, :, 0:DN], dtb[:].unsqueeze(1).broadcast_to([P, TB, DN]),
                                        ALU.add).then_inc(z1, 1)
                nc.vector.tensor_tensor(att_sqr[:, :, 0:ATT], m.qa[:], m.qa[:], ALU.mult)
                link(nc.vector.tensor_tensor(att_sqr[:, :, ATT:], m.kva[:, :, 0:KVW], m.kva[:, :, 0:KVW], ALU.mult))
                for b in range(TB):
                    t = nc.vector.tensor_reduce(ssa[:, b, :], att_sqr[:, b, :].rearrange("p (h d) -> p h d", d=HD),
                                                AX, ALU.add)
                t.then_inc(att_sq, 1)
                dve.wait_ge(small_in[0], 16)
                for c0 in range(0, CT, 4):
                    for j in range(TAPS):
                        for c in range(c0, c0 + 4):
                            w = wconv[:, j, c:c + 1]
                            if j == 0:
                                t = nc.vector.tensor_scalar(convT[:, c, :], m.convin[:, c, 0:T], w, None, ALU.mult)
                            else:
                                t = nc.vector.scalar_tensor_tensor(convT[:, c, :], m.convin[:, c, j:j + T], w,
                                                                   convT[:, c, :], ALU.mult, ALU.add)
                        if j < TAPS - 1:
                            link(t)
                    t.then_inc(convd, 1)
                dve.wait_ge(att_pow, 1)
                dve.wait_ge(small_in[3], 16)
                dve.wait_ge(small_in[4], 16)
                for b in range(TB):
                    qv = qn[:, b, :].rearrange("p (g v d) -> p v g d", v=NKV, g=GRP)
                    kv = kn[:, b, :].rearrange("p (h d) -> p h d", d=HD)
                    nc.vector.tensor_tensor(qv, m.qa[:, b, :].rearrange("p (v g d) -> p v g d", v=NKV, g=GRP),
                                            ssa[:, b, 0:NH].rearrange("p (v g) -> p v g", v=NKV).unsqueeze(3)
                                            .broadcast_to([P, NKV, GRP, HD]), ALU.mult)
                    link(nc.vector.tensor_tensor(kv, m.kva[:, b, 0:KVW].rearrange("p (h d) -> p h d", d=HD),
                                                 ssa[:, b, NH:].unsqueeze(2).broadcast_to([P, NKV, HD]), ALU.mult))
                    qh = qn[:, b, :].rearrange("p (h d) -> p h d", d=HD)
                    nc.vector.tensor_tensor(qh, qh, qg[:].unsqueeze(1).broadcast_to([P, NH, HD]), ALU.mult)
                    nc.vector.tensor_tensor(kv, kv, kg[:].unsqueeze(1).broadcast_to([P, NKV, HD]),
                                            ALU.mult).then_inc(att_unit, 1)
                for c in range(2 * DN):
                    dve.wait_ge(squared, c + 1)
                    t = nc.vector.tensor_reduce(ssd[:, c, :], sq[:, c, :].rearrange("p (b d) -> p b d", d=DH),
                                                AX, ALU.add)
                t.then_inc(summed, 1)
                for b in range(TB):
                    banks.wait_full(dve, ("attq", b))
                    nc.vector.tensor_scalar(m.attqT[:, :, b * P:(b + 1) * P],
                                            banks.bank(("attq", b))[:].rearrange("p (g t) -> p g t", g=GRP),
                                            HD ** -0.5, None, ALU.mult).then_inc(banks.taken["dve"], 1)
                    banks.wait_full(dve, ("attk", b))
                    nc.vector.tensor_copy(m.attkT[:, b * P:(b + 1) * P],
                                          banks.bank(("attk", b))[:, 0:P]).then_inc(banks.taken["dve"], 1)
                dve.wait_ge(scaled, 1)
                for c in range(2 * DN):
                    v = m.tok[:, c, :].rearrange("p (b d) -> p b d", d=DH)
                    nc.vector.tensor_tensor(v, v, ssd[:, c, :].unsqueeze(2).broadcast_to([P, TB, DH]),
                                            ALU.mult).then_inc(unit, 1)
                dve.wait_ge(z2, 1)
                link(nc.vector.scalar_tensor_tensor(zz[:], zz[:], 0.0, za[:], ALU.max, ALU.add))
                dve.wait_ge(z3, 1)
                nc.vector.scalar_tensor_tensor(m.g[:], zz[:], -1.0,
                                               alog[:].unsqueeze(1).broadcast_to([P, TB, DN]), ALU.mult, ALU.mult)
                dve.wait_ge(b2, 1)
                link(nc.vector.tensor_scalar(eb[:], eb[:], 1.0, None, ALU.add))
                nc.vector.reciprocal(m.beta[:], eb[:])

            @block.gpsimd
            def _(pool):
                link = chain(pool, plink, [0])
                pool.wait_ge(att_sq, 1)
                link(nc.gpsimd.tensor_scalar(ssa[:], ssa[:], 1.0 / HD, EPS, ALU.mult, ALU.add))
                nc.gpsimd.tensor_tensor(ssa[:], ssa[:], m.neg_half[:, 0:1].unsqueeze(2)
                                        .broadcast_to([P, TB, NH + NKV]), ALU.pow).then_inc(att_pow, 1)
                pool.wait_ge(summed, 1)
                link(nc.gpsimd.tensor_scalar(ssd[:], ssd[:], EPS, None, ALU.add))
                link(nc.gpsimd.tensor_tensor(ssd[:], ssd[:], m.neg_half[:, 0:1].unsqueeze(2)
                                             .broadcast_to([P, 2 * DN, TB]), ALU.pow))
                nc.gpsimd.tensor_scalar(ssd[:, 0:DN, :], ssd[:, 0:DN, :], DH ** -0.5, None,
                                        ALU.mult).then_inc(scaled, 1)

            @block.scalar
            def _(act):
                link = chain(act, alink, [0])
                act.wait_ge(small_in[1], 16)
                nc.scalar.activation(alog[:], alog[:], ACT.Exp).then_inc(z3, 1)
                nc.scalar.activation(eb[:], m.ab[:, :, DN:], ACT.Exp, scale=-1.0).then_inc(b2, 1)
                act.wait_ge(z1, 1)
                link(nc.scalar.activation(za[:], zz[:], ACT.Abs))
                link(nc.scalar.activation(za[:], za[:], ACT.Exp, scale=-1.0))
                nc.scalar.activation(za[:], za[:], ACT.Ln, bias=1.0).then_inc(z2, 1)
                for c in range(CT):
                    act.wait_ge(convd, c // 4 + 1)
                    nc.scalar.activation(convT[:, c, :], convT[:, c, :], ACT.Silu).then_inc(silud, 1)
                for c in range(CT):
                    banks.wait_full(act, ("tok", c))
                    if c < 2 * DN:
                        nc.scalar.activation(sq[:, c, :], banks.bank(("tok", c))[:], ACT.Square).then_inc(squared, 1)
                    nc.scalar.activation(m.tok[:, c, :], banks.bank(("tok", c))[:],
                                         ACT.Copy).then_inc(banks.taken["act"], 1)
                for c in range(2 * DN):
                    banks.wait_full(act, ("unitT", c))
                    nc.scalar.activation(m.unitT[:, c, :], banks.bank(("unitT", c))[:],
                                         ACT.Copy).then_inc(banks.taken["act"], 1)

            @block.tensor
            def _(pe):
                for c in range(CT):
                    banks.wait_free(pe, ("tok", c))
                    pe.wait_ge(silud, c + 1)
                    for b in range(TB):
                        t = nc.tensor.transpose(banks.bank(("tok", c))[:, b * P:(b + 1) * P],
                                                convT[:, c, b * P:(b + 1) * P], m.ident[:])
                    t.then_inc(done, 1)
                for b in range(TB):
                    pe.wait_ge(att_unit, b + 1)
                    banks.wait_free(pe, ("attq", b))
                    for g in range(GRP):
                        t = nc.tensor.transpose(banks.bank(("attq", b))[:, g * P:(g + 1) * P],
                                                qn[:, b, g * P:(g + 1) * P], m.ident[:])
                    t.then_inc(done, 1)
                    banks.wait_free(pe, ("attk", b))
                    nc.tensor.transpose(banks.bank(("attk", b))[:, 0:P], kn[:, b, :], m.ident[:]).then_inc(done, 1)
                for c in range(2 * DN):
                    banks.wait_free(pe, ("unitT", c))
                    pe.wait_ge(unit, c + 1)
                    for b in range(TB):
                        t = nc.tensor.transpose(banks.bank(("unitT", c))[:, b * P:(b + 1) * P],
                                                m.tok[:, c, b * P:(b + 1) * P], m.ident[:])
                    t.then_inc(done, 1)


def delta_prepare(nc, m, ps, sem):
    done, plink, vlink, alink = sem("prep_done"), sem("prep_pool"), sem("prep_dve"), sem("prep_act")
    diffs, decays, strict = sem("prep_diffs"), sem("prep_decays"), sem("prep_strict")
    cols, col_exp, tok_scaled, level_in = sem("gate_cols"), sem("gate_exps"), sem("tok_scaled"), sem("level_in")
    x0 = sem("solve_start")
    banks = Banks(ps, done, {"act": sem("prep_by_act"), "dve": sem("prep_by_dve")})
    banks.add("gcol", "dve")
    for b in range(TB):
        banks.add(("grow", b), "act")
    for b in range(TB):
        banks.add(("kk", b), "dve")
        banks.add(("qkT", b), "dve")
    for b in range(TB):
        banks.add(("B0T", b), "dve")
    LV = range(1, 6)
    for l in LV:
        for b in range(TB):
            banks.add(("WT", b, l), "act")
        for b in range(TB):
            if l < 5:
                banks.add(("Z", b, l), "dve")
            banks.add(("ZT", b, l), "dve")
    for b in range(TB):
        banks.add(("wT", b), "act")
        banks.add(("u", b), "dve")

    def h4(ap):
        return ap.rearrange("p (h c) -> p h c", h=DN)

    with ExitStack() as ctx:
        sb = m.mem.local(ctx)
        gc = sb("gc_col", [P, 2, TB, DN])
        egc = sb("egc_col", [P, 2, TB, DN])
        bec = sb("bec_col", [P, TB, DN])
        grow = sb("gc_row", [P, TB, DN, P])
        dec = sb("decay", [P, TB, DN, P])
        decT = sb("decayT", [P, TB, DN, P])
        mm = sb("m_low", [P, TB, DN, P])
        lev = sb("m_level", [P, 2, TB, DN, P])
        X, XT, WT = grow, dec, decT
        vb = sb("v_beta", [P, DN, T])
        kbe = sb("k_beta_decay", [P, DN, T])
        bc4 = lambda ap: ap.unsqueeze(2).broadcast_to([P, DN, P])
        with nc.Block() as block:
            @block.tensor
            def _(pe):
                gflat = m.g[:].rearrange("p b h -> p (b h)")
                nc.tensor.matmul(banks.bank("gcol")[:, 0:16], m.upper[:], gflat, start=True, stop=True)
                nc.tensor.matmul(banks.bank("gcol")[:, 16:32], m.chunk_ones[:], gflat,
                                 start=True, stop=True).then_inc(done, 1)
                for b in range(TB):
                    for h in range(DN):
                        t = nc.tensor.matmul(banks.bank(("grow", b))[:, h * P:(h + 1) * P],
                                             m.g[:, b, h:h + 1].broadcast_to([P, P]), m.upper[:],
                                             start=True, stop=True)
                    t.then_inc(done, 1)
                for b in range(TB):
                    for g, lhs in (("kk", DN), ("qkT", DN)):
                        banks.wait_free(pe, (g, b))
                        for h in range(DN):
                            rhs = m.unitT[:, (DN + h) if g == "kk" else h, b * P:(b + 1) * P]
                            t = nc.tensor.matmul(banks.bank((g, b))[:, h * P:(h + 1) * P],
                                                 m.unitT[:, DN + h, b * P:(b + 1) * P], rhs, start=True, stop=True)
                        t.then_inc(done, 1)
                for b in range(TB):
                    banks.wait_free(pe, ("B0T", b))
                    pe.wait_ge(level_in, b + 1)
                    for h in range(DN):
                        t = nc.tensor.transpose(banks.bank(("B0T", b))[:, h * P:(h + 1) * P],
                                                lev[:, 0, b, h, :], m.ident[:])
                    t.then_inc(done, 1)
                for l in LV:
                    for b in range(TB):
                        banks.wait_free(pe, ("WT", b, l))
                        pe.wait_ge(level_in, TB * l + b + 1)
                        banks.wait_taken(pe, ("ZT", b, l - 1) if l > 1 else ("B0T", b))
                        for h in range(DN):
                            t = nc.tensor.matmul(banks.bank(("WT", b, l))[:, h * P:(h + 1) * P],
                                                 lev[:, l % 2, b, h, :], XT[:, b, h, :], start=True, stop=True)
                        t.then_inc(done, 1)
                    for b in range(TB):
                        banks.wait_taken(pe, ("WT", b, l))
                        for z, lhs, rhs in (("Z", WT, X), ("ZT", X, WT)):
                            if z == "Z" and l == 5:
                                continue
                            banks.wait_free(pe, (z, b, l))
                            for h in range(DN):
                                t = nc.tensor.matmul(banks.bank((z, b, l))[:, h * P:(h + 1) * P],
                                                     lhs[:, b, h, :], rhs[:, b, h, :], start=True, stop=True)
                            t.then_inc(done, 1)
                for b in range(TB):
                    banks.wait_free(pe, ("wT", b))
                    banks.wait_taken(pe, ("ZT", b, 5))
                    pe.wait_ge(tok_scaled, 1)
                    for h in range(DN):
                        t = nc.tensor.matmul(banks.bank(("wT", b))[:, h * P:(h + 1) * P],
                                             kbe[:, h, b * P:(b + 1) * P], XT[:, b, h, :], start=True, stop=True)
                    t.then_inc(done, 1)
                    banks.wait_free(pe, ("u", b))
                    for h in range(DN):
                        t = nc.tensor.matmul(banks.bank(("u", b))[:, h * P:(h + 1) * P],
                                             XT[:, b, h, :], vb[:, h, b * P:(b + 1) * P], start=True, stop=True)
                    t.then_inc(done, 1)

            @block.scalar
            def _(act):
                link = chain(act, alink, [0])
                act.wait_ge(cols, 1)
                nc.scalar.activation(egc[:], gc[:], ACT.Exp).then_inc(col_exp, 1)
                for b in range(TB):
                    banks.wait_full(act, ("grow", b))
                    nc.scalar.activation(m.egrow[:, b], h4(banks.bank(("grow", b))[:]), ACT.Exp)
                    nc.scalar.activation(grow[:, b], h4(banks.bank(("grow", b))[:]),
                                         ACT.Copy).then_inc(banks.taken["act"], 1)
                for b in range(TB):
                    act.wait_ge(diffs, 2 * b + 2)
                    nc.scalar.activation(dec[:, b], dec[:, b], ACT.Exp, scale=-1.0)
                    nc.scalar.activation(decT[:, b], decT[:, b], ACT.Exp).then_inc(decays, 1)
                for l in LV:
                    for b in range(TB):
                        g = ("WT", b, l)
                        banks.wait_full(act, g)
                        if l > 1:
                            banks.wait_full(act, ("ZT", b, l - 1))
                        nc.scalar.activation(WT[:, b], h4(banks.bank(g)[:]), ACT.Copy).then_inc(banks.taken["act"], 1)
                for b in range(TB):
                    banks.wait_full(act, ("wT", b))
                    nc.scalar.activation(m.wT[:, b], h4(banks.bank(("wT", b))[:]),
                                         ACT.Copy).then_inc(banks.taken["act"], 1)

            @block.gpsimd
            def _(pool):
                up = m.upper[:].unsqueeze(1).broadcast_to([P, DN, P])
                low = m.lower[:].unsqueeze(1).broadcast_to([P, DN, P])
                for b in range(TB):
                    pool.wait_ge(decays, b + 1)
                    nc.gpsimd.tensor_tensor(dec[:, b], dec[:, b], low, ALU.mult).then_inc(strict, 1)
                    nc.gpsimd.tensor_tensor(decT[:, b], decT[:, b], up, ALU.mult).then_inc(strict, 1)
                for l in range(6):
                    for b in range(TB):
                        banks.wait_taken(pool, ("kk", b))
                        if l >= 2:
                            banks.wait_full(pool, ("WT", b, l - 2) if l > 2 else ("B0T", b))
                        if l == 2:
                            pool.wait_ge(x0, b + 1)
                        nc.gpsimd.tensor_tensor(lev[:, l % 2, b], mm[:, b],
                                                m.levels[:, l, :].unsqueeze(1).broadcast_to([P, DN, P]),
                                                ALU.mult).then_inc(level_in, 1)

            @block.vector
            def _(dve):
                link = chain(dve, vlink, [0])
                banks.wait_full(dve, "gcol")
                g2 = banks.bank("gcol")[:, 0:32].rearrange("p (s b h) -> p s b h", s=2, b=TB)
                link(nc.vector.tensor_copy(gc[:], g2))
                nc.vector.tensor_tensor(gc[:, 1], gc[:, 1], gc[:, 0], ALU.subtract).then_inc(cols, 1)
                dve.wait_ge(col_exp, 1)
                nc.vector.tensor_tensor(bec[:], m.beta[:], egc[:, 0], ALU.mult).then_inc(banks.taken["dve"], 1)
                for b in range(TB):
                    banks.wait_taken(dve, ("grow", b))
                    link(nc.vector.tensor_tensor(grow[:, b], grow[:, b], bc4(gc[:, 0, b, :]), ALU.subtract))
                    nc.vector.tensor_scalar(dec[:, b], grow[:, b], 0.0, None, ALU.max).then_inc(diffs, 1)
                    nc.vector.tensor_scalar(decT[:, b], grow[:, b], 0.0, None, ALU.min).then_inc(diffs, 1)
                for h in range(DN):
                    v = lambda ap: ap.rearrange("p (b d) -> p b d", d=DH)
                    s = lambda ap: ap[:, :, h].unsqueeze(2).broadcast_to([P, TB, DH])
                    nc.vector.tensor_tensor(v(vb[:, h, :]), v(m.tok[:, 2 * DN + h, :]), s(m.beta), ALU.mult)
                    nc.vector.tensor_tensor(v(kbe[:, h, :]), v(m.tok[:, DN + h, :]), s(bec), ALU.mult)
                    t = nc.vector.tensor_tensor(v(m.kdec[:, h, :]), v(m.tok[:, DN + h, :]), s(egc[:, 1]), ALU.mult)
                t.then_inc(tok_scaled, 1)
                for b in range(TB):
                    dve.wait_ge(strict, 2 * b + 2)
                    link(nc.vector.tensor_tensor(dec[:, b], dec[:, b], bc4(m.beta[:, b, :]), ALU.mult))
                    banks.wait_full(dve, ("kk", b))
                    nc.vector.tensor_tensor(mm[:, b], h4(banks.bank(("kk", b))[:]), dec[:, b],
                                            ALU.mult).then_inc(banks.taken["dve"], 1)
                    banks.wait_full(dve, ("qkT", b))
                    nc.vector.tensor_tensor(m.qkT[:, b], h4(banks.bank(("qkT", b))[:]), decT[:, b],
                                            ALU.mult).then_inc(banks.taken["dve"], 1)
                    nc.vector.tensor_tensor(m.qdT[:, b], m.unitT[:, 0:DN, b * P:(b + 1) * P], m.egrow[:, b], ALU.mult)
                idb = m.ident[:].unsqueeze(1).broadcast_to([P, DN, P])
                for b in range(TB):
                    banks.wait_full(dve, ("B0T", b))
                    nc.vector.tensor_tensor(X[:, b], idb, lev[:, 0, b], ALU.subtract).then_inc(x0, 1)
                    nc.vector.scalar_tensor_tensor(XT[:, b], h4(banks.bank(("B0T", b))[:]), -1.0, idb,
                                                   ALU.mult, ALU.add).then_inc(banks.taken["dve"], 1)
                for l in LV:
                    for b in range(TB):
                        banks.wait_full(dve, ("ZT", b, l))
                        if l < 5:
                            nc.vector.tensor_tensor(X[:, b], X[:, b], h4(banks.bank(("Z", b, l))[:]),
                                                    ALU.subtract).then_inc(banks.taken["dve"], 1)
                        nc.vector.tensor_tensor(XT[:, b], XT[:, b], h4(banks.bank(("ZT", b, l))[:]),
                                                ALU.subtract).then_inc(banks.taken["dve"], 1)
                for b in range(TB):
                    banks.wait_full(dve, ("u", b))
                    nc.vector.tensor_copy(m.u[:, b], h4(banks.bank(("u", b))[:])).then_inc(banks.taken["dve"], 1)


def mixers(nc, m, ps, sem, sinks, att_out_g, dn_out_g):
    NC = T // CH
    in_ = [sem(f"mixer_small{i}") for i in range(3)]
    ws_done, v_new, s_done, s_new, o_done, o_out = (sem(n) for n in ("ws_done", "v_new", "s_done", "s_new",
                                                                     "o_done", "o_out"))
    zeroed, o_sq, o_ss, o_pow, o_mix = sem("s_zeroed"), sem("o_sq"), sem("o_ss"), sem("o_pow"), sem("z_gate")
    vlink, alink, plink = sem("mix_dve"), sem("mix_act"), sem("mix_pool")
    sc_done, sc_out, negm, prob, den_in, p_done, p_out = (sem(n) for n in (
        "att_scores", "att_scores_out", "att_negmax", "att_probs", "att_sink_exp", "att_pT", "att_pT_out"))
    pv_done, att_o, att_ss, att_rms = (sem(n) for n in ("att_pv", "att_o", "att_ss", "att_rms"))
    bV, bO, bS, bPV = ps[0], ps[1], ps[2], ps[3]
    bA = ps[4:8]

    with ExitStack() as ctx:
        sb = m.mem.local(ctx)
        S = sb("state", [P, 2, DN, P])
        vnew = sb("v_new_t", [P, DN, P])
        ot = sb("o_tok", [P, TB, DNW])
        osq = sb("o_sqr", [P, DNW])
        oss = sb("o_sss", [P, TB, DN])
        dg = sb("dn_gain", [P, DH])
        ag = sb("att_gain", [P, ATT])
        snk = sb("sinks_b", [P, NH])
        sc = sb("att_sc", [P, NH, 2 * P])
        mx = sb("att_mx", [P, TB, NH])
        nm = sb("att_nm", [P, TB, NH])
        sm = sb("att_sm", [P, TB, NH])
        den = sb("att_den", [P, TB, NH])
        pT = sb("att_pTs", [P, 2 * NH, P])
        ao = sb("att_ot", [P, ATT])
        aj = sb("att_junk", [P, ATT])
        ass = sb("att_rss", [P, TB])
        r4 = lambda ap: ap.rearrange("p (h d) -> p h d", h=DN)
        with nc.Block() as block:
            @block.sync
            def _(sp):
                sp.dma_start(snk[:], sinks[0:1, :].broadcast_to([P, NH])).then_inc(in_[0], 16)
                sp.dma_start(ag[:], att_out_g[0:1, :].broadcast_to([P, ATT])).then_inc(in_[1], 16)
                sp.dma_start(dg[:], dn_out_g[0:1, :].broadcast_to([P, DH])).then_inc(in_[2], 16)

            @block.tensor
            def _(pe):
                def scores(b):
                    lo = 0 if b else P
                    if b:
                        pe.wait_ge(p_out, 4 * b)
                    for i in range(4):
                        v = slice(HD * (i // 2), HD * (i // 2) + HD)
                        for e in range(2):
                            g = 2 * (i % 2) + e
                            t = nc.tensor.matmul(bA[i][:, e * 2 * P + lo:(e + 1) * 2 * P],
                                                 m.attqT[v, g, b * P:(b + 1) * P],
                                                 m.attkT[v, (b - 1) * P + lo:(b + 1) * P], start=True, stop=True)
                    t.then_inc(sc_done, 1)

                def p_transposes(b):
                    for i in range(4):
                        pe.wait_ge(prob, NH * b + 2 * i + 2)
                        if i == 0:
                            pe.wait_ge(sc_out, 4 * b + 4)
                        for e in range(2):
                            for half in range(0 if b else 1, 2):
                                t = nc.tensor.transpose(bA[i][:, (2 * e + half) * P:(2 * e + half + 1) * P],
                                                        sc[:, 2 * i + e, half * P:(half + 1) * P], m.ident[:])
                        t.then_inc(p_done, 1)

                def pv(b):
                    pe.wait_ge(p_out, 4 * b + 4)
                    if b:
                        pe.wait_ge(att_o, b)
                    for h in range(NH):
                        kv = h // GRP
                        for half in range(0 if b else 1, 2):
                            t = nc.tensor.matmul(bPV[:, h * HD:(h + 1) * HD], pT[:, 2 * h + half, :],
                                                 m.kva[:, b - 1 + half, KVW + kv * HD:KVW + (kv + 1) * HD],
                                                 start=(half == 0 or b == 0), stop=(half == 1))
                    t.then_inc(pv_done, 1)

                scores(0)
                for c in range(NC):
                    b, q = c // 2, c % 2
                    r = slice(q * CH, (q + 1) * CH)
                    if c == 0:
                        pe.wait_ge(zeroed, 1)
                    else:
                        pe.wait_ge(s_new, DN * c)
                    for h in range(DN):
                        t = nc.tensor.matmul(bV[r, h * P:(h + 1) * P], m.wT[:, b, h, r], S[:, c % 2, h, :],
                                             start=True, stop=True)
                    t.then_inc(ws_done, 1)
                    if q == 0:
                        p_transposes(b)
                    else:
                        pv(b)
                        if b + 1 < TB:
                            scores(b + 1)
                    pe.wait_ge(v_new, c + 1)
                    for h in range(DN):
                        t = nc.tensor.matmul(bS[:, h * P:(h + 1) * P], m.kdec[r, h, b * P:(b + 1) * P],
                                             vnew[r, h, :], start=True, stop=True)
                    t.then_inc(s_done, 1)
                    if c:
                        pe.wait_ge(o_out, c)
                    for h in range(DN):
                        nc.tensor.matmul(bO[r, h * P:(h + 1) * P], m.qdT[:, b, h, r], S[:, c % 2, h, :],
                                         start=True, stop=False)
                        t = nc.tensor.matmul(bO[r, h * P:(h + 1) * P], m.qkT[r, b, h, r], vnew[r, h, :],
                                             start=False, stop=True)
                    t.then_inc(o_done, 1)

            @block.vector
            def _(dve):
                link = chain(dve, vlink, [0])

                def att_max(b):
                    lo = 0 if b else P
                    for i in range(4):
                        dve.wait_ge(sc_done, b + 1)
                        if i == 0 and b:
                            dve.wait_ge(p_done, 4 * b)
                        t = nc.vector.tensor_tensor(
                            sc[:, 2 * i:2 * i + 2, lo:], bA[i][:].rearrange("p (e k) -> p e k", e=2)[:, :, lo:],
                            m.att_mask[:, lo:].unsqueeze(1).broadcast_to([P, 2, 2 * P - lo]), ALU.add)
                        t.then_inc(sc_out, 1)
                    dve.wait_ge(sc_out, 4 * b + 4)
                    link(nc.vector.tensor_reduce(mx[:, b, :], sc[:, :, lo:], AX, ALU.max))
                    if b == 0:
                        dve.wait_ge(in_[0], 16)
                    link(nc.vector.tensor_tensor(mx[:, b, :], mx[:, b, :], snk[:], ALU.max))
                    link(nc.vector.tensor_tensor(sm[:, b, :], snk[:], mx[:, b, :], ALU.subtract))
                    nc.vector.tensor_scalar(nm[:, b, :], mx[:, b, :], -1.0, None, ALU.mult).then_inc(negm, 1)

                def att_out(b):
                    dve.wait_ge(den_in, b + 1)
                    link(nc.vector.tensor_tensor(den[:, b, :], den[:, b, :], sm[:, b, :], ALU.add))
                    link(nc.vector.reciprocal(den[:, b, :], den[:, b, :]))
                    dve.wait_ge(pv_done, b + 1)
                    nc.vector.tensor_tensor(ao[:].rearrange("p (h d) -> p h d", d=HD),
                                            bPV[:].rearrange("p (h d) -> p h d", d=HD),
                                            den[:, b, :].unsqueeze(2).broadcast_to([P, NH, HD]),
                                            ALU.mult).then_inc(att_o, 1)

                def att_norm(b):
                    if b == 0:
                        dve.wait_ge(in_[1], 16)
                    dve.wait_ge(att_rms, b + 1)
                    link(nc.vector.scalar_tensor_tensor(m.mix[:, b, 0:ATT], ao[:], ass[:, b:b + 1], ag[:],
                                                        ALU.mult, ALU.mult))

                def o_sum(b):
                    dve.wait_ge(o_sq, b + 1)
                    nc.vector.tensor_reduce(oss[:, b, :], r4(osq[:]), AX, ALU.add).then_inc(o_ss, 1)

                def o_norm(b):
                    dve.wait_ge(o_pow, b + 1)
                    link(nc.vector.tensor_tensor(r4(ot[:, b, :]), r4(ot[:, b, :]),
                                                 oss[:, b, :].unsqueeze(2).broadcast_to([P, DN, DH]), ALU.mult))
                    nc.vector.tensor_tensor(m.mix[:, b, ATT:], ot[:, b, :], m.z[:, b, :], ALU.mult)

                nc.vector.memset(S[:, 0], 0.0).then_inc(zeroed, 1)
                att_max(0)
                dve.wait_ge(o_mix, 1)
                dve.wait_ge(in_[2], 16)
                for b in range(TB):
                    t = nc.vector.tensor_tensor(r4(m.z[:, b, :]), r4(m.z[:, b, :]),
                                                dg[:].unsqueeze(1).broadcast_to([P, DN, DH]), ALU.mult)
                link(t)
                for c in range(NC):
                    b, q = c // 2, c % 2
                    r = slice(q * CH, (q + 1) * CH)
                    dve.wait_ge(ws_done, c + 1)
                    if c:
                        dve.wait_ge(o_done, c)
                    nc.vector.tensor_tensor(vnew[r], m.u[r, b], r4(bV[:])[r], ALU.subtract).then_inc(v_new, 1)
                    if q == 1:
                        att_out(b)
                        if b + 1 < TB:
                            att_max(b + 1)
                    dve.wait_ge(s_done, c + 1)
                    last = (q + 1) * CH - 1
                    for h in range(DN):
                        nc.vector.scalar_tensor_tensor(S[:, (c + 1) % 2, h, :], S[:, c % 2, h, :],
                                                       m.egrow[:, b, h, last:last + 1],
                                                       bS[:, h * P:(h + 1) * P], ALU.mult, ALU.add).then_inc(s_new, 1)
                    if q == 0 and b:
                        att_norm(b - 1)
                        o_sum(b - 1)
                    elif b:
                        o_norm(b - 1)
                att_norm(TB - 1)
                o_sum(TB - 1)
                o_norm(TB - 1)

            @block.gpsimd
            def _(pool):
                link = chain(pool, plink, [0])
                for b in range(TB):
                    pool.wait_ge(att_ss, b + 1)
                    link(nc.gpsimd.tensor_scalar(ass[:, b:b + 1], ass[:, b:b + 1], 1.0 / ATT, EPS, ALU.mult, ALU.add))
                    nc.gpsimd.tensor_tensor(ass[:, b:b + 1], ass[:, b:b + 1], m.neg_half[:, 0:1],
                                            ALU.pow).then_inc(att_rms, 1)
                    pool.wait_ge(o_ss, b + 1)
                    link(nc.gpsimd.tensor_scalar(oss[:, b, :], oss[:, b, :], 1.0 / DH, EPS, ALU.mult, ALU.add))
                    nc.gpsimd.tensor_tensor(oss[:, b, :], oss[:, b, :], m.neg_half[:, 0:1].broadcast_to([P, DN]),
                                            ALU.pow).then_inc(o_pow, 1)

            @block.scalar
            def _(act):
                def probs(b):
                    lo = 0 if b else P
                    act.wait_ge(negm, b + 1)
                    for h in range(NH):
                        nc.scalar.activation(sc[:, h, lo:], sc[:, h, lo:], ACT.Exp, bias=nm[:, b, h:h + 1],
                                             accum_out=den[:, b, h:h + 1]).then_inc(prob, 1)
                    nc.scalar.activation(sm[:, b, :], sm[:, b, :], ACT.Exp).then_inc(den_in, 1)

                def pT_copies(b):
                    for i in range(4):
                        act.wait_ge(p_done, 4 * b + i + 1)
                        if i == 0 and b:
                            act.wait_ge(pv_done, b)
                        out = pT[:, 4 * i:4 * i + 4, :].rearrange("p (e f) q -> p e f q", e=2)
                        src = bA[i][:].rearrange("p (e f q) -> p e f q", e=2, f=2)
                        lo = 0 if b else 1
                        nc.scalar.activation(out[:, :, lo:], src[:, :, lo:], ACT.Copy).then_inc(p_out, 1)

                def att_square(b):
                    act.wait_ge(att_o, b + 1)
                    nc.scalar.activation(aj[:], ao[:], ACT.Square, accum_out=ass[:, b:b + 1]).then_inc(att_ss, 1)

                nc.scalar.activation(m.z[:], m.z[:], ACT.Silu).then_inc(o_mix, 1)
                for c in range(NC):
                    b, q = c // 2, c % 2
                    r = slice(q * CH, (q + 1) * CH)
                    if q == 0:
                        probs(b)
                        pT_copies(b)
                    act.wait_ge(o_done, c + 1)
                    nc.scalar.activation(ot[r, b, :], bO[r, :], ACT.Copy).then_inc(o_out, 1)
                    if q == 1:
                        att_square(b)
                        act.wait_ge(o_out, c + 1)
                        if b:
                            act.wait_ge(o_ss, b)
                        nc.scalar.activation(osq[:], ot[:, b, :], ACT.Square).then_inc(o_sq, 1)


def output_projection(nc, m, ps, sem, w_out, norm_ffn_g, w_q, h_dram, x_dram):
    done, plink = sem("out_done"), sem("out_pool")
    w_ld = [sem(f"w_out_in{i}") for i in range(4)]
    spilled = [sem("h_spilled"), sem("x_spilled")]
    g_in, squares, scale, normed = sem("ffn_gain_in"), sem("h_squares"), sem("h_scale"), sem("h_normed")
    banks = Banks(ps, done, {"act": sem("out_by_act"), "dve": sem("out_by_dve")})
    for b in range(TB):
        for half in range(2):
            banks.add(("mixT", b, half), "act")
    for b in range(TB):
        for half in range(2):
            banks.add(("h", b, half), "dve")
    for b in range(TB):
        for half in range(2):
            banks.add(("xT", b, half), "act")
    for h in range(PH):
        banks.add(("q", h), "dve" if h % 2 else "act")
    with ExitStack() as ctx:
        sb = m.mem.local(ctx)
        gain = sb("ffn_gain", [P, D])
        xn = sb("hn", [P, 2, D])
        junk = sb("h_junk", [P, D])
        mixT = sb("mixT", [P, KD, T])
        w = sb("w_oq", [P, 4, KD, T])
        ss = sb("h_ss", [P, TB])
        with nc.Block() as block:
            @block.sync
            def _(sp):
                wo = w_out[0].rearrange("(k p) n -> p k n", p=P)
                wq = w_q[0].rearrange("(k p) n -> p k n", p=P)
                for i in range(4):
                    v = (wo if i < 2 else wq)[:, :, (i % 2) * T:(i % 2 + 1) * T]
                    sp.dma_start(w[:, i], v).then_inc(w_ld[i], 16)
                    if i == 1:
                        sp.dma_start(gain[:], norm_ffn_g[0:1, :].broadcast_to([P, D])).then_inc(g_in, 16)
                banks.wait_taken(sp, ("h", TB - 1, 1))
                sp.dma_start(h_dram, m.acc[:]).then_inc(spilled[0], 16)
                banks.wait_taken(sp, ("xT", TB - 1, 1))
                sp.dma_start(x_dram, m.xn2T[:]).then_inc(spilled[1], 16)
                for i in range(2):
                    sp.wait_ge(spilled[i], 16)

            @block.tensor
            def _(pe):
                for b in range(TB):
                    for half in range(2):
                        for k in range(4):
                            kk = 4 * half + k
                            t = nc.tensor.transpose(banks.bank(("mixT", b, half))[:, k * P:(k + 1) * P],
                                                    m.mix[:, b, kk * P:(kk + 1) * P], m.ident[:])
                        t.then_inc(done, 1)
                for b in range(TB):
                    banks.wait_taken(pe, ("mixT", b, 1))
                    for half in range(2):
                        g = ("h", b, half)
                        banks.wait_free(pe, g)
                        pe.wait_ge(w_ld[half], 16)
                        for k in range(KD):
                            t = nc.tensor.matmul(banks.bank(g)[:], mixT[:, k, b * P:(b + 1) * P], w[:, half, k, :],
                                                 start=(k == 0), stop=(k == KD - 1))
                        t.then_inc(done, 1)
                for b in range(TB):
                    pe.wait_ge(normed, b + 1)
                    for half in range(2):
                        banks.wait_free(pe, ("xT", b, half))
                        for k in range(4):
                            kk = 4 * half + k
                            t = nc.tensor.transpose(banks.bank(("xT", b, half))[:, k * P:(k + 1) * P],
                                                    xn[:, b % 2, kk * P:(kk + 1) * P], m.ident[:])
                        t.then_inc(done, 1)
                banks.wait_taken(pe, ("xT", TB - 1, 1))
                for h in range(PH):
                    g = ("q", h)
                    banks.wait_free(pe, g)
                    pe.wait_ge(w_ld[2 + h // 4], 16)
                    for k in range(KD):
                        t = nc.tensor.matmul(banks.bank(g)[:], w[:, 2 + h // 4, k, (h % 4) * P:(h % 4 + 1) * P],
                                             m.xn2T[:, k, :], start=(k == 0), stop=(k == KD - 1))
                    t.then_inc(done, 1)

            @block.scalar
            def _(act):
                for b in range(TB):
                    for half in range(2):
                        g = ("mixT", b, half)
                        banks.wait_full(act, g)
                        nc.scalar.activation(mixT[:, 4 * half:4 * half + 4, b * P:(b + 1) * P],
                                             banks.bank(g)[:].rearrange("p (k t) -> p k t", k=4),
                                             ACT.Copy).then_inc(banks.taken["act"], 1)
                for b in range(TB):
                    banks.wait_taken(act, ("h", b, 1))
                    if b:
                        act.wait_ge(squares, b)
                    nc.scalar.activation(junk[:], m.acc[:, b, :], ACT.Square,
                                         accum_out=ss[:, b:b + 1]).then_inc(squares, 1)
                for b in range(TB):
                    for half in range(2):
                        g = ("xT", b, half)
                        banks.wait_full(act, g)
                        nc.scalar.activation(m.xn2T[:, 4 * half:4 * half + 4, b * P:(b + 1) * P],
                                             banks.bank(g)[:].rearrange("p (k t) -> p k t", k=4),
                                             ACT.Copy).then_inc(banks.taken["act"], 1)
                for h in range(0, PH, 2):
                    banks.wait_full(act, ("q", h))
                    nc.scalar.activation(m.qT[:, h, :], banks.bank(("q", h))[:],
                                         ACT.Copy).then_inc(banks.taken["act"], 1)

            @block.gpsimd
            def _(pool):
                link = chain(pool, plink, [0])
                for b in range(TB):
                    pool.wait_ge(squares, b + 1)
                    link(nc.gpsimd.tensor_scalar(ss[:, b:b + 1], ss[:, b:b + 1], 1.0 / D, EPS, ALU.mult, ALU.add))
                    nc.gpsimd.tensor_tensor(ss[:, b:b + 1], ss[:, b:b + 1], m.neg_half[:, 0:1],
                                            ALU.pow).then_inc(scale, 1)

            @block.vector
            def _(dve):
                for b in range(TB):
                    for half in range(2):
                        g = ("h", b, half)
                        banks.wait_full(dve, g)
                        v = m.acc[:, b, half * T:(half + 1) * T]
                        nc.vector.tensor_tensor(v, v, banks.bank(g)[:], ALU.add).then_inc(banks.taken["dve"], 1)
                dve.wait_ge(g_in, 16)
                for b in range(TB):
                    dve.wait_ge(scale, b + 1)
                    if b >= 2:
                        banks.wait_full(dve, ("xT", b - 2, 1))
                    nc.vector.scalar_tensor_tensor(xn[:, b % 2, :], m.acc[:, b, :], ss[:, b:b + 1], gain[:],
                                                   ALU.mult, ALU.mult).then_inc(normed, 1)
                for h in range(1, PH, 2):
                    banks.wait_full(dve, ("q", h))
                    nc.vector.tensor_copy(m.qT[:, h, :], banks.bank(("q", h))[:]).then_inc(banks.taken["dve"], 1)


def routing(nc, m, ps, sem, keys, gates):
    done, vlink, alink = sem("rt_done"), sem("rt_dve"), sem("rt_act")
    k_in, subbed, exped, r1_row, masked, r2_ready, r1_ready, tops = (sem(n) for n in (
        "keys_in", "rt_subtracted", "rt_exps", "rt_r1_rows", "rt_masked", "rt_r2", "rt_r1", "rt_iota"))
    stored = [sem("gates_out0"), sem("gates_out1")]
    banks = Banks(ps, done, {"act": sem("rt_by_act"), "dve": sem("rt_by_dve")})
    HT = T // TB // 2
    RING = 16

    def add_scores(b):
        for hh in range(2):
            for p in range(2):
                banks.add(("s", b, p, hh), "act")

    add_scores(0)
    for b in range(TB):
        banks.add(("small", b), "dve")
        for jh in range(2):
            for k in range(16):
                banks.add(("r2T", b, jh, k), "act")
        if b + 1 < TB:
            add_scores(b + 1)
        for k in range(P // 4):
            banks.add(("G", b, k), "act")

    with ExitStack() as ctx:
        sb = m.mem.local(ctx)
        kt = sb("sub_keys", [P, PH, NK])
        s = sb("scores", [P, 2, PH, NK])
        top = sb("top", [P, 2, PH, TOPK])
        idx = sb("top_idx", [P, PH, TOPK], U32)
        best = sb("best", [P, PH, TOPK])
        theta = sb("theta", [P, PH, TOPK])
        e1 = sb("e1", [P, PH, TOPK])
        e2 = sb("e2", [P, PH, NK])
        small = sb("rt_small", [P, 2, HA])
        smallT = sb("rt_smallT", [P, 2, P])
        zsum = sb("rt_z", [P, PH])
        iota = sb("rt_iota_row", [P, NK])
        r2 = sb("r2", [P, HA, NK // 2])
        r2T = sb("r2T", [P, P, NK])
        r1 = sb("r1", [P, RING, NK])
        stage = sb("gate_stage", [P, 2, NK, HT])
        flat = r2[:].rearrange("p a j -> p (a j)")
        sr = flat[:, 0:2 * PH * NK].rearrange("p (q h n) -> p q h n", q=2, h=PH)
        c0 = 2 * PH * NK
        cand, cand1, cand2, val = (flat[:, c0 + i * PH * NPAIR:c0 + (i + 1) * PH * NPAIR]
                                   .rearrange("p (h n) -> p h n", h=PH) for i in range(4))

        def rows(buf, off, r, w):
            return buf[:, :, off:off + r * w].rearrange("p h (r w) -> p h r w", w=w)

        def first(a, r, w):
            return top[:, 0, :, a:a + r].unsqueeze(3).broadcast_to([P, PH, r, w])

        def second(r, w):
            return top[:, 1, :, 0:w].unsqueeze(2).broadcast_to([P, PH, r, w])

        with nc.Block() as block:
            @block.sync
            def _(sp):
                sp.dma_start(kt[:], keys.rearrange("p (h n) -> p h n", h=PH)).then_inc(k_in, 16)
                for b in range(TB):
                    for half in range(2):
                        banks.wait_taken(sp, ("G", b, 16 * half + 15))
                        t0 = b * P + half * HT
                        sp.dma_start(gates[:, :, t0:t0 + HT].rearrange("j i t -> i j t"),
                                     stage[:, half]).then_inc(stored[half], 16)
                for half in range(2):
                    sp.wait_ge(stored[half], 16 * TB)

            @block.gpsimd
            def _(pool):
                nc.gpsimd.iota(iota[:], pattern=[[1, NK]], base=0, channel_multiplier=0,
                               allow_small_or_imprecise_dtypes=True).then_inc(tops, 1)
                for b in range(TB):
                    for jh in range(2):
                        pool.wait_ge(masked, 2 * b + jh + 1)
                        v = r2[:].rearrange("p (h a) j -> p h a j", h=PH)
                        nc.gpsimd.tensor_tensor(v, v, e2[:, :, jh * 64:jh * 64 + 64].unsqueeze(2)
                                                .broadcast_to([P, PH, TOPK, 64]), ALU.mult).then_inc(r2_ready, 1)

            @block.tensor
            def _(pe):
                def scores(b):
                    for hh in range(2):
                        for p in range(2):
                            g = ("s", b, p, hh)
                            banks.wait_free(pe, g)
                            for h in range(4):
                                v = slice(p * HALF, (p + 1) * HALF)
                                t = nc.tensor.matmul(banks.bank(g)[:, h * NK:(h + 1) * NK],
                                                     m.qT[v, 4 * hh + h, b * P:(b + 1) * P],
                                                     kt[v, 4 * hh + h, :], start=True, stop=True)
                            t.then_inc(done, 1)

                pe.wait_ge(k_in, 16)
                scores(0)
                for b in range(TB):
                    banks.wait_free(pe, ("small", b))
                    pe.wait_ge(r1_row, b + 1)
                    for i in range(2):
                        t = nc.tensor.transpose(banks.bank(("small", b))[:, i * P:(i + 1) * P], small[:, i, :],
                                                m.ident[:])
                    t.then_inc(done, 1)
                    for jh in range(2):
                        pe.wait_ge(r2_ready, 2 * b + jh + 1)
                        for k in range(16):
                            g = ("r2T", b, jh, k)
                            banks.wait_free(pe, g)
                            for i in range(4):
                                t = nc.tensor.transpose(banks.bank(g)[:, i * P:(i + 1) * P],
                                                        r2[:, :, 4 * k + i], m.ident[:])
                            t.then_inc(done, 1)
                    if b + 1 < TB:
                        scores(b + 1)
                    banks.wait_taken(pe, ("r2T", b, 1, 15))
                    for k in range(P // 4):
                        g = ("G", b, k)
                        banks.wait_free(pe, g)
                        pe.wait_ge(r1_ready, 32 * b + k + 1)
                        for i in range(4):
                            t = nc.tensor.matmul(banks.bank(g)[:, i * NK:(i + 1) * NK],
                                                 r1[:, (4 * k + i) % RING, :], r2T[:, 4 * k + i, :],
                                                 start=True, stop=True)
                        t.then_inc(done, 1)

            @block.scalar
            def _(act):
                def scores_out(b):
                    if b:
                        act.wait_ge(masked, 2 * b)
                    for hh in range(2):
                        for p in range(2):
                            g = ("s", b, p, hh)
                            banks.wait_full(act, g)
                            nc.scalar.activation(s[:, p, 4 * hh:4 * hh + 4, :],
                                                 banks.bank(g)[:].rearrange("p (h n) -> p h n", h=4),
                                                 ACT.Copy).then_inc(banks.taken["act"], 1)

                scores_out(0)
                for b in range(TB):
                    act.wait_ge(subbed, b + 1)
                    nc.scalar.activation(best[:], best[:], ACT.Exp)
                    nc.scalar.activation(e1[:], e1[:], ACT.Exp)
                    nc.scalar.activation(e2[:], e2[:], ACT.Exp).then_inc(exped, 1)
                    for jh in range(2):
                        for k in range(16):
                            g = ("r2T", b, jh, k)
                            banks.wait_full(act, g)
                            if b and jh == 0 and k == 0:
                                banks.wait_full(act, ("G", b - 1, P // 4 - 1))
                            j0 = jh * 64 + 4 * k
                            nc.scalar.activation(r2T[:, :, j0:j0 + 4].rearrange("p t j -> p j t"),
                                                 banks.bank(g)[:].rearrange("p (j t) -> p j t", j=4),
                                                 ACT.Copy).then_inc(banks.taken["act"], 1)
                    if b + 1 < TB:
                        scores_out(b + 1)
                    for k in range(P // 4):
                        g = ("G", b, k)
                        banks.wait_full(act, g)
                        if b and k % 16 == 0:
                            act.wait_ge(stored[k // 16], 16 * b)
                        t0 = 4 * (k % 16)
                        nc.scalar.activation(stage[:, k // 16, :, t0:t0 + 4].rearrange("p j t -> p t j"),
                                             banks.bank(g)[:].rearrange("p (t j) -> p t j", t=4),
                                             ACT.Copy).then_inc(banks.taken["act"], 1)

            @block.vector
            def _(dve):
                link = chain(dve, vlink, [0])
                for b in range(TB):
                    banks.wait_taken(dve, ("s", b, 1, 1))
                    if b:
                        banks.wait_full(dve, ("r2T", b - 1, 1, 15))
                    every = [(p, h) for p in range(2) for h in range(PH)]
                    for p, h in every:
                        t = nc.vector.max(top[:, p, h, 0:8], s[:, p, h, :])
                    link(t)
                    for p, h in every:
                        t = nc.vector.match_replace(out=sr[:, p, h, :], in_to_replace=top[:, p, h, 0:8],
                                                    in_values=s[:, p, h, :], imm_value=-BIG)
                    link(t)
                    for p, h in every:
                        t = nc.vector.max(top[:, p, h, 8:16], sr[:, p, h, :])
                    link(t)
                    for h in range(PH):
                        nc.vector.max_index(idx[:, h, 0:8], top[:, 0, h, 0:8], s[:, 0, h, :])
                        nc.vector.max_index(idx[:, h, 8:16], top[:, 0, h, 8:16], sr[:, 0, h, :])
                    off = 0
                    for a, r, w in PAIRS:
                        t = nc.vector.tensor_tensor(rows(cand, off, r, w), first(a, r, w), second(r, w), ALU.add)
                        off += r * w
                    link(t)
                    for h in range(PH):
                        t = nc.vector.max(best[:, h, 0:8], cand[:, h, :])
                    link(t)
                    for h in range(PH):
                        t = nc.vector.match_replace(out=cand1[:, h, :], in_to_replace=best[:, h, 0:8],
                                                    in_values=cand[:, h, :], imm_value=-BIG)
                    link(t)
                    for h in range(PH):
                        t = nc.vector.max(best[:, h, 8:16], cand1[:, h, :])
                    link(t)
                    for h in range(PH):
                        t = nc.vector.match_replace(out=cand2[:, h, :], in_to_replace=best[:, h, 8:16],
                                                    in_values=cand1[:, h, :], imm_value=-BIG)
                    link(t)
                    link(nc.vector.tensor_tensor(val, cand, cand2, ALU.not_equal))
                    link(nc.vector.tensor_scalar(val, val, -BIG, BIG, ALU.mult, ALU.add))
                    off = 0
                    for a, r, w in PAIRS:
                        t = nc.vector.tensor_tensor(rows(val, off, r, w), rows(val, off, r, w), second(r, w), ALU.add)
                        off += r * w
                    link(t)
                    off = 0
                    for a, r, w in PAIRS:
                        nc.vector.tensor_reduce(theta[:, :, a:a + r], rows(val, off, r, w), AX, ALU.min)
                        off += r * w
                    bc = lambda ap, n: ap.broadcast_to([P, PH, n])
                    nc.vector.tensor_tensor(e1[:], top[:, 0], bc(top[:, 0, :, 0:1], TOPK), ALU.subtract)
                    nc.vector.tensor_tensor(e2[:], s[:, 1], bc(top[:, 1, :, 0:1], NK), ALU.subtract)
                    nc.vector.tensor_tensor(zsum[:].unsqueeze(2), best[:, :, 0:1], best[:, :, 0:1], ALU.max)
                    link(nc.vector.tensor_copy(small[:, 0, :].rearrange("p (h a) -> p h a", h=PH), idx[:]))
                    nc.vector.tensor_tensor(best[:], best[:], bc(zsum[:].unsqueeze(2), TOPK),
                                            ALU.subtract).then_inc(subbed, 1)
                    dve.wait_ge(exped, b + 1)
                    link(nc.vector.tensor_reduce(zsum[:], best[:], AX, ALU.add))
                    link(nc.vector.reciprocal(zsum[:], zsum[:]))
                    nc.vector.tensor_tensor(small[:, 1, :].rearrange("p (h a) -> p h a", h=PH), e1[:],
                                            bc(zsum[:].unsqueeze(2), TOPK), ALU.mult).then_inc(r1_row, 1)
                    for jh in range(2):
                        if jh:
                            banks.wait_full(dve, ("small", b))
                            nc.vector.tensor_copy(smallT[:].rearrange("p i t -> p (i t)"),
                                                  banks.bank(("small", b))[:, 0:2 * P]
                                                  ).then_inc(banks.taken["dve"], 1)
                            banks.wait_full(dve, ("r2T", b, 0, 15))
                        nc.vector.tensor_tensor(r2[:].rearrange("p (h a) j -> p h a j", h=PH),
                                                s[:, 1, :, jh * 64:jh * 64 + 64].unsqueeze(2)
                                                .broadcast_to([P, PH, TOPK, 64]),
                                                theta[:].unsqueeze(3).broadcast_to([P, PH, TOPK, 64]),
                                                ALU.is_ge).then_inc(masked, 1)
                    banks.wait_taken(dve, ("small", b))
                    if b == 0:
                        dve.wait_ge(tops, 1)
                    for k in range(P // 4):
                        if 32 * b + k >= RING // 4:
                            n = 32 * b + k - RING // 4
                            banks.wait_full(dve, ("G", n // 32, n % 32))
                        for i in range(4):
                            t = 4 * k + i
                            ins = nc.vector.tensor_scalar(r1[:, t % RING, :], iota[:], smallT[:, 0, t:t + 1],
                                                          smallT[:, 1, t:t + 1], ALU.is_equal, ALU.mult)
                        ins.then_inc(r1_ready, 1)


def experts(nc, m, ps, sem, u_t, v, gates, h_dram, x_dram, out):
    NU, NV, NGB = 4, 2, 4
    BODY = 2 * GT
    x_in, acc_in, x_hi = sem("ex_x_in"), sem("ex_acc_in"), sem("ex_x_hi")
    u_in = [sem(f"u_in{i}") for i in range(NU)]
    v_in = [sem(f"v_in{i}") for i in range(NV)]
    g_in = [sem(f"gate_in{i}") for i in range(NGB)]
    u_hi_ready, u_ready, v_hi_ready, v_ready = (sem(n) for n in ("u_hi_ready", "u_ready", "v_hi_ready", "v_ready"))
    up_done, gelu_done, gated, gate_f, gate_hi = (sem(n) for n in ("up_done", "gelu_done", "gated", "gate_f", "gate_hi"))
    down_done, added, out_done = sem("down_done"), sem("added"), sem("out_stored")
    bank_up = ps[0:2]
    bank_down = ps[2:6]
    v_rows = v[0].rearrange("(i j) d -> j i d", j=NK)
    u_rows = u_t

    with ExitStack() as ctx:
        sb = m.mem.local(ctx)
        acc = sb("acc_out", [P, TB, D])
        xh = sb("x_hi", [P, KD, T], F32R)
        xl = sb("x_lo", [P, KD, T], F32R)
        f = lambda ap: ap.bitcast(F32)
        xf = m.mem.take("x_full", [P, KD, T])
        with nc.Block() as block:
            @block.sync
            def _(sp):
                sp.dma_start(xf[:], x_dram).then_inc(x_in, 16)
                sp.dma_start(acc[:], h_dram).then_inc(acc_in, 16)
                sp.wait_ge(acc_in, 16)

            @block.scalar
            def _(act):
                act.wait_ge(x_in, 16)
                for k in range(KD):
                    nc.scalar.activation(xh[:, k, :], xf[:, k, :], ACT.Copy).then_inc(x_hi, 1)

            @block.vector
            def _(dve):
                for k in range(KD):
                    dve.wait_ge(x_hi, k + 1)
                    nc.vector.tensor_tensor(xl[:, k, :], xf[:, k, :], f(xh[:, k, :]), ALU.subtract)
        m.mem.drop("x_full")
        u_raw = sb("u_raw", [P, NU, D])
        v_raw = sb("v_raw", [P, NV, D])
        uh = sb("u_hi", [P, 2, D], F32R)
        ul = sb("u_lo", [P, 2, D], F32R)
        vh = sb("v_hi", [P, BODY, D], F32R)
        vl = sb("v_lo", [P, BODY, D], F32R)
        gt = sb("gate_tile", [P, NGB, T])
        ge = sb("gelu_tile", [P, 2, T])
        af = sb("act_tile", [P, 2, T])
        ah = sb("act_hi", [P, BODY, T], F32R)
        al = sb("act_lo", [P, BODY, T], F32R)
        nt = NK // BODY

        with nc.Block() as block:
            @block.sync
            def _(sp):
                def load_u(n, slot):
                    sp.dma_start(u_raw[:, slot, :], u_rows[bass.ds(n, 1)].rearrange("o p d -> p (o d)")
                                 ).then_inc(u_in[slot], 16)

                def load_v(n, slot):
                    sp.dma_start(v_raw[:, slot, :], v_rows[bass.ds(n, 1)].rearrange("o p d -> p (o d)")
                                 ).then_inc(v_in[slot], 16)

                def load_gates(n, slot):
                    sp.dma_start(gt[:, slot, :], gates[bass.ds(n, 1)].rearrange("o p t -> p (o t)")
                                 ).then_inc(g_in[slot], 16)

                def body(it, last=False):
                    for half in range(2):
                        for q in range(GT):
                            jj = half * GT + q
                            n = it * BODY + jj
                            if not (last and jj + NU >= BODY):
                                sp.wait_ge(u_ready, n + 1)
                                load_u(n + NU, jj % NU)
                            if not (last and jj + NGB >= BODY):
                                sp.wait_ge(gated, n + 1)
                                load_gates(n + NGB, jj % NGB)
                        for q in range(GT):
                            jj = half * GT + q
                            if not (last and jj + NV >= BODY):
                                sp.wait_ge(v_ready, it * BODY + jj + 1)
                                load_v(it * BODY + jj + NV, jj % NV)

                for n in range(NU):
                    load_u(n, n)
                    load_gates(n, n)
                for n in range(NV):
                    load_v(n, n)
                with sp.Fori(0, nt - 1) as it:
                    body(it)
                body(nt - 1, last=True)
                sp.wait_ge(added, 8 * NG)
                sp.dma_start(out[0].rearrange("(b p) d -> p b d", p=P), acc[:]).then_inc(out_done, 16)
                sp.wait_ge(out_done, 16)

            @block.tensor
            def _(pe):
                def up(it, jj):
                    n = it * BODY + jj
                    pe.wait_ge(u_ready, n + 1)
                    if not (isinstance(it, int) and it == 0 and jj < 2):
                        pe.wait_ge(gelu_done, n - 1)
                    q, bank = jj % 2, bank_up[jj % 2]
                    for k in range(KD):
                        w = slice(k * P, (k + 1) * P)
                        nc.tensor.matmul(bank[:], uh[:, q, w], xh[:, k, :], start=(k == 0), stop=False)
                        nc.tensor.matmul(bank[:], uh[:, q, w], xl[:, k, :], start=False, stop=False)
                        t = nc.tensor.matmul(bank[:], ul[:, q, w], xh[:, k, :], start=False, stop=(k == KD - 1))
                    t.then_inc(up_done, 1)

                def down(g, half, first):
                    pe.wait_ge(gated, GT * (g + 1))
                    pe.wait_ge(v_ready, GT * (g + 1))
                    for o in range(8):
                        b, dh = o // 2, o % 2
                        if not (first and o < 4):
                            pe.wait_ge(added, 8 * g + o - 3)
                        bank = bank_down[o % 4]
                        for e in range(GT):
                            s = half * GT + e
                            w, c = slice(b * P, (b + 1) * P), slice(dh * T, (dh + 1) * T)
                            nc.tensor.matmul(bank[:], ah[:, s, w], vh[:, s, c], start=(e == 0), stop=False)
                            nc.tensor.matmul(bank[:], ah[:, s, w], vl[:, s, c], start=False, stop=False)
                            t = nc.tensor.matmul(bank[:], al[:, s, w], vh[:, s, c], start=False, stop=(e == GT - 1))
                        t.then_inc(down_done, 1)

                def body(it):
                    for half in range(2):
                        for q in range(GT):
                            up(it, half * GT + q)
                        if half or not isinstance(it, int):
                            down(it * 2 + half - 1, 1 - half, isinstance(it, int))
                body(0)
                with pe.Fori(1, nt) as it:
                    body(it)
                down(NG - 1, 1, False)

            @block.scalar
            def _(act):
                def split_u(it, jj):
                    n = it * BODY + jj
                    act.wait_ge(u_in[jj % NU], 16 * (it * (BODY // NU) + jj // NU + 1))
                    if not (isinstance(it, int) and it == 0 and jj < 2):
                        act.wait_ge(up_done, n - 1)
                    nc.scalar.activation(uh[:, jj % 2, :], u_raw[:, jj % NU, :], ACT.Copy).then_inc(u_hi_ready, 1)

                def body(it, last=False):
                    for half in range(2):
                        for q in range(GT):
                            jj = half * GT + q
                            n = it * BODY + jj
                            act.wait_ge(up_done, n + 1)
                            if not (isinstance(it, int) and it == 0 and jj < 2):
                                act.wait_ge(gated, n - 1)
                            nc.scalar.activation(ge[:, jj % 2, :], bank_up[jj % 2][:], ACT.Gelu).then_inc(gelu_done, 1)
                            if jj + 2 < BODY:
                                split_u(it, jj + 2)
                            elif not last:
                                split_u(it + 1, jj + 2 - BODY)
                        for q in range(GT):
                            jj = half * GT + q
                            n = it * BODY + jj
                            act.wait_ge(v_in[jj % NV], 16 * (it * (BODY // NV) + jj // NV + 1))
                            if not (isinstance(it, int) and it == 0) and q == 0:
                                act.wait_ge(down_done, 8 * (it * 2 + half - 1))
                            nc.scalar.activation(vh[:, jj, :], v_raw[:, jj % NV, :], ACT.Copy).then_inc(v_hi_ready, 1)
                split_u(0, 0)
                split_u(0, 1)
                body(0)
                with act.Fori(1, nt - 1) as it:
                    body(it)
                body(nt - 1, last=True)

            @block.vector
            def _(dve):
                def split_u(it, jj):
                    n = it * BODY + jj
                    dve.wait_ge(u_hi_ready, n + 1)
                    nc.vector.tensor_tensor(ul[:, jj % 2, :], u_raw[:, jj % NU, :], f(uh[:, jj % 2, :]),
                                            ALU.subtract).then_inc(u_ready, 1)

                def add(g, o):
                    dve.wait_ge(down_done, 8 * g + o + 1)
                    v_ = acc[:, o // 2, (o % 2) * T:(o % 2 + 1) * T]
                    nc.vector.tensor_tensor(v_, v_, bank_down[o % 4][:], ALU.add).then_inc(added, 1)

                def body(it, last=False):
                    zero = isinstance(it, int) and it == 0
                    for half in range(2):
                        for q in range(GT):
                            jj = half * GT + q
                            n = it * BODY + jj
                            dve.wait_ge(gelu_done, n + 1)
                            dve.wait_ge(g_in[jj % NGB], 16 * (it * (BODY // NGB) + jj // NGB + 1))
                            if not zero and q == 0:
                                dve.wait_ge(down_done, 8 * (it * 2 + half - 1))
                            nc.vector.tensor_tensor(af[:, jj % 2, :], ge[:, jj % 2, :], gt[:, jj % NGB, :],
                                                    ALU.mult).then_inc(gate_f, 1)
                            dve.wait_ge(gate_f, n + 1)
                            nc.vector.tensor_scalar(ah[:, jj, :], af[:, jj % 2, :], 1.0, None, ALU.mult
                                                    ).then_inc(gate_hi, 1)
                            dve.wait_ge(gate_hi, n + 1)
                            nc.vector.tensor_tensor(al[:, jj, :], af[:, jj % 2, :], f(ah[:, jj, :]),
                                                    ALU.subtract).then_inc(gated, 1)
                            if jj + 2 < BODY:
                                split_u(it, jj + 2)
                            elif not last:
                                split_u(it + 1, jj + 2 - BODY)
                        for q in range(GT):
                            jj = half * GT + q
                            n = it * BODY + jj
                            if half or not zero:
                                add(it * 2 + half - 1, 2 * q)
                                add(it * 2 + half - 1, 2 * q + 1)
                            dve.wait_ge(v_hi_ready, n + 1)
                            nc.vector.tensor_tensor(vl[:, jj, :], v_raw[:, jj % NV, :], f(vh[:, jj, :]),
                                                    ALU.subtract).then_inc(v_ready, 1)
                split_u(0, 0)
                split_u(0, 1)
                body(0)
                with dve.Fori(1, nt - 1) as it:
                    body(it)
                body(nt - 1, last=True)
                for o in range(8):
                    add(NG - 1, o)


def hybrid_layer(nc, a, out):
    gates = nc.dram_tensor("gates", [NK, NK, T], F32, kind="Internal").ap()
    h_dram = nc.dram_tensor("h_spill", [P, TB, D], F32, kind="Internal").ap()
    x_dram = nc.dram_tensor("x_spill", [P, KD, T], F32, kind="Internal").ap()
    with ExitStack() as ctx:
        sem = lambda name: ctx.enter_context(nc.semaphore(name))
        ps = [ctx.enter_context(nc.psum_tensor(f"bank{i}", [P, 512], F32)) for i in range(8)]
        mem = Memory(nc)
        m = Tensors()
        m.mem = mem
        m.ident = mem.take("ident", [P, P])
        m.neg_half = mem.take("neg_half", [P, 1])
        m.acc = mem.take("acc", [P, TB, D])
        m.upper = mem.take("upper", [P, P])
        m.lower = mem.take("lower", [P, P])
        m.chunk_ones = mem.take("chunk_ones", [P, P])
        m.blockdiag = mem.take("blockdiag", [P, 6, P])
        m.levels = mem.take("levels", [P, 6, P])
        m.att_mask = mem.take("att_mask", [P, 2 * P])
        m.kva = mem.take("kva", [P, TB, 2 * KVW])
        m.z = mem.take("z", [P, TB, DNW])
        m.ab = mem.take("ab", [P, TB, 2 * DN])
        m.qa = mem.take("qa", [P, TB, ATT])
        m.convin = mem.take("convin", [P, CT, T + TAPS - 1])
        m.g = mem.take("g", [P, TB, DN])
        m.beta = mem.take("beta", [P, TB, DN])
        constants(nc, m, sem)
        input_projection(nc, m, ps, sem, a["x"], a["norm_mix_g"], a["w_in"])
        m.tok = mem.take("tok", [P, CT, T])
        m.unitT = mem.take("unitT", [P, 2 * DN, T])
        m.attqT = mem.take("attqT", [P, GRP, T])
        m.attkT = mem.take("attkT", [P, T])
        conv_and_norms(nc, m, ps, sem, a["dn_conv_w"], a["dn_a_log"], a["dn_dt_bias"], a["att_q_norm_g"],
                       a["att_k_norm_g"])
        mem.drop("convin", "qa", "ab")
        m.wT = mem.take("wT", [P, TB, DN, P])
        m.u = mem.take("u", [P, TB, DN, P])
        m.qkT = mem.take("qkT", [P, TB, DN, P])
        m.qdT = mem.take("qdT", [P, TB, DN, P])
        m.kdec = mem.take("kdec", [P, DN, T])
        m.egrow = mem.take("egrow", [P, TB, DN, P])
        delta_prepare(nc, m, ps, sem)
        mem.drop("tok", "unitT", "g", "beta", "upper", "lower", "chunk_ones", "blockdiag", "levels")
        m.mix = mem.take("mix", [P, TB, D])
        mixers(nc, m, ps, sem, a["att_sinks"], a["att_out_norm_g"], a["dn_out_norm_g"])
        mem.drop("kva", "z", "wT", "u", "qkT", "qdT", "kdec", "egrow", "attqT", "attkT", "att_mask")
        m.qT = mem.take("qT", [P, PH, T])
        m.xn2T = mem.take("xn2T", [P, KD, T])
        output_projection(nc, m, ps, sem, a["w_out"], a["norm_ffn_g"], a["peer_w_q"],
                          h_dram, x_dram)
        mem.drop("mix", "acc", "xn2T")
        routing(nc, m, ps, sem, a["peer_sub_keys"], gates)
        mem.drop("qT")
        experts(nc, m, ps, sem, a["peer_u"], a["peer_v"], gates, h_dram, x_dram, out)


def kernel(**inputs):
    import numpy as np
    import concourse.bacc as bacc
    from concourse.bass_utils import run_bass_kernel_spmd

    a = {name: np.asarray(value) for name, value in inputs.items()}
    a["dn_conv_w"] = a["dn_conv_w"][0].reshape(TAPS, CT, P).transpose(2, 0, 1).reshape(P, TAPS * CT)
    a["peer_sub_keys"] = a["peer_sub_keys"][0].transpose(1, 3, 0, 2).reshape(P, PH * NK)
    a["peer_u"] = a["peer_u"][0].reshape(NK, NK, KD, P).transpose(1, 3, 2, 0).reshape(NK, P, D)
    nc = bacc.Bacc("TRN2", target_bir_lowering=False, num_devices=1)
    arrays, aps = {}, {}
    for name, value in a.items():
        value = np.ascontiguousarray(value)
        arrays["in_" + name] = value
        aps[name] = nc.dram_tensor("in_" + name, value.shape, mybir.dt.from_np(value.dtype),
                                   kind="ExternalInput").ap()
    out = nc.dram_tensor("out_0", (1, T, D), F32, kind="ExternalOutput").ap()
    hybrid_layer(nc, aps, out)
    r = run_bass_kernel_spmd(nc, [arrays], core_ids=[0])
    return r.results[0]["out_0"]
```

```python
from contextlib import ExitStack

import concourse.bass as bass
from concourse import mybir

P = 128
T = 512
TB = T // P
D = 1024
KD = D // P
EPS = 1e-6

HD = 64
NH = 8
NKV = 2
GRP = NH // NKV
ATT = NH * HD
KVW = NKV * HD

DH = 128
DN = 4
DNW = DN * DH
TAPS = 4
CH = 64
CT = 3 * DN

W_TOK = ATT + 2 * KVW
W_CONV0 = W_TOK
W_AB0 = W_CONV0 + 3 * DNW
W_Z0 = W_AB0 + 2 * DN
W_END = W_Z0 + DNW

PH = 8
NK = 128
HALF = 64
TOPK = 16
HA = PH * TOPK
PAIRS = [(0, 1, 16), (1, 1, 8), (2, 1, 5), (3, 1, 4), (4, 1, 3), (5, 3, 2), (8, 8, 1)]
NPAIR = sum(r * w for _, r, w in PAIRS)

GT = 4
NG = NK // GT
EARLY = 24
GJ = 2 * GT
BIG = 3.0e38

F32 = mybir.dt.float32
F32R = mybir.dt.float32r
U32 = mybir.dt.uint32
ALU = mybir.AluOpType
ACT = mybir.ActivationFunctionType
AX = mybir.AxisListType.X


def chain(eng, sem, count):
    def link(ins):
        count[0] += 1
        ins.then_inc(sem, 1)
        eng.wait_ge(sem, count[0])
    return link


class Banks:

    def __init__(self, banks, done, taken):
        self.banks, self.done, self.taken = banks, done, taken
        self.names, self.consumer = [], []

    def add(self, name, consumer):
        self.names.append(name)
        self.consumer.append(consumer)

    def n(self, name):
        return self.names.index(name)

    def bank(self, name):
        return self.banks[self.n(name) % len(self.banks)]

    def rank(self, n):
        return self.consumer[:n + 1].count(self.consumer[n])

    def wait_free(self, pe, name):
        n = self.n(name) - len(self.banks)
        if n >= 0:
            pe.wait_ge(self.taken[self.consumer[n]], self.rank(n))

    def wait_full(self, eng, name):
        eng.wait_ge(self.done, self.n(name) + 1)

    def wait_taken(self, eng, name):
        n = self.n(name)
        eng.wait_ge(self.taken[self.consumer[n]], self.rank(n))


class Tensors:
    pass


class Memory:

    def __init__(self, nc):
        self.nc, self.live = nc, {}

    def take(self, name, shape, dt=F32, at_end=False):
        size = 4
        for n in shape[1:]:
            size *= n
        size = -(-size // 64) * 64
        at = -(-self.nc.sbuf_base // 64) * 64
        gaps = []
        for a, b in sorted(self.live.values()) + [(self.nc.sbuf_usable_end // 64 * 64, 0)]:
            if a - at >= size:
                gaps.append((at, a - size))
            at = max(at, b)
        assert gaps, (name, size, self.live)
        at = gaps[-1][1] if at_end else gaps[0][0]
        self.live[name] = (at, at + size)
        return self.nc.alloc_sbuf_tensor_at(name, shape, dt, offset=at)

    def drop(self, *names):
        for name in names:
            del self.live[name]

    def local(self, ctx):
        def sb(name, shape, dt=F32):
            t = self.take(name, shape, dt)
            ctx.callback(self.drop, name)
            return t
        return sb


def constants(nc, m, sem):
    made = sem("masks_made")
    with nc.Block() as block:
        @block.gpsimd
        def _(pool):
            link = chain(pool, made, [0])
            nc.gpsimd.memset(m.ident[:], 0.0)
            nc.gpsimd.memset(m.upper[:], 0.0)
            nc.gpsimd.memset(m.lower[:], 0.0)
            nc.gpsimd.memset(m.chunk_ones[:], 0.0)
            nc.gpsimd.memset(m.convin[:, :, 0:TAPS - 1], 0.0)
            nc.gpsimd.memset(m.neg_half[:], -0.5)
            nc.gpsimd.memset(m.att_mask[:], 0.0)
            link(nc.gpsimd.memset(m.blockdiag[:], 1.0))
            for q in range(P // CH):
                a = slice(q * CH, (q + 1) * CH)
                nc.gpsimd.memset(m.upper[a, a], 1.0)
                nc.gpsimd.memset(m.lower[a, a], 1.0)
                link(nc.gpsimd.memset(m.chunk_ones[a, a], 1.0))
            nc.gpsimd.affine_select(out=m.ident[:], in_=m.ident[:], compare_op=ALU.not_equal, fill=1.0,
                                    base=0, pattern=[[-1, P]], channel_multiplier=1)
            nc.gpsimd.affine_select(out=m.upper[:], in_=m.upper[:], compare_op=ALU.is_ge, fill=0.0,
                                    base=0, pattern=[[1, P]], channel_multiplier=-1)
            nc.gpsimd.affine_select(out=m.lower[:], in_=m.lower[:], compare_op=ALU.is_gt, fill=0.0,
                                    base=0, pattern=[[-1, P]], channel_multiplier=1)
            nc.gpsimd.affine_select(out=m.att_mask[:, 0:P], in_=m.att_mask[:, 0:P], compare_op=ALU.is_gt,
                                    fill=-1e30, base=0, pattern=[[1, P]], channel_multiplier=-1)
            nc.gpsimd.affine_select(out=m.att_mask[:, P:2 * P], in_=m.att_mask[:, P:2 * P],
                                    compare_op=ALU.is_ge, fill=-1e30, base=0, pattern=[[-1, P]],
                                    channel_multiplier=1)
            for l in range(6):
                s = 1 << l
                v = m.blockdiag[:, l, :].rearrange("p (b r) -> p b r", r=s)
                link(nc.gpsimd.affine_select(out=v, in_=v, compare_op=ALU.is_ge, fill=0.0, base=0,
                                             pattern=[[-s, P // s], [0, s]], channel_multiplier=1))
                link(nc.gpsimd.affine_select(out=v, in_=v, compare_op=ALU.is_ge, fill=0.0, base=s - 1,
                                             pattern=[[s, P // s], [0, s]], channel_multiplier=-1))
            for l in range(6):
                above = m.blockdiag[:, l + 1, :] if l < 5 else m.chunk_ones[:]
                nc.gpsimd.tensor_tensor(m.levels[:, l, :], above, m.blockdiag[:, l, :], ALU.subtract)


def input_projection(nc, m, ps, sem, x, norm_mix_g, w_in):
    x_in = [sem(f"x_in{b}") for b in range(TB)]
    g_in = sem("mix_gain_in")
    w_cols = [(W_CONV0 + 512 * c, 512) for c in range(3)] + [(0, 512), (512, W_TOK - 512),
                                                            (W_AB0, W_END - W_AB0)]
    w_ld = [sem(f"w_in{i}") for i in range(len(w_cols))]
    squares, scale, normed, done = sem("x_squares"), sem("x_scale"), sem("x_normed"), sem("proj_done")
    plink, vlink = sem("proj_pool"), sem("proj_dve")
    banks = Banks(ps, done, {"act": sem("proj_act"), "dve": sem("proj_vec")})
    for b in range(TB):
        for half in range(2):
            banks.add(("xT", b, half), "act")
    for c in range(3):
        for i in range(4):
            banks.add(("conv", c, i), "dve" if i % 2 else "act")
    for b in range(TB):
        banks.add(("tok0", b), "act")
    for b in range(TB):
        banks.add(("tok1", b), "dve")
    for b in range(TB):
        banks.add(("ab", b), "act")
        banks.add(("z", b), "dve")
    wview = w_in[0].rearrange("(k p) n -> p k n", p=P)
    last = [("conv", c, 3) for c in range(3)] + [("tok0", TB - 1), ("tok1", TB - 1), ("z", TB - 1)]

    with ExitStack() as ctx:
        sb = m.mem.local(ctx)
        gain = sb("mix_gain", [P, D])
        xn = sb("xn", [P, 2, D])
        junk = sb("x_junk", [P, D])
        xnT = sb("xnT", [P, KD, T])
        wbuf = sb("wbuf", [P, 3, KD, 520])
        ss = sb("x_ss", [P, TB])
        with nc.Block() as block:
            @block.sync
            def _(sp):
                xv = x[0].rearrange("(b p) d -> b p d", p=P)
                for b in range(TB):
                    sp.dma_start(m.acc[:, b, :], xv[b]).then_inc(x_in[b], 16)
                sp.dma_start(gain[:], norm_mix_g[0:1, :].broadcast_to([P, D])).then_inc(g_in, 16)
                for i, (c0, n) in enumerate(w_cols):
                    if i >= 3:
                        sp.wait_ge(done, banks.n(last[i - 3]) + 1)
                    sp.dma_start(wbuf[:, i % 3, :, 0:n], wview[:, :, c0:c0 + n]).then_inc(w_ld[i], 16)

            @block.gpsimd
            def _(pool):
                link = chain(pool, plink, [0])
                for b in range(TB):
                    pool.wait_ge(squares, b + 1)
                    link(nc.gpsimd.tensor_scalar(ss[:, b:b + 1], ss[:, b:b + 1], 1.0 / D, EPS, ALU.mult, ALU.add))
                    nc.gpsimd.tensor_tensor(ss[:, b:b + 1], ss[:, b:b + 1], m.neg_half[:, 0:1],
                                            ALU.pow).then_inc(scale, 1)

            @block.scalar
            def _(act):
                for b in range(TB):
                    act.wait_ge(x_in[b], 16)
                    if b:
                        act.wait_ge(squares, b)
                    nc.scalar.activation(junk[:], m.acc[:, b, :], ACT.Square,
                                         accum_out=ss[:, b:b + 1]).then_inc(squares, 1)
                for b in range(TB):
                    for half in range(2):
                        g = ("xT", b, half)
                        banks.wait_full(act, g)
                        nc.scalar.activation(xnT[:, 4 * half:4 * half + 4, b * P:(b + 1) * P],
                                             banks.bank(g)[:].rearrange("p (k t) -> p k t", k=4),
                                             ACT.Copy).then_inc(banks.taken["act"], 1)
                for c in range(3):
                    for i in (0, 2):
                        g = ("conv", c, i)
                        banks.wait_full(act, g)
                        nc.scalar.activation(m.convin[:, 4 * c + i, TAPS - 1:], banks.bank(g)[:],
                                             ACT.Copy).then_inc(banks.taken["act"], 1)
                for b in range(TB):
                    banks.wait_full(act, ("tok0", b))
                    nc.scalar.activation(m.qa[:, b, :], banks.bank(("tok0", b))[:],
                                         ACT.Copy).then_inc(banks.taken["act"], 1)
                for b in range(TB):
                    banks.wait_full(act, ("ab", b))
                    nc.scalar.activation(m.ab[:, b, :], banks.bank(("ab", b))[:, 0:2 * DN],
                                         ACT.Copy).then_inc(banks.taken["act"], 1)

            @block.vector
            def _(dve):
                dve.wait_ge(g_in, 16)
                for b in range(TB):
                    dve.wait_ge(scale, b + 1)
                    if b >= 2:
                        dve.wait_ge(done, 2 * (b - 1))
                    nc.vector.scalar_tensor_tensor(xn[:, b % 2, :], m.acc[:, b, :], ss[:, b:b + 1], gain[:],
                                                   ALU.mult, ALU.mult).then_inc(normed, 1)
                for c in range(3):
                    for i in (1, 3):
                        g = ("conv", c, i)
                        banks.wait_full(dve, g)
                        nc.vector.tensor_copy(m.convin[:, 4 * c + i, TAPS - 1:],
                                              banks.bank(g)[:]).then_inc(banks.taken["dve"], 1)
                for b in range(TB):
                    banks.wait_full(dve, ("tok1", b))
                    nc.vector.tensor_copy(m.kva[:, b, :], banks.bank(("tok1", b))[:, 0:2 * KVW]
                                          ).then_inc(banks.taken["dve"], 1)
                for b in range(TB):
                    banks.wait_full(dve, ("z", b))
                    nc.vector.tensor_copy(m.z[:, b, :], banks.bank(("z", b))[:]).then_inc(banks.taken["dve"], 1)

            @block.tensor
            def _(pe):
                for b in range(TB):
                    pe.wait_ge(normed, b + 1)
                    for half in range(2):
                        g = ("xT", b, half)
                        for k in range(4):
                            kk = 4 * half + k
                            t = nc.tensor.transpose(banks.bank(g)[:, k * P:(k + 1) * P],
                                                    xn[:, b % 2, kk * P:(kk + 1) * P], m.ident[:])
                        t.then_inc(done, 1)
                banks.wait_taken(pe, ("xT", TB - 1, 1))
                for c in range(3):
                    pe.wait_ge(w_ld[c], 16)
                    for i in range(4):
                        g = ("conv", c, i)
                        banks.wait_free(pe, g)
                        for k in range(KD):
                            t = nc.tensor.matmul(banks.bank(g)[:], wbuf[:, c, k, i * P:(i + 1) * P], xnT[:, k, :],
                                                 start=(k == 0), stop=(k == KD - 1))
                        t.then_inc(done, 1)

                def by_token(g, b, slot, c0, n):
                    banks.wait_free(pe, g)
                    for k in range(KD):
                        t = nc.tensor.matmul(banks.bank(g)[:, 0:n], xnT[:, k, b * P:(b + 1) * P],
                                             wbuf[:, slot, k, c0:c0 + n], start=(k == 0), stop=(k == KD - 1))
                    t.then_inc(done, 1)

                pe.wait_ge(w_ld[3], 16)
                for b in range(TB):
                    by_token(("tok0", b), b, 0, 0, 512)
                pe.wait_ge(w_ld[4], 16)
                for b in range(TB):
                    by_token(("tok1", b), b, 1, 0, W_TOK - 512)
                pe.wait_ge(w_ld[5], 16)
                for b in range(TB):
                    by_token(("ab", b), b, 2, 0, 2 * DN)
                    by_token(("z", b), b, 2, 2 * DN, DNW)


def conv_and_norms(nc, m, ps, sem, conv_w, a_log, dt_bias, q_norm_g, k_norm_g):
    small_in = [sem(f"small_in{i}") for i in range(5)]
    convd, silud, done = sem("conv_done"), sem("silu_done"), sem("norms_done")
    squared, summed, scaled = sem("qk_squared"), sem("qk_summed"), sem("qk_scaled")
    unit, att_sq, att_pow, att_unit = sem("qk_unit"), sem("att_squares"), sem("att_pow"), sem("att_unit")
    z1, z2, z3, b2 = sem("gate_z"), sem("gate_softplus"), sem("gate_alog"), sem("gate_beta")
    plink, vlink, alink = sem("norms_pool"), sem("norms_dve"), sem("norms_act")
    banks = Banks(ps, done, {"act": sem("norms_by_act"), "dve": sem("norms_by_dve")})
    for c in range(CT):
        banks.add(("tok", c), "act")
    for b in range(TB):
        banks.add(("attq", b), "dve")
        banks.add(("attk", b), "dve")
    for c in range(2 * DN):
        banks.add(("unitT", c), "act")

    with ExitStack() as ctx:
        sb = m.mem.local(ctx)
        wconv = sb("wconv", [P, TAPS, CT])
        convT = sb("convT", [P, CT, T])
        sq = sb("qk_sq", [P, 2 * DN, T])
        ssd = sb("qk_ss", [P, 2 * DN, TB])
        att_sqr = sb("att_sqr", [P, TB, ATT + KVW])
        ssa = sb("att_ss", [P, TB, NH + NKV])
        qg = sb("att_qg", [P, HD])
        kg = sb("att_kg", [P, HD])
        alog = sb("alog", [P, DN])
        dtb = sb("dtb", [P, DN])
        zz = sb("gate_zz", [P, TB, DN])
        za = sb("gate_za", [P, TB, DN])
        eb = sb("gate_eb", [P, TB, DN])
        qn = sb("att_qn", [P, TB, ATT])
        kn = sb("att_kn", [P, TB, KVW])
        with nc.Block() as block:
            @block.sync
            def _(sp):
                sp.dma_start(wconv[:].rearrange("p j c -> p (j c)"), conv_w).then_inc(small_in[0], 16)
                sp.dma_start(alog[:], a_log[0:1, :].broadcast_to([P, DN])).then_inc(small_in[1], 16)
                sp.dma_start(dtb[:], dt_bias[0:1, :].broadcast_to([P, DN])).then_inc(small_in[2], 16)
                sp.dma_start(qg[:], q_norm_g[0:1, :].broadcast_to([P, HD])).then_inc(small_in[3], 16)
                sp.dma_start(kg[:], k_norm_g[0:1, :].broadcast_to([P, HD])).then_inc(small_in[4], 16)

            @block.vector
            def _(dve):
                link = chain(dve, vlink, [0])
                dve.wait_ge(small_in[2], 16)
                nc.vector.tensor_tensor(zz[:], m.ab[:, :, 0:DN], dtb[:].unsqueeze(1).broadcast_to([P, TB, DN]),
                                        ALU.add).then_inc(z1, 1)
                nc.vector.tensor_tensor(att_sqr[:, :, 0:ATT], m.qa[:], m.qa[:], ALU.mult)
                link(nc.vector.tensor_tensor(att_sqr[:, :, ATT:], m.kva[:, :, 0:KVW], m.kva[:, :, 0:KVW], ALU.mult))
                for b in range(TB):
                    t = nc.vector.tensor_reduce(ssa[:, b, :], att_sqr[:, b, :].rearrange("p (h d) -> p h d", d=HD),
                                                AX, ALU.add)
                t.then_inc(att_sq, 1)
                dve.wait_ge(small_in[0], 16)
                for c0 in range(0, CT, 4):
                    for j in range(TAPS):
                        for c in range(c0, c0 + 4):
                            w = wconv[:, j, c:c + 1]
                            if j == 0:
                                t = nc.vector.tensor_scalar(convT[:, c, :], m.convin[:, c, 0:T], w, None, ALU.mult)
                            else:
                                t = nc.vector.scalar_tensor_tensor(convT[:, c, :], m.convin[:, c, j:j + T], w,
                                                                   convT[:, c, :], ALU.mult, ALU.add)
                        if j < TAPS - 1:
                            link(t)
                    t.then_inc(convd, 1)
                dve.wait_ge(att_pow, 1)
                dve.wait_ge(small_in[3], 16)
                dve.wait_ge(small_in[4], 16)
                for b in range(TB):
                    qv = qn[:, b, :].rearrange("p (g v d) -> p v g d", v=NKV, g=GRP)
                    kv = kn[:, b, :].rearrange("p (h d) -> p h d", d=HD)
                    nc.vector.tensor_tensor(qv, m.qa[:, b, :].rearrange("p (v g d) -> p v g d", v=NKV, g=GRP),
                                            ssa[:, b, 0:NH].rearrange("p (v g) -> p v g", v=NKV).unsqueeze(3)
                                            .broadcast_to([P, NKV, GRP, HD]), ALU.mult)
                    link(nc.vector.tensor_tensor(kv, m.kva[:, b, 0:KVW].rearrange("p (h d) -> p h d", d=HD),
                                                 ssa[:, b, NH:].unsqueeze(2).broadcast_to([P, NKV, HD]), ALU.mult))
                    qh = qn[:, b, :].rearrange("p (h d) -> p h d", d=HD)
                    nc.vector.tensor_tensor(qh, qh, qg[:].unsqueeze(1).broadcast_to([P, NH, HD]), ALU.mult)
                    nc.vector.tensor_tensor(kv, kv, kg[:].unsqueeze(1).broadcast_to([P, NKV, HD]),
                                            ALU.mult).then_inc(att_unit, 1)
                for c in range(2 * DN):
                    dve.wait_ge(squared, c + 1)
                    t = nc.vector.tensor_reduce(ssd[:, c, :], sq[:, c, :].rearrange("p (b d) -> p b d", d=DH),
                                                AX, ALU.add)
                t.then_inc(summed, 1)
                for b in range(TB):
                    banks.wait_full(dve, ("attq", b))
                    nc.vector.tensor_scalar(m.attqT[:, :, b * P:(b + 1) * P],
                                            banks.bank(("attq", b))[:].rearrange("p (g t) -> p g t", g=GRP),
                                            HD ** -0.5, None, ALU.mult).then_inc(banks.taken["dve"], 1)
                    banks.wait_full(dve, ("attk", b))
                    nc.vector.tensor_copy(m.attkT[:, b * P:(b + 1) * P],
                                          banks.bank(("attk", b))[:, 0:P]).then_inc(banks.taken["dve"], 1)
                dve.wait_ge(scaled, 1)
                for c in range(2 * DN):
                    v = m.tok[:, c, :].rearrange("p (b d) -> p b d", d=DH)
                    nc.vector.tensor_tensor(v, v, ssd[:, c, :].unsqueeze(2).broadcast_to([P, TB, DH]),
                                            ALU.mult).then_inc(unit, 1)
                dve.wait_ge(z2, 1)
                link(nc.vector.scalar_tensor_tensor(zz[:], zz[:], 0.0, za[:], ALU.max, ALU.add))
                dve.wait_ge(z3, 1)
                nc.vector.scalar_tensor_tensor(m.g[:], zz[:], -1.0,
                                               alog[:].unsqueeze(1).broadcast_to([P, TB, DN]), ALU.mult, ALU.mult)
                dve.wait_ge(b2, 1)
                link(nc.vector.tensor_scalar(eb[:], eb[:], 1.0, None, ALU.add))
                nc.vector.reciprocal(m.beta[:], eb[:])

            @block.gpsimd
            def _(pool):
                link = chain(pool, plink, [0])
                pool.wait_ge(att_sq, 1)
                link(nc.gpsimd.tensor_scalar(ssa[:], ssa[:], 1.0 / HD, EPS, ALU.mult, ALU.add))
                nc.gpsimd.tensor_tensor(ssa[:], ssa[:], m.neg_half[:, 0:1].unsqueeze(2)
                                        .broadcast_to([P, TB, NH + NKV]), ALU.pow).then_inc(att_pow, 1)
                pool.wait_ge(summed, 1)
                link(nc.gpsimd.tensor_scalar(ssd[:], ssd[:], EPS, None, ALU.add))
                link(nc.gpsimd.tensor_tensor(ssd[:], ssd[:], m.neg_half[:, 0:1].unsqueeze(2)
                                             .broadcast_to([P, 2 * DN, TB]), ALU.pow))
                nc.gpsimd.tensor_scalar(ssd[:, 0:DN, :], ssd[:, 0:DN, :], DH ** -0.5, None,
                                        ALU.mult).then_inc(scaled, 1)

            @block.scalar
            def _(act):
                link = chain(act, alink, [0])
                act.wait_ge(small_in[1], 16)
                nc.scalar.activation(alog[:], alog[:], ACT.Exp).then_inc(z3, 1)
                nc.scalar.activation(eb[:], m.ab[:, :, DN:], ACT.Exp, scale=-1.0).then_inc(b2, 1)
                act.wait_ge(z1, 1)
                link(nc.scalar.activation(za[:], zz[:], ACT.Abs))
                link(nc.scalar.activation(za[:], za[:], ACT.Exp, scale=-1.0))
                nc.scalar.activation(za[:], za[:], ACT.Ln, bias=1.0).then_inc(z2, 1)
                for c in range(CT):
                    act.wait_ge(convd, c // 4 + 1)
                    nc.scalar.activation(convT[:, c, :], convT[:, c, :], ACT.Silu).then_inc(silud, 1)
                for c in range(CT):
                    banks.wait_full(act, ("tok", c))
                    if c < 2 * DN:
                        nc.scalar.activation(sq[:, c, :], banks.bank(("tok", c))[:], ACT.Square).then_inc(squared, 1)
                    nc.scalar.activation(m.tok[:, c, :], banks.bank(("tok", c))[:],
                                         ACT.Copy).then_inc(banks.taken["act"], 1)
                for c in range(2 * DN):
                    banks.wait_full(act, ("unitT", c))
                    nc.scalar.activation(m.unitT[:, c, :], banks.bank(("unitT", c))[:],
                                         ACT.Copy).then_inc(banks.taken["act"], 1)

            @block.tensor
            def _(pe):
                for c in range(CT):
                    banks.wait_free(pe, ("tok", c))
                    pe.wait_ge(silud, c + 1)
                    for b in range(TB):
                        t = nc.tensor.transpose(banks.bank(("tok", c))[:, b * P:(b + 1) * P],
                                                convT[:, c, b * P:(b + 1) * P], m.ident[:])
                    t.then_inc(done, 1)
                for b in range(TB):
                    pe.wait_ge(att_unit, b + 1)
                    banks.wait_free(pe, ("attq", b))
                    for g in range(GRP):
                        t = nc.tensor.transpose(banks.bank(("attq", b))[:, g * P:(g + 1) * P],
                                                qn[:, b, g * P:(g + 1) * P], m.ident[:])
                    t.then_inc(done, 1)
                    banks.wait_free(pe, ("attk", b))
                    nc.tensor.transpose(banks.bank(("attk", b))[:, 0:P], kn[:, b, :], m.ident[:]).then_inc(done, 1)
                for c in range(2 * DN):
                    banks.wait_free(pe, ("unitT", c))
                    pe.wait_ge(unit, c + 1)
                    for b in range(TB):
                        t = nc.tensor.transpose(banks.bank(("unitT", c))[:, b * P:(b + 1) * P],
                                                m.tok[:, c, b * P:(b + 1) * P], m.ident[:])
                    t.then_inc(done, 1)


def delta_prepare(nc, m, ps, sem):
    done, plink, vlink, alink = sem("prep_done"), sem("prep_pool"), sem("prep_dve"), sem("prep_act")
    diffs, decays, strict = sem("prep_diffs"), sem("prep_decays"), sem("prep_strict")
    cols, col_exp, tok_scaled, level_in = sem("gate_cols"), sem("gate_exps"), sem("tok_scaled"), sem("level_in")
    x0 = sem("solve_start")
    banks = Banks(ps, done, {"act": sem("prep_by_act"), "dve": sem("prep_by_dve")})
    banks.add("gcol", "dve")
    for b in range(TB):
        banks.add(("grow", b), "act")
    for b in range(TB):
        banks.add(("kk", b), "dve")
        banks.add(("qkT", b), "dve")
    for b in range(TB):
        banks.add(("B0T", b), "dve")
    LV = range(1, 6)
    for l in LV:
        for b in range(TB):
            banks.add(("WT", b, l), "act")
        for b in range(TB):
            if l < 5:
                banks.add(("Z", b, l), "dve")
            banks.add(("ZT", b, l), "dve")
    for b in range(TB):
        banks.add(("wT", b), "act")
        banks.add(("u", b), "dve")

    def h4(ap):
        return ap.rearrange("p (h c) -> p h c", h=DN)

    with ExitStack() as ctx:
        sb = m.mem.local(ctx)
        gc = sb("gc_col", [P, 2, TB, DN])
        egc = sb("egc_col", [P, 2, TB, DN])
        bec = sb("bec_col", [P, TB, DN])
        grow = sb("gc_row", [P, TB, DN, P])
        dec = sb("decay", [P, TB, DN, P])
        decT = sb("decayT", [P, TB, DN, P])
        mm = sb("m_low", [P, TB, DN, P])
        lev = sb("m_level", [P, 2, TB, DN, P])
        X, XT, WT = grow, dec, decT
        vb = sb("v_beta", [P, DN, T])
        kbe = sb("k_beta_decay", [P, DN, T])
        bc4 = lambda ap: ap.unsqueeze(2).broadcast_to([P, DN, P])
        with nc.Block() as block:
            @block.tensor
            def _(pe):
                gflat = m.g[:].rearrange("p b h -> p (b h)")
                nc.tensor.matmul(banks.bank("gcol")[:, 0:16], m.upper[:], gflat, start=True, stop=True)
                nc.tensor.matmul(banks.bank("gcol")[:, 16:32], m.chunk_ones[:], gflat,
                                 start=True, stop=True).then_inc(done, 1)
                for b in range(TB):
                    for h in range(DN):
                        t = nc.tensor.matmul(banks.bank(("grow", b))[:, h * P:(h + 1) * P],
                                             m.g[:, b, h:h + 1].broadcast_to([P, P]), m.upper[:],
                                             start=True, stop=True)
                    t.then_inc(done, 1)
                for b in range(TB):
                    for g, lhs in (("kk", DN), ("qkT", DN)):
                        banks.wait_free(pe, (g, b))
                        for h in range(DN):
                            rhs = m.unitT[:, (DN + h) if g == "kk" else h, b * P:(b + 1) * P]
                            t = nc.tensor.matmul(banks.bank((g, b))[:, h * P:(h + 1) * P],
                                                 m.unitT[:, DN + h, b * P:(b + 1) * P], rhs, start=True, stop=True)
                        t.then_inc(done, 1)
                for b in range(TB):
                    banks.wait_free(pe, ("B0T", b))
                    pe.wait_ge(level_in, b + 1)
                    for h in range(DN):
                        t = nc.tensor.transpose(banks.bank(("B0T", b))[:, h * P:(h + 1) * P],
                                                lev[:, 0, b, h, :], m.ident[:])
                    t.then_inc(done, 1)
                for l in LV:
                    for b in range(TB):
                        banks.wait_free(pe, ("WT", b, l))
                        pe.wait_ge(level_in, TB * l + b + 1)
                        banks.wait_taken(pe, ("ZT", b, l - 1) if l > 1 else ("B0T", b))
                        for h in range(DN):
                            t = nc.tensor.matmul(banks.bank(("WT", b, l))[:, h * P:(h + 1) * P],
                                                 lev[:, l % 2, b, h, :], XT[:, b, h, :], start=True, stop=True)
                        t.then_inc(done, 1)
                    for b in range(TB):
                        banks.wait_taken(pe, ("WT", b, l))
                        for z, lhs, rhs in (("Z", WT, X), ("ZT", X, WT)):
                            if z == "Z" and l == 5:
                                continue
                            banks.wait_free(pe, (z, b, l))
                            for h in range(DN):
                                t = nc.tensor.matmul(banks.bank((z, b, l))[:, h * P:(h + 1) * P],
                                                     lhs[:, b, h, :], rhs[:, b, h, :], start=True, stop=True)
                            t.then_inc(done, 1)
                for b in range(TB):
                    banks.wait_free(pe, ("wT", b))
                    banks.wait_taken(pe, ("ZT", b, 5))
                    pe.wait_ge(tok_scaled, 1)
                    for h in range(DN):
                        t = nc.tensor.matmul(banks.bank(("wT", b))[:, h * P:(h + 1) * P],
                                             kbe[:, h, b * P:(b + 1) * P], XT[:, b, h, :], start=True, stop=True)
                    t.then_inc(done, 1)
                    banks.wait_free(pe, ("u", b))
                    for h in range(DN):
                        t = nc.tensor.matmul(banks.bank(("u", b))[:, h * P:(h + 1) * P],
                                             XT[:, b, h, :], vb[:, h, b * P:(b + 1) * P], start=True, stop=True)
                    t.then_inc(done, 1)

            @block.scalar
            def _(act):
                link = chain(act, alink, [0])
                act.wait_ge(cols, 1)
                nc.scalar.activation(egc[:], gc[:], ACT.Exp).then_inc(col_exp, 1)
                for b in range(TB):
                    banks.wait_full(act, ("grow", b))
                    nc.scalar.activation(m.egrow[:, b], h4(banks.bank(("grow", b))[:]), ACT.Exp)
                    nc.scalar.activation(grow[:, b], h4(banks.bank(("grow", b))[:]),
                                         ACT.Copy).then_inc(banks.taken["act"], 1)
                for b in range(TB):
                    act.wait_ge(diffs, 2 * b + 2)
                    nc.scalar.activation(dec[:, b], dec[:, b], ACT.Exp, scale=-1.0)
                    nc.scalar.activation(decT[:, b], decT[:, b], ACT.Exp).then_inc(decays, 1)
                for l in LV:
                    for b in range(TB):
                        g = ("WT", b, l)
                        banks.wait_full(act, g)
                        if l > 1:
                            banks.wait_full(act, ("ZT", b, l - 1))
                        nc.scalar.activation(WT[:, b], h4(banks.bank(g)[:]), ACT.Copy).then_inc(banks.taken["act"], 1)
                for b in range(TB):
                    banks.wait_full(act, ("wT", b))
                    nc.scalar.activation(m.wT[:, b], h4(banks.bank(("wT", b))[:]),
                                         ACT.Copy).then_inc(banks.taken["act"], 1)

            @block.gpsimd
            def _(pool):
                up = m.upper[:].unsqueeze(1).broadcast_to([P, DN, P])
                low = m.lower[:].unsqueeze(1).broadcast_to([P, DN, P])
                for b in range(TB):
                    pool.wait_ge(decays, b + 1)
                    nc.gpsimd.tensor_tensor(dec[:, b], dec[:, b], low, ALU.mult).then_inc(strict, 1)
                    nc.gpsimd.tensor_tensor(decT[:, b], decT[:, b], up, ALU.mult).then_inc(strict, 1)
                for l in range(6):
                    for b in range(TB):
                        banks.wait_taken(pool, ("kk", b))
                        if l >= 2:
                            banks.wait_full(pool, ("WT", b, l - 2) if l > 2 else ("B0T", b))
                        if l == 2:
                            pool.wait_ge(x0, b + 1)
                        nc.gpsimd.tensor_tensor(lev[:, l % 2, b], mm[:, b],
                                                m.levels[:, l, :].unsqueeze(1).broadcast_to([P, DN, P]),
                                                ALU.mult).then_inc(level_in, 1)

            @block.vector
            def _(dve):
                link = chain(dve, vlink, [0])
                banks.wait_full(dve, "gcol")
                g2 = banks.bank("gcol")[:, 0:32].rearrange("p (s b h) -> p s b h", s=2, b=TB)
                link(nc.vector.tensor_copy(gc[:], g2))
                nc.vector.tensor_tensor(gc[:, 1], gc[:, 1], gc[:, 0], ALU.subtract).then_inc(cols, 1)
                dve.wait_ge(col_exp, 1)
                nc.vector.tensor_tensor(bec[:], m.beta[:], egc[:, 0], ALU.mult).then_inc(banks.taken["dve"], 1)
                for b in range(TB):
                    banks.wait_taken(dve, ("grow", b))
                    link(nc.vector.tensor_tensor(grow[:, b], grow[:, b], bc4(gc[:, 0, b, :]), ALU.subtract))
                    nc.vector.tensor_scalar(dec[:, b], grow[:, b], 0.0, None, ALU.max).then_inc(diffs, 1)
                    nc.vector.tensor_scalar(decT[:, b], grow[:, b], 0.0, None, ALU.min).then_inc(diffs, 1)
                for h in range(DN):
                    v = lambda ap: ap.rearrange("p (b d) -> p b d", d=DH)
                    s = lambda ap: ap[:, :, h].unsqueeze(2).broadcast_to([P, TB, DH])
                    nc.vector.tensor_tensor(v(vb[:, h, :]), v(m.tok[:, 2 * DN + h, :]), s(m.beta), ALU.mult)
                    nc.vector.tensor_tensor(v(kbe[:, h, :]), v(m.tok[:, DN + h, :]), s(bec), ALU.mult)
                    t = nc.vector.tensor_tensor(v(m.kdec[:, h, :]), v(m.tok[:, DN + h, :]), s(egc[:, 1]), ALU.mult)
                t.then_inc(tok_scaled, 1)
                for b in range(TB):
                    dve.wait_ge(strict, 2 * b + 2)
                    link(nc.vector.tensor_tensor(dec[:, b], dec[:, b], bc4(m.beta[:, b, :]), ALU.mult))
                    banks.wait_full(dve, ("kk", b))
                    nc.vector.tensor_tensor(mm[:, b], h4(banks.bank(("kk", b))[:]), dec[:, b],
                                            ALU.mult).then_inc(banks.taken["dve"], 1)
                    banks.wait_full(dve, ("qkT", b))
                    nc.vector.tensor_tensor(m.qkT[:, b], h4(banks.bank(("qkT", b))[:]), decT[:, b],
                                            ALU.mult).then_inc(banks.taken["dve"], 1)
                    nc.vector.tensor_tensor(m.qdT[:, b], m.unitT[:, 0:DN, b * P:(b + 1) * P], m.egrow[:, b], ALU.mult)
                idb = m.ident[:].unsqueeze(1).broadcast_to([P, DN, P])
                for b in range(TB):
                    banks.wait_full(dve, ("B0T", b))
                    nc.vector.tensor_tensor(X[:, b], idb, lev[:, 0, b], ALU.subtract).then_inc(x0, 1)
                    nc.vector.scalar_tensor_tensor(XT[:, b], h4(banks.bank(("B0T", b))[:]), -1.0, idb,
                                                   ALU.mult, ALU.add).then_inc(banks.taken["dve"], 1)
                for l in LV:
                    for b in range(TB):
                        banks.wait_full(dve, ("ZT", b, l))
                        if l < 5:
                            nc.vector.tensor_tensor(X[:, b], X[:, b], h4(banks.bank(("Z", b, l))[:]),
                                                    ALU.subtract).then_inc(banks.taken["dve"], 1)
                        nc.vector.tensor_tensor(XT[:, b], XT[:, b], h4(banks.bank(("ZT", b, l))[:]),
                                                ALU.subtract).then_inc(banks.taken["dve"], 1)
                for b in range(TB):
                    banks.wait_full(dve, ("u", b))
                    nc.vector.tensor_copy(m.u[:, b], h4(banks.bank(("u", b))[:])).then_inc(banks.taken["dve"], 1)


def mixers(nc, m, ps, sem, sinks, att_out_g, dn_out_g):
    NC = T // CH
    in_ = [sem(f"mixer_small{i}") for i in range(3)]
    ws_done, v_new, s_done, s_new, o_done, o_out = (sem(n) for n in ("ws_done", "v_new", "s_done", "s_new",
                                                                     "o_done", "o_out"))
    zeroed, o_sq, o_ss, o_pow, o_mix = sem("s_zeroed"), sem("o_sq"), sem("o_ss"), sem("o_pow"), sem("z_gate")
    vlink, alink, plink = sem("mix_dve"), sem("mix_act"), sem("mix_pool")
    sc_done, sc_out, negm, prob, den_in, p_done, p_out = (sem(n) for n in (
        "att_scores", "att_scores_out", "att_negmax", "att_probs", "att_sink_exp", "att_pT", "att_pT_out"))
    pv_done, att_o, att_ss, att_rms = (sem(n) for n in ("att_pv", "att_o", "att_ss", "att_rms"))
    bV, bO, bS, bPV = ps[0], ps[1], ps[2], ps[3]
    bA = ps[4:8]

    with ExitStack() as ctx:
        sb = m.mem.local(ctx)
        S = sb("state", [P, 2, DN, P])
        vnew = sb("v_new_t", [P, DN, P])
        ot = sb("o_tok", [P, TB, DNW])
        osq = sb("o_sqr", [P, DNW])
        oss = sb("o_sss", [P, TB, DN])
        dg = sb("dn_gain", [P, DH])
        ag = sb("att_gain", [P, ATT])
        snk = sb("sinks_b", [P, NH])
        sc = sb("att_sc", [P, NH, 2 * P])
        mx = sb("att_mx", [P, TB, NH])
        nm = sb("att_nm", [P, TB, NH])
        sm = sb("att_sm", [P, TB, NH])
        den = sb("att_den", [P, TB, NH])
        pT = sb("att_pTs", [P, 2 * NH, P])
        ao = sb("att_ot", [P, ATT])
        aj = sb("att_junk", [P, ATT])
        ass = sb("att_rss", [P, TB])
        r4 = lambda ap: ap.rearrange("p (h d) -> p h d", h=DN)
        with nc.Block() as block:
            @block.sync
            def _(sp):
                sp.dma_start(snk[:], sinks[0:1, :].broadcast_to([P, NH])).then_inc(in_[0], 16)
                sp.dma_start(ag[:], att_out_g[0:1, :].broadcast_to([P, ATT])).then_inc(in_[1], 16)
                sp.dma_start(dg[:], dn_out_g[0:1, :].broadcast_to([P, DH])).then_inc(in_[2], 16)

            @block.tensor
            def _(pe):
                def scores(b):
                    lo = 0 if b else P
                    if b:
                        pe.wait_ge(p_out, 4 * b)
                    for i in range(4):
                        v = slice(HD * (i // 2), HD * (i // 2) + HD)
                        for e in range(2):
                            g = 2 * (i % 2) + e
                            t = nc.tensor.matmul(bA[i][:, e * 2 * P + lo:(e + 1) * 2 * P],
                                                 m.attqT[v, g, b * P:(b + 1) * P],
                                                 m.attkT[v, (b - 1) * P + lo:(b + 1) * P], start=True, stop=True)
                    t.then_inc(sc_done, 1)

                def p_transposes(b):
                    for i in range(4):
                        pe.wait_ge(prob, NH * b + 2 * i + 2)
                        if i == 0:
                            pe.wait_ge(sc_out, 4 * b + 4)
                        for e in range(2):
                            for half in range(0 if b else 1, 2):
                                t = nc.tensor.transpose(bA[i][:, (2 * e + half) * P:(2 * e + half + 1) * P],
                                                        sc[:, 2 * i + e, half * P:(half + 1) * P], m.ident[:])
                        t.then_inc(p_done, 1)

                def pv(b):
                    pe.wait_ge(p_out, 4 * b + 4)
                    if b:
                        pe.wait_ge(att_o, b)
                    for h in range(NH):
                        kv = h // GRP
                        for half in range(0 if b else 1, 2):
                            t = nc.tensor.matmul(bPV[:, h * HD:(h + 1) * HD], pT[:, 2 * h + half, :],
                                                 m.kva[:, b - 1 + half, KVW + kv * HD:KVW + (kv + 1) * HD],
                                                 start=(half == 0 or b == 0), stop=(half == 1))
                    t.then_inc(pv_done, 1)

                scores(0)
                for c in range(NC):
                    b, q = c // 2, c % 2
                    r = slice(q * CH, (q + 1) * CH)
                    if c == 0:
                        pe.wait_ge(zeroed, 1)
                    else:
                        pe.wait_ge(s_new, DN * c)
                    for h in range(DN):
                        t = nc.tensor.matmul(bV[r, h * P:(h + 1) * P], m.wT[:, b, h, r], S[:, c % 2, h, :],
                                             start=True, stop=True)
                    t.then_inc(ws_done, 1)
                    if q == 0:
                        p_transposes(b)
                    else:
                        pv(b)
                        if b + 1 < TB:
                            scores(b + 1)
                    pe.wait_ge(v_new, c + 1)
                    for h in range(DN):
                        t = nc.tensor.matmul(bS[:, h * P:(h + 1) * P], m.kdec[r, h, b * P:(b + 1) * P],
                                             vnew[r, h, :], start=True, stop=True)
                    t.then_inc(s_done, 1)
                    if c:
                        pe.wait_ge(o_out, c)
                    for h in range(DN):
                        nc.tensor.matmul(bO[r, h * P:(h + 1) * P], m.qdT[:, b, h, r], S[:, c % 2, h, :],
                                         start=True, stop=False)
                        t = nc.tensor.matmul(bO[r, h * P:(h + 1) * P], m.qkT[r, b, h, r], vnew[r, h, :],
                                             start=False, stop=True)
                    t.then_inc(o_done, 1)

            @block.vector
            def _(dve):
                link = chain(dve, vlink, [0])

                def att_max(b):
                    lo = 0 if b else P
                    for i in range(4):
                        dve.wait_ge(sc_done, b + 1)
                        if i == 0 and b:
                            dve.wait_ge(p_done, 4 * b)
                        t = nc.vector.tensor_tensor(
                            sc[:, 2 * i:2 * i + 2, lo:], bA[i][:].rearrange("p (e k) -> p e k", e=2)[:, :, lo:],
                            m.att_mask[:, lo:].unsqueeze(1).broadcast_to([P, 2, 2 * P - lo]), ALU.add)
                        t.then_inc(sc_out, 1)
                    dve.wait_ge(sc_out, 4 * b + 4)
                    link(nc.vector.tensor_reduce(mx[:, b, :], sc[:, :, lo:], AX, ALU.max))
                    if b == 0:
                        dve.wait_ge(in_[0], 16)
                    link(nc.vector.tensor_tensor(mx[:, b, :], mx[:, b, :], snk[:], ALU.max))
                    link(nc.vector.tensor_tensor(sm[:, b, :], snk[:], mx[:, b, :], ALU.subtract))
                    nc.vector.tensor_scalar(nm[:, b, :], mx[:, b, :], -1.0, None, ALU.mult).then_inc(negm, 1)

                def att_out(b):
                    dve.wait_ge(den_in, b + 1)
                    link(nc.vector.tensor_tensor(den[:, b, :], den[:, b, :], sm[:, b, :], ALU.add))
                    link(nc.vector.reciprocal(den[:, b, :], den[:, b, :]))
                    dve.wait_ge(pv_done, b + 1)
                    nc.vector.tensor_tensor(ao[:].rearrange("p (h d) -> p h d", d=HD),
                                            bPV[:].rearrange("p (h d) -> p h d", d=HD),
                                            den[:, b, :].unsqueeze(2).broadcast_to([P, NH, HD]),
                                            ALU.mult).then_inc(att_o, 1)

                def att_norm(b):
                    if b == 0:
                        dve.wait_ge(in_[1], 16)
                    dve.wait_ge(att_rms, b + 1)
                    link(nc.vector.scalar_tensor_tensor(m.mix[:, b, 0:ATT], ao[:], ass[:, b:b + 1], ag[:],
                                                        ALU.mult, ALU.mult))

                def o_sum(b):
                    dve.wait_ge(o_sq, b + 1)
                    nc.vector.tensor_reduce(oss[:, b, :], r4(osq[:]), AX, ALU.add).then_inc(o_ss, 1)

                def o_norm(b):
                    dve.wait_ge(o_pow, b + 1)
                    link(nc.vector.tensor_tensor(r4(ot[:, b, :]), r4(ot[:, b, :]),
                                                 oss[:, b, :].unsqueeze(2).broadcast_to([P, DN, DH]), ALU.mult))
                    nc.vector.tensor_tensor(m.mix[:, b, ATT:], ot[:, b, :], m.z[:, b, :], ALU.mult)

                nc.vector.memset(S[:, 0], 0.0).then_inc(zeroed, 1)
                att_max(0)
                dve.wait_ge(o_mix, 1)
                dve.wait_ge(in_[2], 16)
                for b in range(TB):
                    t = nc.vector.tensor_tensor(r4(m.z[:, b, :]), r4(m.z[:, b, :]),
                                                dg[:].unsqueeze(1).broadcast_to([P, DN, DH]), ALU.mult)
                link(t)
                for c in range(NC):
                    b, q = c // 2, c % 2
                    r = slice(q * CH, (q + 1) * CH)
                    dve.wait_ge(ws_done, c + 1)
                    if c:
                        dve.wait_ge(o_done, c)
                    nc.vector.tensor_tensor(vnew[r], m.u[r, b], r4(bV[:])[r], ALU.subtract).then_inc(v_new, 1)
                    if q == 1:
                        att_out(b)
                        if b + 1 < TB:
                            att_max(b + 1)
                    dve.wait_ge(s_done, c + 1)
                    last = (q + 1) * CH - 1
                    for h in range(DN):
                        nc.vector.scalar_tensor_tensor(S[:, (c + 1) % 2, h, :], S[:, c % 2, h, :],
                                                       m.egrow[:, b, h, last:last + 1],
                                                       bS[:, h * P:(h + 1) * P], ALU.mult, ALU.add).then_inc(s_new, 1)
                    if q == 0 and b:
                        att_norm(b - 1)
                        o_sum(b - 1)
                    elif b:
                        o_norm(b - 1)
                att_norm(TB - 1)
                o_sum(TB - 1)
                o_norm(TB - 1)

            @block.gpsimd
            def _(pool):
                link = chain(pool, plink, [0])
                for b in range(TB):
                    pool.wait_ge(att_ss, b + 1)
                    link(nc.gpsimd.tensor_scalar(ass[:, b:b + 1], ass[:, b:b + 1], 1.0 / ATT, EPS, ALU.mult, ALU.add))
                    nc.gpsimd.tensor_tensor(ass[:, b:b + 1], ass[:, b:b + 1], m.neg_half[:, 0:1],
                                            ALU.pow).then_inc(att_rms, 1)
                    pool.wait_ge(o_ss, b + 1)
                    link(nc.gpsimd.tensor_scalar(oss[:, b, :], oss[:, b, :], 1.0 / DH, EPS, ALU.mult, ALU.add))
                    nc.gpsimd.tensor_tensor(oss[:, b, :], oss[:, b, :], m.neg_half[:, 0:1].broadcast_to([P, DN]),
                                            ALU.pow).then_inc(o_pow, 1)

            @block.scalar
            def _(act):
                def probs(b):
                    lo = 0 if b else P
                    act.wait_ge(negm, b + 1)
                    for h in range(NH):
                        nc.scalar.activation(sc[:, h, lo:], sc[:, h, lo:], ACT.Exp, bias=nm[:, b, h:h + 1],
                                             accum_out=den[:, b, h:h + 1]).then_inc(prob, 1)
                    nc.scalar.activation(sm[:, b, :], sm[:, b, :], ACT.Exp).then_inc(den_in, 1)

                def pT_copies(b):
                    for i in range(4):
                        act.wait_ge(p_done, 4 * b + i + 1)
                        if i == 0 and b:
                            act.wait_ge(pv_done, b)
                        out = pT[:, 4 * i:4 * i + 4, :].rearrange("p (e f) q -> p e f q", e=2)
                        src = bA[i][:].rearrange("p (e f q) -> p e f q", e=2, f=2)
                        lo = 0 if b else 1
                        nc.scalar.activation(out[:, :, lo:], src[:, :, lo:], ACT.Copy).then_inc(p_out, 1)

                def att_square(b):
                    act.wait_ge(att_o, b + 1)
                    nc.scalar.activation(aj[:], ao[:], ACT.Square, accum_out=ass[:, b:b + 1]).then_inc(att_ss, 1)

                nc.scalar.activation(m.z[:], m.z[:], ACT.Silu).then_inc(o_mix, 1)
                for c in range(NC):
                    b, q = c // 2, c % 2
                    r = slice(q * CH, (q + 1) * CH)
                    if q == 0:
                        probs(b)
                        pT_copies(b)
                    act.wait_ge(o_done, c + 1)
                    nc.scalar.activation(ot[r, b, :], bO[r, :], ACT.Copy).then_inc(o_out, 1)
                    if q == 1:
                        att_square(b)
                        act.wait_ge(o_out, c + 1)
                        if b:
                            act.wait_ge(o_ss, b)
                        nc.scalar.activation(osq[:], ot[:, b, :], ACT.Square).then_inc(o_sq, 1)


def output_projection(nc, m, ps, sem, w_out, norm_ffn_g, w_q, keys, h_dram):
    done, plink = sem("out_done"), sem("out_pool")
    w_ld = [sem(f"w_out_in{i}") for i in range(4)]
    h_spilled, k_in, x_hi = sem("h_spilled"), sem("keys_in"), sem("x_hi")
    g_in, squares, scale, normed = sem("ffn_gain_in"), sem("h_squares"), sem("h_scale"), sem("h_normed")
    banks = Banks(ps, done, {"act": sem("out_by_act"), "dve": sem("out_by_dve")})
    for b in range(TB):
        for half in range(2):
            banks.add(("mixT", b, half), "act")
    for b in range(TB):
        for half in range(2):
            banks.add(("h", b, half), "dve")
    for b in range(TB):
        for half in range(2):
            banks.add(("xT", b, half), "act")
    for h in range(PH):
        banks.add(("q", h), "dve" if h % 2 else "act")
    for b in range(TB):
        for hh in range(2):
            for p in range(2):
                banks.add(("s", b, p, hh), "dve" if p else "act")
    with ExitStack() as ctx:
        sb = m.mem.local(ctx)
        gain = sb("ffn_gain", [P, D])
        xn = sb("hn", [P, 2, D])
        junk = sb("h_junk", [P, D])
        mixT = sb("mixT", [P, KD, T])
        wo = m.s[:].rearrange("p b q h n -> p (b q h n)").rearrange("p (i k n) -> p i k n", i=2, k=KD)
        wq = sb("w_q", [P, 2, KD, T])
        w = [wo[:, 0], wo[:, 1], wq[:, 0], wq[:, 1]]
        xn2T = sb("xn2T", [P, KD, T])
        qT = sb("qT", [P, PH, T])
        kt = sb("sub_keys", [P, PH, NK])
        ss = sb("h_ss", [P, TB])
        with nc.Block() as block:
            @block.sync
            def _(sp):
                for i in range(4):
                    v = (w_out if i < 2 else w_q)[0].rearrange("(k p) n -> p k n", p=P)
                    sp.dma_start(w[i], v[:, :, (i % 2) * T:(i % 2 + 1) * T]).then_inc(w_ld[i], 16)
                    if i == 1:
                        sp.dma_start(gain[:], norm_ffn_g[0:1, :].broadcast_to([P, D])).then_inc(g_in, 16)
                sp.dma_start(kt[:], keys.rearrange("p (h n) -> p h n", h=PH)).then_inc(k_in, 16)
                banks.wait_taken(sp, ("h", TB - 1, 1))
                sp.dma_start(h_dram, m.acc[:]).then_inc(h_spilled, 16)
                sp.wait_ge(h_spilled, 16)

            @block.tensor
            def _(pe):
                for b in range(TB):
                    for half in range(2):
                        for k in range(4):
                            kk = 4 * half + k
                            t = nc.tensor.transpose(banks.bank(("mixT", b, half))[:, k * P:(k + 1) * P],
                                                    m.mix[:, b, kk * P:(kk + 1) * P], m.ident[:])
                        t.then_inc(done, 1)
                for b in range(TB):
                    banks.wait_taken(pe, ("mixT", b, 1))
                    for half in range(2):
                        g = ("h", b, half)
                        banks.wait_free(pe, g)
                        pe.wait_ge(w_ld[half], 16)
                        for k in range(KD):
                            t = nc.tensor.matmul(banks.bank(g)[:], mixT[:, k, b * P:(b + 1) * P], w[half][:, k, :],
                                                 start=(k == 0), stop=(k == KD - 1))
                        t.then_inc(done, 1)
                for b in range(TB):
                    pe.wait_ge(normed, b + 1)
                    for half in range(2):
                        banks.wait_free(pe, ("xT", b, half))
                        for k in range(4):
                            kk = 4 * half + k
                            t = nc.tensor.transpose(banks.bank(("xT", b, half))[:, k * P:(k + 1) * P],
                                                    xn[:, b % 2, kk * P:(kk + 1) * P], m.ident[:])
                        t.then_inc(done, 1)
                banks.wait_taken(pe, ("xT", TB - 1, 1))
                for h in range(PH):
                    g = ("q", h)
                    banks.wait_free(pe, g)
                    pe.wait_ge(w_ld[2 + h // 4], 16)
                    for k in range(KD):
                        t = nc.tensor.matmul(banks.bank(g)[:], w[2 + h // 4][:, k, (h % 4) * P:(h % 4 + 1) * P],
                                             xn2T[:, k, :], start=(k == 0), stop=(k == KD - 1))
                    t.then_inc(done, 1)
                banks.wait_taken(pe, ("q", PH - 2))
                banks.wait_taken(pe, ("q", PH - 1))
                pe.wait_ge(k_in, 16)
                for b in range(TB):
                    for hh in range(2):
                        for p in range(2):
                            g = ("s", b, p, hh)
                            banks.wait_free(pe, g)
                            for h in range(4):
                                v = slice(p * HALF, (p + 1) * HALF)
                                t = nc.tensor.matmul(banks.bank(g)[:, h * NK:(h + 1) * NK],
                                                     qT[v, 4 * hh + h, b * P:(b + 1) * P],
                                                     kt[v, 4 * hh + h, :], start=True, stop=True)
                            t.then_inc(done, 1)

            @block.scalar
            def _(act):
                for b in range(TB):
                    for half in range(2):
                        g = ("mixT", b, half)
                        banks.wait_full(act, g)
                        nc.scalar.activation(mixT[:, 4 * half:4 * half + 4, b * P:(b + 1) * P],
                                             banks.bank(g)[:].rearrange("p (k t) -> p k t", k=4),
                                             ACT.Copy).then_inc(banks.taken["act"], 1)
                for b in range(TB):
                    banks.wait_taken(act, ("h", b, 1))
                    if b:
                        act.wait_ge(squares, b)
                    nc.scalar.activation(junk[:], m.acc[:, b, :], ACT.Square,
                                         accum_out=ss[:, b:b + 1]).then_inc(squares, 1)
                for b in range(TB):
                    for half in range(2):
                        g = ("xT", b, half)
                        banks.wait_full(act, g)
                        nc.scalar.activation(xn2T[:, 4 * half:4 * half + 4, b * P:(b + 1) * P],
                                             banks.bank(g)[:].rearrange("p (k t) -> p k t", k=4),
                                             ACT.Copy).then_inc(banks.taken["act"], 1)
                for k in range(KD):
                    if k == 0:
                        banks.wait_taken(act, ("xT", TB - 1, 1))
                    nc.scalar.activation(m.xh[:, k, :], xn2T[:, k, :], ACT.Copy).then_inc(x_hi, 1)
                for h in range(0, PH, 2):
                    banks.wait_full(act, ("q", h))
                    nc.scalar.activation(qT[:, h, :], banks.bank(("q", h))[:],
                                         ACT.Copy).then_inc(banks.taken["act"], 1)
                for b in range(TB):
                    for hh in range(2):
                        g = ("s", b, 0, hh)
                        banks.wait_full(act, g)
                        nc.scalar.activation(m.s[:, b, 0, 4 * hh:4 * hh + 4, :],
                                             banks.bank(g)[:].rearrange("p (h n) -> p h n", h=4),
                                             ACT.Copy).then_inc(banks.taken["act"], 1)

            @block.gpsimd
            def _(pool):
                link = chain(pool, plink, [0])
                for b in range(TB):
                    pool.wait_ge(squares, b + 1)
                    link(nc.gpsimd.tensor_scalar(ss[:, b:b + 1], ss[:, b:b + 1], 1.0 / D, EPS, ALU.mult, ALU.add))
                    nc.gpsimd.tensor_tensor(ss[:, b:b + 1], ss[:, b:b + 1], m.neg_half[:, 0:1],
                                            ALU.pow).then_inc(scale, 1)

            @block.vector
            def _(dve):
                for b in range(TB):
                    for half in range(2):
                        g = ("h", b, half)
                        banks.wait_full(dve, g)
                        v = m.acc[:, b, half * T:(half + 1) * T]
                        nc.vector.tensor_tensor(v, v, banks.bank(g)[:], ALU.add).then_inc(banks.taken["dve"], 1)
                dve.wait_ge(g_in, 16)
                for b in range(TB):
                    dve.wait_ge(scale, b + 1)
                    if b >= 2:
                        banks.wait_full(dve, ("xT", b - 2, 1))
                    nc.vector.scalar_tensor_tensor(xn[:, b % 2, :], m.acc[:, b, :], ss[:, b:b + 1], gain[:],
                                                   ALU.mult, ALU.mult).then_inc(normed, 1)
                for k in range(KD):
                    dve.wait_ge(x_hi, k + 1)
                    nc.vector.tensor_tensor(m.xl[:, k, :], xn2T[:, k, :], m.xh[:, k, :].bitcast(F32), ALU.subtract)
                for h in range(1, PH, 2):
                    banks.wait_full(dve, ("q", h))
                    nc.vector.tensor_copy(qT[:, h, :], banks.bank(("q", h))[:]).then_inc(banks.taken["dve"], 1)
                for b in range(TB):
                    for hh in range(2):
                        g = ("s", b, 1, hh)
                        banks.wait_full(dve, g)
                        nc.vector.tensor_copy(m.s[:, b, 1, 4 * hh:4 * hh + 4, :],
                                              banks.bank(g)[:].rearrange("p (h n) -> p h n", h=4)
                                              ).then_inc(banks.taken["dve"], 1)


def routing(nc, m, ps, sem, u_t, gates, gelus):
    done, vlink = sem("rt_done"), sem("rt_dve")
    subbed, exped, r1_row, masked, r2_ready, r1_ready, iota_made = (sem(n) for n in (
        "rt_subtracted", "rt_exps", "rt_r1_rows", "rt_masked", "rt_r2", "rt_r1", "rt_iota"))
    r1_pool = sem("rt_r1_pool")
    u_in = [sem("early_u_in0"), sem("early_u_in1")]
    u_hi, u_lo = sem("early_u_hi"), sem("early_u_lo")
    ge_out = sem("early_gelu_out")
    stored = [sem("gates_out0"), sem("gates_out1")]
    banks = Banks(ps, done, {"act": sem("rt_by_act"), "dve": sem("rt_by_dve")})
    JS = 16
    NS = NK // JS
    RING = 12
    ST = 16
    FIRST = 7
    AFTER = [(0, 2, 3, 5), (-1, 1, 2, 4, 5), (-1, 1, 3, 5), (-1, 1, 3, 5)]
    assert FIRST + sum(len(v) for v in AFTER) == EARLY

    def early(b, e):
        if b < 0:
            return range(FIRST)
        n = FIRST + sum(len(v) for v in AFTER[:b]) + sum(i < e for i in AFTER[b])
        return range(n, n + (e in AFTER[b]))

    for n in early(-1, 0):
        banks.add(("up", n), "act")
    for b in range(TB):
        for n in early(b, -1):
            banks.add(("up", n), "act")
        banks.add(("small", b), "dve")
        for e in range(NS):
            for k in range(JS // 4):
                banks.add(("r2T", b, e, k), "act")
            for n in early(b, e):
                banks.add(("up", n), "act")
        for k in range(P // 4):
            banks.add(("G", b, k), "act")

    with ExitStack() as ctx:
        sb = m.mem.local(ctx)
        r2T = sb("r2T", [P, P, NK])
        stage = sb("gate_stage", [P, 2, NK // GJ, ST, GJ])
        r2 = sb("r2", [P, 2, HA, JS])
        e2 = sb("e2", [P, 2, PH, NK])
        cand = sb("sums", [P, PH, NPAIR])
        top = sb("top", [P, 2, PH, TOPK])
        best = sb("best", [P, PH, TOPK])
        theta = sb("theta", [P, 2, PH, TOPK])
        small = sb("rt_small", [P, 2, HA])
        key_row = small[:, 0, :].rearrange("p (h a) -> p h a", h=PH)
        idx = key_row.bitcast(U32)
        e1 = small[:, 1, :].rearrange("p (h a) -> p h a", h=PH)
        smallT = sb("rt_smallT", [P, 2, P])
        zsum = sb("rt_z", [P, PH])
        iota = sb("rt_iota_row", [P, NK])
        r1 = sb("r1", [P, RING, NK])
        u_raw = sb("early_u", [P, 2, D])
        uh = sb("early_u_h", [P, 2, D], F32R)
        ul = sb("early_u_l", [P, 2, D], F32R)
        ge = sb("early_gelu", [P, T])

        def rows(buf, off, r, w):
            return buf[:, :, off:off + r * w].rearrange("p h (r w) -> p h r w", w=w)

        def first(a, r, w):
            return top[:, 0, :, a:a + r].unsqueeze(3).broadcast_to([P, PH, r, w])

        def second(r, w):
            return top[:, 1, :, 0:w].unsqueeze(2).broadcast_to([P, PH, r, w])

        def bc(ap, n):
            return ap.broadcast_to([P, PH, n])

        def u_low(on, n):
            return on.tensor_tensor(ul[:, n % 2, :], u_raw[:, n % 2, :], uh[:, n % 2, :].bitcast(F32), ALU.subtract)

        def wait_ring(eng, b, k):
            n = 32 * b + k - RING // 4
            if n >= 0:
                banks.wait_full(eng, ("G", n // 32, n % 32))

        def one_hot(on, b, t):
            return on.tensor_scalar(r1[:, (P * b + t) % RING, :], iota[:], smallT[:, 0, t:t + 1],
                                    smallT[:, 1, t:t + 1], ALU.is_equal, ALU.mult)

        with nc.Block() as block:
            @block.sync
            def _(sp):
                def load_u(n):
                    if n >= 2:
                        sp.wait_ge(u_lo, n - 1)
                    sp.dma_start(u_raw[:, n % 2, :], u_t[NK - EARLY + n]).then_inc(u_in[n % 2], 16)

                for n in range(min(FIRST + 2, EARLY)):
                    load_u(n)
                for b in range(TB):
                    for e in range(-1, NS):
                        for n in early(b, e):
                            if n + 2 < EARLY:
                                load_u(n + 2)
                    for k in range(P // ST):
                        banks.wait_taken(sp, ("G", b, (k + 1) * ST // 4 - 1))
                        t0 = b * P + k * ST
                        sp.dma_start(gates[:, :, t0:t0 + ST, :].rearrange("g i t j -> i g (t j)"),
                                     stage[:, k % 2].rearrange("p g t j -> p g (t j)")).then_inc(stored[k % 2], 16)
                for half in range(2):
                    sp.wait_ge(stored[half], 16 * (T // ST // 2))
                sp.wait_ge(ge_out, 16 * EARLY)

            @block.gpsimd
            def _(pool):
                nc.gpsimd.iota(iota[:], pattern=[[1, NK]], base=0, channel_multiplier=0,
                               allow_small_or_imprecise_dtypes=True).then_inc(iota_made, 1)
                for n in early(-1, 0):
                    pool.wait_ge(u_hi, n + 1)
                    u_low(nc.gpsimd, n).then_inc(u_lo, 1)
                for b in range(TB):
                    for e in range(NS):
                        pool.wait_ge(masked, NS * b + e + 1)
                        v = r2[:, e % 2].rearrange("p (h a) j -> p h a j", h=PH)
                        nc.gpsimd.tensor_tensor(v, v, e2[:, b % 2, :, e * JS:(e + 1) * JS].unsqueeze(2)
                                                .broadcast_to([P, PH, TOPK, JS]), ALU.mult).then_inc(r2_ready, 1)
                    banks.wait_taken(pool, ("small", b))
                    for k in range(1, P // 4, 2):
                        wait_ring(pool, b, k)
                        one_hot(nc.gpsimd, b, 4 * k + 3).then_inc(r1_pool, 1)

            @block.tensor
            def _(pe):
                def up(n):
                    g = ("up", n)
                    banks.wait_free(pe, g)
                    pe.wait_ge(u_lo, n + 1)
                    q = n % 2
                    for k in range(KD):
                        w = slice(k * P, (k + 1) * P)
                        nc.tensor.matmul(banks.bank(g)[:], uh[:, q, w], m.xh[:, k, :], start=(k == 0), stop=False)
                        nc.tensor.matmul(banks.bank(g)[:], uh[:, q, w], m.xl[:, k, :], start=False, stop=False)
                        t = nc.tensor.matmul(banks.bank(g)[:], ul[:, q, w], m.xh[:, k, :], start=False,
                                             stop=(k == KD - 1))
                    t.then_inc(done, 1)

                for n in early(-1, 0):
                    up(n)
                for b in range(TB):
                    for n in early(b, -1):
                        up(n)
                    banks.wait_free(pe, ("small", b))
                    pe.wait_ge(r1_row, b + 1)
                    for i in range(2):
                        t = nc.tensor.transpose(banks.bank(("small", b))[:, i * P:(i + 1) * P], small[:, i, :],
                                                m.ident[:])
                    t.then_inc(done, 1)
                    for e in range(NS):
                        pe.wait_ge(r2_ready, NS * b + e + 1)
                        for k in range(JS // 4):
                            g = ("r2T", b, e, k)
                            banks.wait_free(pe, g)
                            for i in range(4):
                                t = nc.tensor.transpose(banks.bank(g)[:, i * P:(i + 1) * P],
                                                        r2[:, e % 2, :, 4 * k + i], m.ident[:])
                            t.then_inc(done, 1)
                        for n in early(b, e):
                            up(n)
                    banks.wait_taken(pe, ("r2T", b, NS - 1, JS // 4 - 1))
                    for k in range(P // 4):
                        g = ("G", b, k)
                        banks.wait_free(pe, g)
                        pe.wait_ge(r1_ready, 32 * b + k + 1)
                        if k % 2:
                            pe.wait_ge(r1_pool, 16 * b + k // 2 + 1)
                        for i in range(4):
                            t = nc.tensor.matmul(banks.bank(g)[:, i * NK:(i + 1) * NK],
                                                 r1[:, (P * b + 4 * k + i) % RING, :], r2T[:, 4 * k + i, :],
                                                 start=True, stop=True)
                        t.then_inc(done, 1)

            @block.scalar
            def _(act):
                def split_u(n):
                    act.wait_ge(u_in[n % 2], 16 * (n // 2 + 1))
                    if n >= 2:
                        banks.wait_full(act, ("up", n - 2))
                    nc.scalar.activation(uh[:, n % 2, :], u_raw[:, n % 2, :], ACT.Copy).then_inc(u_hi, 1)

                def gelu(n):
                    banks.wait_full(act, ("up", n))
                    if n:
                        act.wait_ge(ge_out, 16 * n)
                    nc.scalar.activation(ge[:], banks.bank(("up", n))[:],
                                         ACT.Gelu).then_inc(banks.taken["act"], 1)
                    if n + 2 < EARLY:
                        split_u(n + 2)
                    banks.wait_taken(act, ("up", n))
                    act.dma_start(gelus[n], ge[:]).then_inc(ge_out, 16)

                def exps(b):
                    act.wait_ge(subbed, b + 1)
                    nc.scalar.activation(best[:], best[:], ACT.Exp)
                    nc.scalar.activation(e1, e1, ACT.Exp)
                    nc.scalar.activation(e2[:, b % 2], e2[:, b % 2], ACT.Exp).then_inc(exped, 1)

                split_u(0)
                split_u(1)
                for n in early(-1, 0):
                    gelu(n)
                    if n == 3:
                        exps(0)
                for b in range(TB):
                    for n in early(b, -1):
                        gelu(n)
                    for e in range(NS):
                        for k in range(JS // 4):
                            g = ("r2T", b, e, k)
                            banks.wait_full(act, g)
                            if b and e == 0 and k == 0:
                                banks.wait_full(act, ("G", b - 1, P // 4 - 1))
                            j0 = e * JS + 4 * k
                            nc.scalar.activation(r2T[:, :, j0:j0 + 4].rearrange("p t j -> p j t"),
                                                 banks.bank(g)[:].rearrange("p (j t) -> p j t", j=4),
                                                 ACT.Copy).then_inc(banks.taken["act"], 1)
                        for n in early(b, e):
                            gelu(n)
                    if b + 1 < TB:
                        exps(b + 1)
                    for k in range(P // 4):
                        g = ("G", b, k)
                        banks.wait_full(act, g)
                        slot, q = (4 * k // ST) % 2, b * (P // ST) + 4 * k // ST
                        if q >= 2 and 4 * k % ST == 0:
                            act.wait_ge(stored[slot], 16 * (q // 2))
                        t0 = 4 * k % ST
                        nc.scalar.activation(stage[:, slot, :, t0:t0 + 4, :].rearrange("p g t j -> p t g j"),
                                             banks.bank(g)[:].rearrange("p (t g j) -> p t g j", t=4, j=GJ),
                                             ACT.Copy).then_inc(banks.taken["act"], 1)

            @block.vector
            def _(dve):
                link = chain(dve, vlink, [0])

                def prepare(b, part):
                    s1, s2, left = m.s[:, b, 0], m.s[:, b, 1], e2[:, b % 2]
                    th = theta[:, b % 2]
                    if part == 0:
                        for h in range(PH):
                            nc.vector.max(top[:, 0, h, 0:8], s1[:, h, :])
                        for h in range(PH):
                            t = nc.vector.max(top[:, 1, h, 0:8], s2[:, h, :])
                        link(t)
                    elif part == 1:
                        if b >= 2:
                            dve.wait_ge(r2_ready, NS * (b - 1))
                        for h in range(PH):
                            t = nc.vector.max_index(idx[:, h, 0:8], top[:, 0, h, 0:8], s1[:, h, :])
                        link(t)
                        for h in range(PH):
                            nc.vector.match_replace(out=s1[:, h, :], in_to_replace=top[:, 0, h, 0:8],
                                                    in_values=s1[:, h, :], imm_value=-BIG)
                        for h in range(PH):
                            t = nc.vector.match_replace(out=left[:, h, :], in_to_replace=top[:, 1, h, 0:8],
                                                        in_values=s2[:, h, :], imm_value=-BIG)
                        link(t)
                    elif part == 2:
                        for h in range(PH):
                            nc.vector.max(top[:, 0, h, 8:16], s1[:, h, :])
                        for h in range(PH):
                            t = nc.vector.max(top[:, 1, h, 8:16], left[:, h, :])
                        link(t)
                        for h in range(PH):
                            nc.vector.max_index(idx[:, h, 8:16], top[:, 0, h, 8:16], s1[:, h, :])
                    elif part == 3:
                        off = 0
                        for a, r, w in PAIRS:
                            t = nc.vector.tensor_tensor(rows(cand, off, r, w), first(a, r, w), second(r, w), ALU.add)
                            off += r * w
                        link(t)
                        for h in range(PH):
                            t = nc.vector.max(best[:, h, 0:8], cand[:, h, :])
                        link(t)
                        for h in range(PH):
                            t = nc.vector.match_replace(out=cand[:, h, :], in_to_replace=best[:, h, 0:8],
                                                        in_values=cand[:, h, :], imm_value=-BIG)
                        link(t)
                    elif part == 4:
                        for h in range(PH):
                            t = nc.vector.max(best[:, h, 8:16], cand[:, h, :])
                        link(t)
                        for h in range(PH):
                            t = nc.vector.match_replace(out=cand[:, h, :], in_to_replace=best[:, h, 8:16],
                                                        in_values=cand[:, h, :], imm_value=-BIG)
                        link(t)
                    elif part == 5:
                        link(nc.vector.tensor_scalar(cand[:], cand[:], -BIG, BIG, ALU.is_gt, ALU.mult))
                        off = 0
                        for a, r, w in PAIRS:
                            v = rows(cand, off, r, w)
                            t = nc.vector.tensor_tensor(v, v, second(r, w), ALU.add)
                            off += r * w
                        link(t)
                        off = 0
                        for a, r, w in PAIRS:
                            nc.vector.tensor_reduce(th[:, :, a:a + r], rows(cand, off, r, w), AX, ALU.min)
                            off += r * w
                    elif part == 6:
                        nc.vector.tensor_tensor(e1, top[:, 0], bc(top[:, 0, :, 0:1], TOPK), ALU.subtract)
                        nc.vector.tensor_tensor(left, s2, bc(top[:, 1, :, 0:1], NK), ALU.subtract)
                        link(nc.vector.tensor_copy(zsum[:].unsqueeze(2), best[:, :, 0:1]))
                        nc.vector.tensor_copy(key_row, idx)
                        nc.vector.tensor_tensor(best[:], best[:], bc(zsum[:].unsqueeze(2), TOPK),
                                                ALU.subtract).then_inc(subbed, 1)
                    else:
                        dve.wait_ge(exped, b + 1)
                        link(nc.vector.tensor_reduce(zsum[:], best[:], AX, ALU.add))
                        link(nc.vector.reciprocal(zsum[:], zsum[:]))
                        nc.vector.tensor_tensor(e1, e1, bc(zsum[:].unsqueeze(2), TOPK), ALU.mult).then_inc(r1_row, 1)

                def mask(b, e):
                    if NS * b + e >= 2:
                        pb, pe_ = divmod(NS * b + e - 2, NS)
                        banks.wait_full(dve, ("r2T", pb, pe_, JS // 4 - 1))
                    nc.vector.tensor_tensor(r2[:, e % 2].rearrange("p (h a) j -> p h a j", h=PH),
                                            m.s[:, b, 1, :, e * JS:(e + 1) * JS].unsqueeze(2)
                                            .broadcast_to([P, PH, TOPK, JS]),
                                            theta[:, b % 2].unsqueeze(3).broadcast_to([P, PH, TOPK, JS]),
                                            ALU.is_ge).then_inc(masked, 1)

                def split_u(b, e):
                    for n in early(b, e):
                        dve.wait_ge(u_hi, n + 1)
                        u_low(nc.vector, n).then_inc(u_lo, 1)

                for part in range(8):
                    prepare(0, part)
                dve.wait_ge(iota_made, 1)
                mask(0, 0)
                mask(0, 1)
                dve.wait_ge(u_lo, FIRST)
                for b in range(TB):
                    for e in range(-1, 2):
                        split_u(b, e)
                    for e in range(2, NS):
                        if b + 1 < TB and e < 6:
                            prepare(b + 1, e - 2)
                        mask(b, e)
                        split_u(b, e)
                        if e == 2:
                            banks.wait_full(dve, ("small", b))
                            if b:
                                dve.wait_ge(r1_pool, 16 * b)
                            nc.vector.tensor_copy(smallT[:].rearrange("p i t -> p (i t)"),
                                                  banks.bank(("small", b))[:, 0:2 * P]).then_inc(banks.taken["dve"], 1)
                    banks.wait_taken(dve, ("small", b))
                    if b + 1 < TB:
                        for part in range(4, 7):
                            prepare(b + 1, part)
                    for k in range(P // 4):
                        if b + 1 < TB and k in (RING // 4, 3 * RING // 4):
                            if k == RING // 4:
                                prepare(b + 1, 7)
                            mask(b + 1, 0 if k == RING // 4 else 1)
                        wait_ring(dve, b, k)
                        for i in range(3 if k % 2 else 4):
                            ins = one_hot(nc.vector, b, 4 * k + i)
                        ins.then_inc(r1_ready, 1)


def experts(nc, m, ps, sem, u_t, v, gates, gelus, h_dram, out):
    NU, NV, NGE = 4, 2, 2
    BODY = 2 * GT
    NM = (NK - EARLY) // BODY
    NT = NK // BODY
    acc_in = sem("acc_in")
    u_in = [sem(f"u_in{i}") for i in range(NU)]
    v_in = [sem(f"v_in{i}") for i in range(NV)]
    g_in = sem("gates_in")
    ge_in = [sem(f"gelu_in{i}") for i in range(NGE)]
    u_hi_ready, u_ready, v_hi_ready, v_ready = (sem(n) for n in ("u_hi_ready", "u_ready", "v_hi_ready", "v_ready"))
    up_done, gelu_done, gated, gate_f, gate_hi = (sem(n) for n in ("up_done", "gelu_done", "gated", "gate_f", "gate_hi"))
    down_done, added, out_done = sem("down_done"), sem("added"), sem("out_stored")
    bank_up = ps[0:2]
    bank_down = ps[2:6]
    v_rows = v[0].rearrange("(i j) d -> j i d", j=NK)

    f = lambda ap: ap.bitcast(F32)
    with ExitStack() as ctx:
        sb = m.mem.local(ctx)
        acc = sb("acc_out", [P, TB, D])
        u_raw = sb("u_raw", [P, NU, D])
        v_raw = sb("v_raw", [P, NV, D])
        uh = sb("u_hi", [P, 2, D], F32R)
        ul = sb("u_lo", [P, 2, D], F32R)
        vh = sb("v_hi", [P, BODY, D], F32R)
        vl = sb("v_lo", [P, BODY, D], F32R)
        gt = sb("gate_tiles", [P, T, GJ])
        ge = sb("gelu_tile", [P, 2, T])
        af = sb("act_tile", [P, T])
        ah = sb("act_hi", [P, BODY, T], F32R)
        al = sb("act_lo", [P, BODY, T], F32R)
        with nc.Block() as block:
            @block.sync
            def _(sp):
                def load_u(n, slot):
                    sp.dma_start(u_raw[:, slot, :], u_t[bass.ds(n, 1)].rearrange("o p d -> p (o d)")
                                 ).then_inc(u_in[slot], 16)

                def load_v(n, slot):
                    sp.dma_start(v_raw[:, slot, :], v_rows[bass.ds(n, 1)].rearrange("o p d -> p (o d)")
                                 ).then_inc(v_in[slot], 16)

                def load_gates(it):
                    sp.dma_start(gt[:], gates[bass.ds(it, 1)].rearrange("o i t j -> i (o t) j")
                                 ).then_inc(g_in, 16)

                def body(it, u_left=BODY, last=False):
                    for half in range(2):
                        for q in range(GT):
                            jj = half * GT + q
                            n = it * BODY + jj
                            if jj < u_left:
                                sp.wait_ge(u_ready, n + 1)
                                load_u(n + NU, jj % NU)
                        if half and not last:
                            sp.wait_ge(gated, (it + 1) * BODY)
                            load_gates(it + 1)
                        for q in range(GT):
                            jj = half * GT + q
                            if not (last and jj + NV >= BODY):
                                sp.wait_ge(v_ready, it * BODY + jj + 1)
                                load_v(it * BODY + jj + NV, jj % NV)

                def late(it):
                    last = it == NT - 1
                    for half in range(2):
                        for q in range(GT):
                            jj = half * GT + q
                            n = it * BODY + jj
                            sp.wait_ge(gated, n - NGE + 1)
                            sp.dma_start(ge[:, jj % NGE, :], gelus[n - NM * BODY]).then_inc(ge_in[jj % NGE], 16)
                        if half and not last:
                            sp.wait_ge(gated, (it + 1) * BODY)
                            load_gates(it + 1)
                        for q in range(GT):
                            jj = half * GT + q
                            if not (last and jj + NV >= BODY):
                                sp.wait_ge(v_ready, it * BODY + jj + 1)
                                load_v(it * BODY + jj + NV, jj % NV)

                for n in range(NU):
                    load_u(n, n)
                    if n == 1:
                        load_gates(0)
                for n in range(NV):
                    load_v(n, n)
                sp.dma_start(acc[:], h_dram).then_inc(acc_in, 16)
                with sp.Fori(0, NM - 1) as it:
                    body(it)
                body(NM - 1, u_left=BODY - NU)
                for it in range(NM, NT):
                    late(it)
                sp.wait_ge(added, 8 * NG)
                sp.dma_start(out[0].rearrange("(b p) d -> p b d", p=P), acc[:]).then_inc(out_done, 16)
                sp.wait_ge(out_done, 16)

            @block.tensor
            def _(pe):
                def up(it, jj):
                    n = it * BODY + jj
                    pe.wait_ge(u_ready, n + 1)
                    if not (isinstance(it, int) and it == 0 and jj < 2):
                        pe.wait_ge(gelu_done, n - 1)
                    q, bank = jj % 2, bank_up[jj % 2]
                    for k in range(KD):
                        w = slice(k * P, (k + 1) * P)
                        nc.tensor.matmul(bank[:], uh[:, q, w], m.xh[:, k, :], start=(k == 0), stop=False)
                        nc.tensor.matmul(bank[:], uh[:, q, w], m.xl[:, k, :], start=False, stop=False)
                        t = nc.tensor.matmul(bank[:], ul[:, q, w], m.xh[:, k, :], start=False, stop=(k == KD - 1))
                    t.then_inc(up_done, 1)

                def down(g, half, first):
                    pe.wait_ge(gated, GT * (g + 1))
                    pe.wait_ge(v_ready, GT * (g + 1))
                    for o in range(8):
                        b, dh = o // 2, o % 2
                        if not (first and o < 4):
                            pe.wait_ge(added, 8 * g + o - 3)
                        bank = bank_down[o % 4]
                        for e in range(GT):
                            s = half * GT + e
                            w, c = slice(b * P, (b + 1) * P), slice(dh * T, (dh + 1) * T)
                            nc.tensor.matmul(bank[:], ah[:, s, w], vh[:, s, c], start=(e == 0), stop=False)
                            nc.tensor.matmul(bank[:], ah[:, s, w], vl[:, s, c], start=False, stop=False)
                            t = nc.tensor.matmul(bank[:], al[:, s, w], vh[:, s, c], start=False, stop=(e == GT - 1))
                        t.then_inc(down_done, 1)

                def body(it):
                    for half in range(2):
                        for q in range(GT):
                            up(it, half * GT + q)
                        if half or not isinstance(it, int):
                            down(it * 2 + half - 1, 1 - half, isinstance(it, int))
                body(0)
                with pe.Fori(1, NM) as it:
                    body(it)
                for g in range(2 * NM - 1, NG):
                    down(g, g % 2, False)

            @block.scalar
            def _(act):
                def split_u(it, jj):
                    n = it * BODY + jj
                    act.wait_ge(u_in[jj % NU], 16 * (it * (BODY // NU) + jj // NU + 1))
                    if not (isinstance(it, int) and it == 0 and jj < 2):
                        act.wait_ge(up_done, n - 1)
                    nc.scalar.activation(uh[:, jj % 2, :], u_raw[:, jj % NU, :], ACT.Copy).then_inc(u_hi_ready, 1)

                def split_v(it, half):
                    for q in range(GT):
                        jj = half * GT + q
                        act.wait_ge(v_in[jj % NV], 16 * (it * (BODY // NV) + jj // NV + 1))
                        if not (isinstance(it, int) and it == 0) and q == 0:
                            act.wait_ge(down_done, 8 * (it * 2 + half - 1))
                        nc.scalar.activation(vh[:, jj, :], v_raw[:, jj % NV, :], ACT.Copy).then_inc(v_hi_ready, 1)

                def body(it, last=False):
                    for half in range(2):
                        for q in range(GT):
                            jj = half * GT + q
                            n = it * BODY + jj
                            act.wait_ge(up_done, n + 1)
                            if not (isinstance(it, int) and it == 0 and jj < 2):
                                act.wait_ge(gated, n - 1)
                            nc.scalar.activation(ge[:, jj % 2, :], bank_up[jj % 2][:], ACT.Gelu).then_inc(gelu_done, 1)
                            if jj + 2 < BODY:
                                split_u(it, jj + 2)
                            elif not last:
                                split_u(it + 1, jj + 2 - BODY)
                        split_v(it, half)

                split_u(0, 0)
                split_u(0, 1)
                body(0)
                with act.Fori(1, NM - 1) as it:
                    body(it)
                body(NM - 1, last=True)
                for it in range(NM, NT):
                    for half in range(2):
                        split_v(it, half)

            @block.vector
            def _(dve):
                def split_u(it, jj):
                    n = it * BODY + jj
                    dve.wait_ge(u_hi_ready, n + 1)
                    nc.vector.tensor_tensor(ul[:, jj % 2, :], u_raw[:, jj % NU, :], f(uh[:, jj % 2, :]),
                                            ALU.subtract).then_inc(u_ready, 1)

                def add(g, o):
                    dve.wait_ge(down_done, 8 * g + o + 1)
                    v_ = acc[:, o // 2, (o % 2) * T:(o % 2 + 1) * T]
                    nc.vector.tensor_tensor(v_, v_, bank_down[o % 4][:], ALU.add).then_inc(added, 1)

                def gate(it, jj):
                    n = it * BODY + jj
                    if not (isinstance(it, int) and it == 0 and jj == 0):
                        dve.wait_ge(gated, n)
                    nc.vector.tensor_tensor(af[:], ge[:, jj % 2, :], gt[:, :, jj],
                                            ALU.mult).then_inc(gate_f, 1)
                    dve.wait_ge(gate_f, n + 1)
                    nc.vector.tensor_scalar(ah[:, jj, :], af[:], 1.0, None, ALU.mult
                                            ).then_inc(gate_hi, 1)
                    dve.wait_ge(gate_hi, n + 1)
                    nc.vector.tensor_tensor(al[:, jj, :], af[:], f(ah[:, jj, :]),
                                            ALU.subtract).then_inc(gated, 1)

                def body(it, last=False, late=False):
                    zero = isinstance(it, int) and it == 0
                    for half in range(2):
                        for q in range(GT):
                            jj = half * GT + q
                            n = it * BODY + jj
                            if late:
                                dve.wait_ge(ge_in[jj % NGE], 16 * ((n - NM * BODY) // NGE + 1))
                            else:
                                dve.wait_ge(gelu_done, n + 1)
                            if jj == 0:
                                dve.wait_ge(g_in, 16 * (it + 1))
                            if not zero and q == 0:
                                dve.wait_ge(down_done, 8 * (it * 2 + half - 1))
                            gate(it, jj)
                            if late:
                                pass
                            elif jj + 2 < BODY:
                                split_u(it, jj + 2)
                            elif not last:
                                split_u(it + 1, jj + 2 - BODY)
                        if zero and half:
                            dve.wait_ge(acc_in, 16)
                        for q in range(GT):
                            jj = half * GT + q
                            n = it * BODY + jj
                            if half or not zero:
                                add(it * 2 + half - 1, 2 * q)
                                add(it * 2 + half - 1, 2 * q + 1)
                            dve.wait_ge(v_hi_ready, n + 1)
                            nc.vector.tensor_tensor(vl[:, jj, :], v_raw[:, jj % NV, :], f(vh[:, jj, :]),
                                                    ALU.subtract).then_inc(v_ready, 1)
                split_u(0, 0)
                split_u(0, 1)
                body(0)
                with dve.Fori(1, NM - 1) as it:
                    body(it)
                body(NM - 1, last=True)
                for it in range(NM, NT):
                    body(it, late=True)
                for o in range(8):
                    add(NG - 1, o)


def hybrid_layer(nc, a, out):
    gates = nc.dram_tensor("gates", [NK // GJ, NK, T, GJ], F32, kind="Internal").ap()
    gelus = nc.dram_tensor("early_gelus", [EARLY, P, T], F32, kind="Internal").ap()
    h_dram = nc.dram_tensor("h_spill", [P, TB, D], F32, kind="Internal").ap()
    with ExitStack() as ctx:
        sem = lambda name: ctx.enter_context(nc.semaphore(name))
        ps = [ctx.enter_context(nc.psum_tensor(f"bank{i}", [P, 512], F32)) for i in range(8)]
        mem = Memory(nc)
        m = Tensors()
        m.mem = mem
        m.ident = mem.take("ident", [P, P])
        m.neg_half = mem.take("neg_half", [P, 1])
        m.acc = mem.take("acc", [P, TB, D])
        m.upper = mem.take("upper", [P, P])
        m.lower = mem.take("lower", [P, P])
        m.chunk_ones = mem.take("chunk_ones", [P, P])
        m.blockdiag = mem.take("blockdiag", [P, 6, P])
        m.levels = mem.take("levels", [P, 6, P])
        m.att_mask = mem.take("att_mask", [P, 2 * P])
        m.kva = mem.take("kva", [P, TB, 2 * KVW])
        m.z = mem.take("z", [P, TB, DNW])
        m.ab = mem.take("ab", [P, TB, 2 * DN])
        m.qa = mem.take("qa", [P, TB, ATT])
        m.convin = mem.take("convin", [P, CT, T + TAPS - 1])
        m.g = mem.take("g", [P, TB, DN])
        m.beta = mem.take("beta", [P, TB, DN])
        constants(nc, m, sem)
        input_projection(nc, m, ps, sem, a["x"], a["norm_mix_g"], a["w_in"])
        m.tok = mem.take("tok", [P, CT, T])
        m.unitT = mem.take("unitT", [P, 2 * DN, T])
        m.attqT = mem.take("attqT", [P, GRP, T])
        m.attkT = mem.take("attkT", [P, T])
        conv_and_norms(nc, m, ps, sem, a["dn_conv_w"], a["dn_a_log"], a["dn_dt_bias"], a["att_q_norm_g"],
                       a["att_k_norm_g"])
        mem.drop("convin", "qa", "ab")
        m.wT = mem.take("wT", [P, TB, DN, P])
        m.u = mem.take("u", [P, TB, DN, P])
        m.qkT = mem.take("qkT", [P, TB, DN, P])
        m.qdT = mem.take("qdT", [P, TB, DN, P])
        m.kdec = mem.take("kdec", [P, DN, T])
        m.egrow = mem.take("egrow", [P, TB, DN, P])
        delta_prepare(nc, m, ps, sem)
        mem.drop("tok", "unitT", "g", "beta", "upper", "lower", "chunk_ones", "blockdiag", "levels")
        m.mix = mem.take("mix", [P, TB, D])
        mixers(nc, m, ps, sem, a["att_sinks"], a["att_out_norm_g"], a["dn_out_norm_g"])
        mem.drop("kva", "z", "wT", "u", "qkT", "qdT", "kdec", "egrow", "attqT", "attkT", "att_mask")
        m.s = mem.take("scores", [P, TB, 2, PH, NK], at_end=True)
        m.xh = mem.take("x_hi", [P, KD, T], F32R, at_end=True)
        m.xl = mem.take("x_lo", [P, KD, T], F32R, at_end=True)
        output_projection(nc, m, ps, sem, a["w_out"], a["norm_ffn_g"], a["peer_w_q"], a["peer_sub_keys"], h_dram)
        mem.drop("mix", "acc")
        routing(nc, m, ps, sem, a["peer_u"], gates, gelus)
        mem.drop("scores")
        experts(nc, m, ps, sem, a["peer_u"], a["peer_v"], gates, gelus, h_dram, out)


def kernel(**inputs):
    import numpy as np
    import concourse.bacc as bacc
    from concourse.bass_utils import run_bass_kernel_spmd

    a = {name: np.asarray(value) for name, value in inputs.items()}
    a["dn_conv_w"] = a["dn_conv_w"][0].reshape(TAPS, CT, P).transpose(2, 0, 1).reshape(P, TAPS * CT)
    a["peer_sub_keys"] = a["peer_sub_keys"][0].transpose(1, 3, 0, 2).reshape(P, PH * NK)
    a["peer_u"] = a["peer_u"][0].reshape(NK, NK, KD, P).transpose(1, 3, 2, 0).reshape(NK, P, D)
    nc = bacc.Bacc("TRN2", target_bir_lowering=False, num_devices=1)
    arrays, aps = {}, {}
    for name, value in a.items():
        value = np.ascontiguousarray(value)
        arrays["in_" + name] = value
        aps[name] = nc.dram_tensor("in_" + name, value.shape, mybir.dt.from_np(value.dtype),
                                   kind="ExternalInput").ap()
    out = nc.dram_tensor("out_0", (1, T, D), F32, kind="ExternalOutput").ap()
    hybrid_layer(nc, aps, out)
    r = run_bass_kernel_spmd(nc, [arrays], core_ids=[0])
    return r.results[0]["out_0"]
```

```python
from contextlib import ExitStack

import concourse.bass as bass
from concourse import mybir

P = 128
T = 512
TB = T // P
D = 1024
KD = D // P
EPS = 1e-6

HD = 64
NH = 8
NKV = 2
GRP = NH // NKV
ATT = NH * HD
KVW = NKV * HD

DH = 128
DN = 4
DNW = DN * DH
TAPS = 4
CH = 64
CT = 3 * DN

W_TOK = ATT + 2 * KVW
W_CONV0 = W_TOK
W_AB0 = W_CONV0 + 3 * DNW
W_Z0 = W_AB0 + 2 * DN
W_END = W_Z0 + DNW

PH = 8
NK = 128
HALF = 64
TOPK = 16
HA = PH * TOPK
PAIRS = [(0, 1, 16), (1, 1, 8), (2, 1, 5), (3, 1, 4), (4, 1, 3), (5, 3, 2), (8, 8, 1)]
NPAIR = sum(r * w for _, r, w in PAIRS)

GT = 4
NG = NK // GT
EARLY = 32
GJ = 2 * GT
BIG = 3.0e38

F32 = mybir.dt.float32
F32R = mybir.dt.float32r
U32 = mybir.dt.uint32
ALU = mybir.AluOpType
ACT = mybir.ActivationFunctionType
AX = mybir.AxisListType.X


def chain(eng, sem, count):
    def link(ins):
        count[0] += 1
        ins.then_inc(sem, 1)
        eng.wait_ge(sem, count[0])
    return link


class Banks:

    def __init__(self, banks, done, taken):
        self.banks, self.done, self.taken = banks, done, taken
        self.names, self.consumer = [], []

    def add(self, name, consumer):
        self.names.append(name)
        self.consumer.append(consumer)

    def n(self, name):
        return self.names.index(name)

    def bank(self, name):
        return self.banks[self.n(name) % len(self.banks)]

    def rank(self, n):
        return self.consumer[:n + 1].count(self.consumer[n])

    def wait_free(self, pe, name):
        n = self.n(name) - len(self.banks)
        if n >= 0:
            pe.wait_ge(self.taken[self.consumer[n]], self.rank(n))

    def wait_full(self, eng, name):
        eng.wait_ge(self.done, self.n(name) + 1)

    def wait_taken(self, eng, name):
        n = self.n(name)
        eng.wait_ge(self.taken[self.consumer[n]], self.rank(n))


class Tensors:
    pass


class Memory:

    def __init__(self, nc):
        self.nc, self.live = nc, {}

    def take(self, name, shape, dt=F32, at_end=False):
        size = 4
        for n in shape[1:]:
            size *= n
        size = -(-size // 64) * 64
        at = -(-self.nc.sbuf_base // 64) * 64
        gaps = []
        for a, b in sorted(self.live.values()) + [(self.nc.sbuf_usable_end // 64 * 64, 0)]:
            if a - at >= size:
                gaps.append((at, a - size))
            at = max(at, b)
        assert gaps, (name, size, self.live)
        at = gaps[-1][1] if at_end else gaps[0][0]
        self.live[name] = (at, at + size)
        return self.nc.alloc_sbuf_tensor_at(name, shape, dt, offset=at)

    def over(self, name, shape, under):
        return self.nc.alloc_sbuf_tensor_at(name, shape, F32, offset=self.live[under][0])

    def drop(self, *names):
        for name in names:
            del self.live[name]

    def local(self, ctx):
        def sb(name, shape, dt=F32):
            t = self.take(name, shape, dt)
            ctx.callback(self.drop, name)
            return t
        return sb


def build_masks(nc, m, pool, made):
    link = chain(pool, made, [0])
    link(nc.gpsimd.memset(m.ident[:], 0.0))
    link(nc.gpsimd.affine_select(out=m.ident[:], in_=m.ident[:], compare_op=ALU.not_equal, fill=1.0,
                                 base=0, pattern=[[-1, P]], channel_multiplier=1))
    nc.gpsimd.memset(m.neg_half[:], -0.5)
    nc.gpsimd.memset(m.upper[:], 0.0)
    nc.gpsimd.memset(m.lower[:], 0.0)
    nc.gpsimd.memset(m.chunk_ones[:], 0.0)
    nc.gpsimd.memset(m.att_mask[:], 0.0)
    return link


def fill_masks(nc, m, link):
    link(nc.gpsimd.memset(m.blockdiag[:], 1.0))
    for q in range(P // CH):
        a = slice(q * CH, (q + 1) * CH)
        nc.gpsimd.memset(m.upper[a, a], 1.0)
        nc.gpsimd.memset(m.lower[a, a], 1.0)
        link(nc.gpsimd.memset(m.chunk_ones[a, a], 1.0))
    nc.gpsimd.affine_select(out=m.upper[:], in_=m.upper[:], compare_op=ALU.is_ge, fill=0.0,
                            base=0, pattern=[[1, P]], channel_multiplier=-1)
    nc.gpsimd.affine_select(out=m.lower[:], in_=m.lower[:], compare_op=ALU.is_gt, fill=0.0,
                            base=0, pattern=[[-1, P]], channel_multiplier=1)
    nc.gpsimd.affine_select(out=m.att_mask[:, 0:P], in_=m.att_mask[:, 0:P], compare_op=ALU.is_gt,
                            fill=-1e30, base=0, pattern=[[1, P]], channel_multiplier=-1)
    nc.gpsimd.affine_select(out=m.att_mask[:, P:2 * P], in_=m.att_mask[:, P:2 * P],
                            compare_op=ALU.is_ge, fill=-1e30, base=0, pattern=[[-1, P]],
                            channel_multiplier=1)
    for l in range(6):
        s = 1 << l
        v = m.blockdiag[:, l, :].rearrange("p (b r) -> p b r", r=s)
        link(nc.gpsimd.affine_select(out=v, in_=v, compare_op=ALU.is_ge, fill=0.0, base=0,
                                     pattern=[[-s, P // s], [0, s]], channel_multiplier=1))
        link(nc.gpsimd.affine_select(out=v, in_=v, compare_op=ALU.is_ge, fill=0.0, base=s - 1,
                                     pattern=[[s, P // s], [0, s]], channel_multiplier=-1))
    for l in range(6):
        above = m.blockdiag[:, l + 1, :] if l < 5 else m.chunk_ones[:]
        nc.gpsimd.tensor_tensor(m.levels[:, l, :], above, m.blockdiag[:, l, :], ALU.subtract)


def input_projection(nc, m, ps, sem, x, norm_mix_g, w_in, conv_w, a_log, dt_bias, q_norm_g, k_norm_g):
    NCONV = 6
    cols = [(W_CONV0 + 256 * c, 256) for c in range(NCONV)] + [(0, 256), (256, 256), (512, 2 * KVW)]
    zc = (W_END - W_AB0) // 2
    cols += [(W_AB0, zc), (W_AB0 + zc, zc)]
    NC_ = len(cols)
    made, ident_ready = sem("masks_made"), 2
    x_in = [sem(f"x_in{b}") for b in range(TB)]
    g_in = sem("mix_gain_in")
    w_ld = [sem("w_in0"), sem("w_in1")]
    small_in = [sem(f"small_in{i}") for i in range(5)]
    squares, scale, normed, x_hi = sem("x_squares"), sem("x_scale"), sem("x_normed"), sem("x_in_hi")
    w_hi, w_lo, pads = sem("w_in_hi"), sem("w_in_lo"), sem("conv_pads")
    convd, silud, done = sem("conv_done"), sem("silu_done"), sem("proj_done")
    squared, scaled, unit = sem("qk_squared"), sem("qk_scaled"), sem("qk_unit")
    att_sq, att_pow, att_unit = sem("att_squares"), sem("att_pow"), sem("att_unit")
    z1, z2, z3, b2 = sem("gate_z"), sem("gate_softplus"), sem("gate_alog"), sem("gate_beta")
    plink, vlink, alink = sem("proj_pool"), sem("proj_vec"), sem("proj_scal")
    banks = Banks(ps, done, {"act": sem("proj_by_act"), "dve": sem("proj_by_dve")})
    for b in range(TB):
        for half in range(2):
            banks.add(("xT", b, half), "dve")
    for c in range(NC_):
        if c < NCONV:
            for i in range(2):
                banks.add(("conv", c, i), "act")
        else:
            for b in range(TB):
                banks.add(("tokens", c, b), "act")
        if 2 <= c < NCONV + 2:
            for i in range(2):
                banks.add(("tok", 2 * (c - 2) + i), "act")
        if c in (8, 9):
            for i in range(4):
                banks.add(("unitT", 4 * (c - 8) + i), "act")
    for b in range(TB):
        banks.add(("attq", b), "dve")
        banks.add(("attk", b), "dve")

    def last(c):
        return ("conv", c, 1) if c < NCONV else ("tokens", c, TB - 1)

    wview = w_in[0].rearrange("(k p) n -> p k n", p=P)
    with ExitStack() as ctx:
        sb = m.mem.local(ctx)
        xs = m.tok[:].rearrange("p c t -> p (c t)")[:, 0:TB * D].rearrange("p (b d) -> p b d", b=TB)
        gain = sb("mix_gain", [P, D])
        xn = sb("xn", [P, 2, D])
        junk = sb("x_junk", [P, D])
        xh = sb("xn_hi", [P, KD, T], F32R)
        xl = sb("xn_lo", [P, KD, T], F32R)
        wraw = sb("w_raw", [P, 2, KD, zc])
        wh = sb("w_hi", [P, 2, KD, zc], F32R)
        wl = sb("w_lo", [P, 2, KD, zc], F32R)
        ss = sb("x_ss", [P, TB])
        convin = sb("convin", [P, 2, 2, T + TAPS - 1])
        convT = sb("convT", [P, 2, 2, T])
        wconv = sb("wconv", [P, TAPS, CT])
        sq = sb("qk_sq", [P, T])
        ssd = sb("qk_ss", [P, 2 * DN, TB])
        ssa = sb("att_ss", [P, TB, NH + NKV])
        qg = sb("att_qg", [P, HD])
        kg = sb("att_kg", [P, HD])
        alog = sb("alog", [P, DN])
        dtb = sb("dtb", [P, DN])
        zz = sb("gate_zz", [P, TB, DN])
        za = sb("gate_za", [P, TB, DN])
        eb = sb("gate_eb", [P, TB, DN])
        kn = sb("att_kn", [P, TB, KVW])
        qn = xn[:].rearrange("p i d -> p (i d)").rearrange("p (b d) -> p b d", b=TB)

        with nc.Block() as block:
            @block.sync
            def _(sp):
                def load_w(c):
                    if c >= 2:
                        sp.wait_ge(w_lo, c - 1)
                    c0, n = cols[c]
                    sp.dma_start(wraw[:, c % 2, :, 0:n], wview[:, :, c0:c0 + n]).then_inc(w_ld[c % 2], 16)

                xv = x[0].rearrange("(b p) d -> b p d", p=P)
                for b in range(TB):
                    sp.dma_start(xs[:, b, :], xv[b]).then_inc(x_in[b], 16)
                    if b == 0:
                        sp.dma_start(gain[:], norm_mix_g[0:1, :].broadcast_to([P, D])).then_inc(g_in, 16)
                load_w(0)
                load_w(1)
                sp.dma_start(wconv[:].rearrange("p j c -> p (j c)"), conv_w).then_inc(small_in[0], 16)
                sp.dma_start(alog[:], a_log[0:1, :].broadcast_to([P, DN])).then_inc(small_in[1], 16)
                sp.dma_start(dtb[:], dt_bias[0:1, :].broadcast_to([P, DN])).then_inc(small_in[2], 16)
                sp.dma_start(qg[:], q_norm_g[0:1, :].broadcast_to([P, HD])).then_inc(small_in[3], 16)
                sp.dma_start(kg[:], k_norm_g[0:1, :].broadcast_to([P, HD])).then_inc(small_in[4], 16)
                for c in range(2, NC_):
                    load_w(c)

            @block.gpsimd
            def _(pool):
                mask_link = build_masks(nc, m, pool, made)
                nc.gpsimd.memset(convin[:, :, :, 0:TAPS - 1], 0.0).then_inc(pads, 1)
                pool.wait_ge(pads, 1)
                link = chain(pool, plink, [0])
                for b in range(TB):
                    pool.wait_ge(squares, b + 1)
                    link(nc.gpsimd.tensor_scalar(ss[:, b:b + 1], ss[:, b:b + 1], 1.0 / D, EPS, ALU.mult, ALU.add))
                    nc.gpsimd.tensor_tensor(ss[:, b:b + 1], ss[:, b:b + 1], m.neg_half[:, 0:1],
                                            ALU.pow).then_inc(scale, 1)
                fill_masks(nc, m, mask_link)
                pool.wait_ge(squared, 2 * DN)
                link(nc.gpsimd.tensor_scalar(ssd[:], ssd[:], EPS, None, ALU.add))
                link(nc.gpsimd.tensor_tensor(ssd[:], ssd[:], m.neg_half[:, 0:1].unsqueeze(2)
                                             .broadcast_to([P, 2 * DN, TB]), ALU.pow))
                nc.gpsimd.tensor_scalar(ssd[:, 0:DN, :], ssd[:, 0:DN, :], DH ** -0.5, None,
                                        ALU.mult).then_inc(scaled, 1)
                pool.wait_ge(att_sq, TB)
                link(nc.gpsimd.tensor_scalar(ssa[:], ssa[:], 1.0 / HD, EPS, ALU.mult, ALU.add))
                nc.gpsimd.tensor_tensor(ssa[:], ssa[:], m.neg_half[:, 0:1].unsqueeze(2)
                                        .broadcast_to([P, TB, NH + NKV]), ALU.pow).then_inc(att_pow, 1)

            @block.scalar
            def _(act):
                link = chain(act, alink, [0])

                def split_w(c):
                    act.wait_ge(w_ld[c % 2], 16 * (c // 2 + 1))
                    if c >= 2:
                        banks.wait_full(act, last(c - 2))
                    n = cols[c][1]
                    nc.scalar.activation(wh[:, c % 2, :, 0:n], wraw[:, c % 2, :, 0:n], ACT.Copy).then_inc(w_hi, 1)

                for b in range(TB):
                    act.wait_ge(x_in[b], 16)
                    if b:
                        act.wait_ge(squares, b)
                    nc.scalar.activation(junk[:], xs[:, b, :], ACT.Square,
                                         accum_out=ss[:, b:b + 1]).then_inc(squares, 1)
                for b in range(TB):
                    for half in range(2):
                        g = ("xT", b, half)
                        banks.wait_full(act, g)
                        nc.scalar.activation(xh[:, 4 * half:4 * half + 4, b * P:(b + 1) * P],
                                             banks.bank(g)[:].rearrange("p (k t) -> p k t", k=4),
                                             ACT.Copy).then_inc(x_hi, 1)
                split_w(0)
                split_w(1)
                for c in range(NC_):
                    if c < NCONV:
                        for i in range(2):
                            g = ("conv", c, i)
                            banks.wait_full(act, g)
                            if c >= 2:
                                act.wait_ge(convd, c - 1)
                            elif i == 0:
                                act.wait_ge(pads, 1)
                            nc.scalar.activation(convin[:, c % 2, i, TAPS - 1:], banks.bank(g)[:],
                                                 ACT.Copy).then_inc(banks.taken["act"], 1)
                    else:
                        for b in range(TB):
                            g = ("tokens", c, b)
                            banks.wait_full(act, g)
                            bank = banks.bank(g)
                            if c < NCONV + 2:
                                q = (c - NCONV) * 256
                                t = nc.scalar.activation(m.qa[:, b, q:q + 256], bank[:, 0:256], ACT.Copy)
                            elif c == NCONV + 2:
                                t = nc.scalar.activation(m.kva[:, b, :], bank[:, 0:2 * KVW], ACT.Copy)
                            elif c == NCONV + 3:
                                nc.scalar.activation(m.ab[:, b, :], bank[:, 0:2 * DN], ACT.Copy)
                                t = nc.scalar.activation(m.z[:, b, 0:zc - 2 * DN], bank[:, 2 * DN:zc], ACT.Copy)
                            else:
                                t = nc.scalar.activation(m.z[:, b, zc - 2 * DN:], bank[:, 0:zc], ACT.Copy)
                            t.then_inc(banks.taken["act"], 1)
                    if c + 2 < NC_:
                        split_w(c + 2)
                    if 1 <= c < NCONV + 1:
                        act.wait_ge(convd, c)
                        nc.scalar.activation(convT[:, (c - 1) % 2], convT[:, (c - 1) % 2],
                                             ACT.Silu).then_inc(silud, 1)
                    if 2 <= c < NCONV + 2:
                        for i in range(2):
                            tile = 2 * (c - 2) + i
                            bank = banks.bank(("tok", tile))
                            banks.wait_full(act, ("tok", tile))
                            if tile < 2 * DN:
                                if tile:
                                    act.wait_ge(squared, tile)
                                for b in range(TB):
                                    v = slice(b * DH, (b + 1) * DH)
                                    t = nc.scalar.activation(sq[:, v], bank[:, v], ACT.Square,
                                                             accum_out=ssd[:, tile, b:b + 1])
                                t.then_inc(squared, 1)
                            nc.scalar.activation(m.tok[:, tile, :], bank[:], ACT.Copy
                                                 ).then_inc(banks.taken["act"], 1)
                    if c in (8, 9):
                        for i in range(4):
                            g = ("unitT", 4 * (c - 8) + i)
                            banks.wait_full(act, g)
                            nc.scalar.activation(m.unitT[:, g[1], :], banks.bank(g)[:],
                                                 ACT.Copy).then_inc(banks.taken["act"], 1)
                act.wait_ge(small_in[1], 16)
                nc.scalar.activation(alog[:], alog[:], ACT.Exp).then_inc(z3, 1)
                banks.wait_taken(act, ("tokens", 9, TB - 1))
                nc.scalar.activation(eb[:], m.ab[:, :, DN:], ACT.Exp, scale=-1.0).then_inc(b2, 1)
                act.wait_ge(z1, 1)
                link(nc.scalar.activation(za[:], zz[:], ACT.Abs))
                link(nc.scalar.activation(za[:], za[:], ACT.Exp, scale=-1.0))
                nc.scalar.activation(za[:], za[:], ACT.Ln, bias=1.0).then_inc(z2, 1)

            @block.vector
            def _(dve):
                link = chain(dve, vlink, [0])

                def split_w(c):
                    dve.wait_ge(w_hi, c + 1)
                    n = cols[c][1]
                    nc.vector.tensor_tensor(wl[:, c % 2, :, 0:n], wraw[:, c % 2, :, 0:n],
                                            wh[:, c % 2, :, 0:n].bitcast(F32), ALU.subtract).then_inc(w_lo, 1)

                def x_low(b):
                    for half in range(2):
                        g = ("xT", b, half)
                        dve.wait_ge(x_hi, 2 * b + half + 1)
                        v = (slice(None), slice(4 * half, 4 * half + 4), slice(b * P, (b + 1) * P))
                        nc.vector.tensor_tensor(xl[v], banks.bank(g)[:].rearrange("p (k t) -> p k t", k=4),
                                                xh[v].bitcast(F32), ALU.subtract).then_inc(banks.taken["dve"], 1)

                dve.wait_ge(g_in, 16)
                for b in range(TB):
                    dve.wait_ge(scale, b + 1)
                    if b >= 2:
                        banks.wait_full(dve, ("xT", b - 2, 1))
                    nc.vector.scalar_tensor_tensor(xn[:, b % 2, :], xs[:, b, :], ss[:, b:b + 1], gain[:],
                                                   ALU.mult, ALU.mult).then_inc(normed, 1)
                    if b:
                        x_low(b - 1)
                x_low(TB - 1)
                split_w(0)
                split_w(1)
                dve.wait_ge(small_in[0], 16)
                for c in range(NC_):
                    if c < NCONV:
                        banks.wait_taken(dve, ("conv", c, 1))
                        if c >= 2:
                            banks.wait_full(dve, ("tok", 2 * (c - 2) + 1))
                        for j in range(TAPS):
                            for i in range(2):
                                w, out = wconv[:, j, 2 * c + i:2 * c + i + 1], convT[:, c % 2, i, :]
                                if j == 0:
                                    t = nc.vector.tensor_scalar(out, convin[:, c % 2, i, 0:T], w, None, ALU.mult)
                                else:
                                    t = nc.vector.scalar_tensor_tensor(out, convin[:, c % 2, i, j:j + T], w, out,
                                                                       ALU.mult, ALU.add)
                            if j < TAPS - 1:
                                link(t)
                        t.then_inc(convd, 1)
                    if c + 2 < NC_:
                        split_w(c + 2)
                    if c == 6:
                        dve.wait_ge(scaled, 1)
                        banks.wait_taken(dve, ("tok", 2 * DN - 1))
                        for i in range(2 * DN):
                            v = m.tok[:, i, :].rearrange("p (b d) -> p b d", d=DH)
                            nc.vector.tensor_tensor(v, v, ssd[:, i, :].unsqueeze(2).broadcast_to([P, TB, DH]),
                                                    ALU.mult).then_inc(unit, 1)
                    if c == 8:
                        banks.wait_taken(dve, ("tokens", 8, TB - 1))
                        for b in range(TB):
                            if b:
                                dve.wait_ge(att_sq, b)
                            nc.vector.tensor_tensor(junk[:, 0:ATT], m.qa[:, b, :], m.qa[:, b, :], ALU.mult)
                            link(nc.vector.tensor_tensor(junk[:, ATT:ATT + KVW], m.kva[:, b, 0:KVW],
                                                         m.kva[:, b, 0:KVW], ALU.mult))
                            nc.vector.tensor_reduce(ssa[:, b, :], junk[:, 0:ATT + KVW].rearrange(
                                "p (h d) -> p h d", d=HD), AX, ALU.add).then_inc(att_sq, 1)
                    if c == 9:
                        dve.wait_ge(att_pow, 1)
                        dve.wait_ge(small_in[3], 16)
                        dve.wait_ge(small_in[4], 16)
                        for b in range(TB):
                            qv = qn[:, b, :].rearrange("p (g v d) -> p v g d", v=NKV, g=GRP)
                            kv = kn[:, b, :].rearrange("p (h d) -> p h d", d=HD)
                            nc.vector.tensor_tensor(qv, m.qa[:, b, :].rearrange("p (v g d) -> p v g d", v=NKV, g=GRP),
                                                    ssa[:, b, 0:NH].rearrange("p (v g) -> p v g", v=NKV).unsqueeze(3)
                                                    .broadcast_to([P, NKV, GRP, HD]), ALU.mult)
                            link(nc.vector.tensor_tensor(kv, m.kva[:, b, 0:KVW].rearrange("p (h d) -> p h d", d=HD),
                                                         ssa[:, b, NH:].unsqueeze(2).broadcast_to([P, NKV, HD]),
                                                         ALU.mult))
                            qh = qn[:, b, :].rearrange("p (h d) -> p h d", d=HD)
                            nc.vector.tensor_tensor(qh, qh, qg[:].unsqueeze(1).broadcast_to([P, NH, HD]), ALU.mult)
                            nc.vector.tensor_tensor(kv, kv, kg[:].unsqueeze(1).broadcast_to([P, NKV, HD]),
                                                    ALU.mult).then_inc(att_unit, 1)
                dve.wait_ge(small_in[2], 16)
                banks.wait_taken(dve, ("tokens", 9, TB - 1))
                nc.vector.tensor_tensor(zz[:], m.ab[:, :, 0:DN], dtb[:].unsqueeze(1).broadcast_to([P, TB, DN]),
                                        ALU.add).then_inc(z1, 1)
                for b in range(TB):
                    banks.wait_full(dve, ("attq", b))
                    nc.vector.tensor_scalar(m.attqT[:, :, b * P:(b + 1) * P],
                                            banks.bank(("attq", b))[:].rearrange("p (g t) -> p g t", g=GRP),
                                            HD ** -0.5, None, ALU.mult).then_inc(banks.taken["dve"], 1)
                    banks.wait_full(dve, ("attk", b))
                    nc.vector.tensor_copy(m.attkT[:, b * P:(b + 1) * P],
                                          banks.bank(("attk", b))[:, 0:P]).then_inc(banks.taken["dve"], 1)
                dve.wait_ge(z2, 1)
                link(nc.vector.scalar_tensor_tensor(zz[:], zz[:], 0.0, za[:], ALU.max, ALU.add))
                dve.wait_ge(z3, 1)
                nc.vector.scalar_tensor_tensor(m.g[:], zz[:], -1.0,
                                               alog[:].unsqueeze(1).broadcast_to([P, TB, DN]), ALU.mult, ALU.mult)
                dve.wait_ge(b2, 1)
                link(nc.vector.tensor_scalar(eb[:], eb[:], 1.0, None, ALU.add))
                nc.vector.reciprocal(m.beta[:], eb[:])

            @block.tensor
            def _(pe):
                def three_passes(bank, lh, ll, rh, rl):
                    for k in range(KD):
                        nc.tensor.matmul(bank, lh(k), rh(k), start=(k == 0), stop=False)
                        nc.tensor.matmul(bank, lh(k), rl(k), start=False, stop=False)
                        t = nc.tensor.matmul(bank, ll(k), rh(k), start=False, stop=(k == KD - 1))
                    t.then_inc(done, 1)

                pe.wait_ge(made, ident_ready)
                for b in range(TB):
                    pe.wait_ge(normed, b + 1)
                    for half in range(2):
                        g = ("xT", b, half)
                        for k in range(4):
                            kk = 4 * half + k
                            t = nc.tensor.transpose(banks.bank(g)[:, k * P:(k + 1) * P],
                                                    xn[:, b % 2, kk * P:(kk + 1) * P], m.ident[:])
                        t.then_inc(done, 1)
                banks.wait_taken(pe, ("xT", TB - 1, 1))
                for c in range(NC_):
                    pe.wait_ge(w_lo, c + 1)
                    q = c % 2
                    if c < NCONV:
                        for i in range(2):
                            g = ("conv", c, i)
                            banks.wait_free(pe, g)
                            v = slice(i * P, (i + 1) * P)
                            three_passes(banks.bank(g)[:], lambda k: wh[:, q, k, v], lambda k: wl[:, q, k, v],
                                         lambda k: xh[:, k, :], lambda k: xl[:, k, :])
                    else:
                        for b in range(TB):
                            g, n = ("tokens", c, b), cols[c][1]
                            banks.wait_free(pe, g)
                            v = slice(b * P, (b + 1) * P)
                            three_passes(banks.bank(g)[:, 0:n], lambda k: xh[:, k, v], lambda k: xl[:, k, v],
                                         lambda k: wh[:, q, k, 0:n], lambda k: wl[:, q, k, 0:n])
                    if 2 <= c < NCONV + 2:
                        pe.wait_ge(silud, c - 1)
                        for i in range(2):
                            g = ("tok", 2 * (c - 2) + i)
                            banks.wait_free(pe, g)
                            for b in range(TB):
                                t = nc.tensor.transpose(banks.bank(g)[:, b * P:(b + 1) * P],
                                                        convT[:, c % 2, i, b * P:(b + 1) * P], m.ident[:])
                            t.then_inc(done, 1)
                    if c in (8, 9):
                        for i in range(4):
                            g = ("unitT", 4 * (c - 8) + i)
                            pe.wait_ge(unit, g[1] + 1)
                            banks.wait_free(pe, g)
                            for b in range(TB):
                                t = nc.tensor.transpose(banks.bank(g)[:, b * P:(b + 1) * P],
                                                        m.tok[:, g[1], b * P:(b + 1) * P], m.ident[:])
                            t.then_inc(done, 1)
                for b in range(TB):
                    pe.wait_ge(att_unit, b + 1)
                    banks.wait_free(pe, ("attq", b))
                    for g in range(GRP):
                        t = nc.tensor.transpose(banks.bank(("attq", b))[:, g * P:(g + 1) * P],
                                                qn[:, b, g * P:(g + 1) * P], m.ident[:])
                    t.then_inc(done, 1)
                    banks.wait_free(pe, ("attk", b))
                    nc.tensor.transpose(banks.bank(("attk", b))[:, 0:P], kn[:, b, :], m.ident[:]).then_inc(done, 1)


def delta_prepare(nc, m, ps, sem):
    done, vlink, alink = sem("prep_done"), sem("prep_dve"), sem("prep_act")
    diffs, decays, strict = sem("prep_diffs"), sem("prep_decays"), sem("prep_strict")
    cols, col_exp, tok_scaled, level_in = sem("gate_cols"), sem("gate_exps"), sem("tok_scaled"), sem("level_in")
    x0 = sem("solve_start")
    banks = Banks(ps, done, {"act": sem("prep_by_act"), "dve": sem("prep_by_dve")})
    banks.add("gcol", "dve")
    for b in range(TB):
        banks.add(("grow", b), "act")
    for b in range(TB):
        banks.add(("kk", b), "dve")
        banks.add(("qkT", b), "dve")
    for b in range(TB):
        banks.add(("B0T", b), "dve")
    LV = range(1, 6)
    for l in LV:
        for b in range(TB):
            banks.add(("WT", b, l), "act")
        for b in range(TB):
            if l < 5:
                banks.add(("Z", b, l), "dve")
            banks.add(("ZT", b, l), "dve")
    for b in range(TB):
        banks.add(("wT", b), "act")
        banks.add(("u", b), "dve")

    def h4(ap):
        return ap.rearrange("p (h c) -> p h c", h=DN)

    with ExitStack() as ctx:
        sb = m.mem.local(ctx)
        gc = sb("gc_col", [P, 2, TB, DN])
        egc = sb("egc_col", [P, 2, TB, DN])
        bec = sb("bec_col", [P, TB, DN])
        grow = sb("gc_row", [P, TB, DN, P])
        dec = sb("decay", [P, TB, DN, P])
        decT = sb("decayT", [P, TB, DN, P])
        mm = sb("m_low", [P, TB, DN, P])
        lev = sb("m_level", [P, 2, TB, DN, P])
        X, XT, WT = grow, dec, decT
        vb = sb("v_beta", [P, DN, T])
        kbe = sb("k_beta_decay", [P, DN, T])
        bc4 = lambda ap: ap.unsqueeze(2).broadcast_to([P, DN, P])
        with nc.Block() as block:
            @block.tensor
            def _(pe):
                gflat = m.g[:].rearrange("p b h -> p (b h)")
                nc.tensor.matmul(banks.bank("gcol")[:, 0:16], m.upper[:], gflat, start=True, stop=True)
                nc.tensor.matmul(banks.bank("gcol")[:, 16:32], m.chunk_ones[:], gflat,
                                 start=True, stop=True).then_inc(done, 1)
                for b in range(TB):
                    for h in range(DN):
                        t = nc.tensor.matmul(banks.bank(("grow", b))[:, h * P:(h + 1) * P],
                                             m.g[:, b, h:h + 1].broadcast_to([P, P]), m.upper[:],
                                             start=True, stop=True)
                    t.then_inc(done, 1)
                for b in range(TB):
                    for g in ("kk", "qkT"):
                        banks.wait_free(pe, (g, b))
                        for h in range(DN):
                            rhs = m.unitT[:, (DN + h) if g == "kk" else h, b * P:(b + 1) * P]
                            t = nc.tensor.matmul(banks.bank((g, b))[:, h * P:(h + 1) * P],
                                                 m.unitT[:, DN + h, b * P:(b + 1) * P], rhs, start=True, stop=True)
                        t.then_inc(done, 1)
                for b in range(TB):
                    banks.wait_free(pe, ("B0T", b))
                    pe.wait_ge(level_in, b + 1)
                    for h in range(DN):
                        t = nc.tensor.transpose(banks.bank(("B0T", b))[:, h * P:(h + 1) * P],
                                                lev[:, 0, b, h, :], m.ident[:])
                    t.then_inc(done, 1)
                for l in LV:
                    for b in range(TB):
                        banks.wait_free(pe, ("WT", b, l))
                        pe.wait_ge(level_in, TB * l + b + 1)
                        banks.wait_taken(pe, ("ZT", b, l - 1) if l > 1 else ("B0T", b))
                        for h in range(DN):
                            t = nc.tensor.matmul(banks.bank(("WT", b, l))[:, h * P:(h + 1) * P],
                                                 lev[:, l % 2, b, h, :], XT[:, b, h, :], start=True, stop=True)
                        t.then_inc(done, 1)
                    for b in range(TB):
                        banks.wait_taken(pe, ("WT", b, l))
                        for z, lhs, rhs in (("Z", WT, X), ("ZT", X, WT)):
                            if z == "Z" and l == 5:
                                continue
                            banks.wait_free(pe, (z, b, l))
                            for h in range(DN):
                                t = nc.tensor.matmul(banks.bank((z, b, l))[:, h * P:(h + 1) * P],
                                                     lhs[:, b, h, :], rhs[:, b, h, :], start=True, stop=True)
                            t.then_inc(done, 1)
                for b in range(TB):
                    banks.wait_free(pe, ("wT", b))
                    banks.wait_taken(pe, ("ZT", b, 5))
                    pe.wait_ge(tok_scaled, 1)
                    for h in range(DN):
                        t = nc.tensor.matmul(banks.bank(("wT", b))[:, h * P:(h + 1) * P],
                                             kbe[:, h, b * P:(b + 1) * P], XT[:, b, h, :], start=True, stop=True)
                    t.then_inc(done, 1)
                    banks.wait_free(pe, ("u", b))
                    for h in range(DN):
                        t = nc.tensor.matmul(banks.bank(("u", b))[:, h * P:(h + 1) * P],
                                             XT[:, b, h, :], vb[:, h, b * P:(b + 1) * P], start=True, stop=True)
                    t.then_inc(done, 1)

            @block.scalar
            def _(act):
                link = chain(act, alink, [0])
                act.wait_ge(cols, 1)
                nc.scalar.activation(egc[:], gc[:], ACT.Exp).then_inc(col_exp, 1)
                for b in range(TB):
                    banks.wait_full(act, ("grow", b))
                    nc.scalar.activation(m.egrow[:, b], h4(banks.bank(("grow", b))[:]), ACT.Exp)
                    nc.scalar.activation(grow[:, b], h4(banks.bank(("grow", b))[:]),
                                         ACT.Copy).then_inc(banks.taken["act"], 1)
                for b in range(TB):
                    act.wait_ge(diffs, 2 * b + 2)
                    nc.scalar.activation(dec[:, b], dec[:, b], ACT.Exp, scale=-1.0)
                    nc.scalar.activation(decT[:, b], decT[:, b], ACT.Exp).then_inc(decays, 1)
                for l in LV:
                    for b in range(TB):
                        g = ("WT", b, l)
                        banks.wait_full(act, g)
                        if l > 1:
                            banks.wait_full(act, ("ZT", b, l - 1))
                        nc.scalar.activation(WT[:, b], h4(banks.bank(g)[:]), ACT.Copy).then_inc(banks.taken["act"], 1)
                for b in range(TB):
                    banks.wait_full(act, ("wT", b))
                    nc.scalar.activation(m.wT[:, b], h4(banks.bank(("wT", b))[:]),
                                         ACT.Copy).then_inc(banks.taken["act"], 1)

            @block.gpsimd
            def _(pool):
                up = m.upper[:].unsqueeze(1).broadcast_to([P, DN, P])
                low = m.lower[:].unsqueeze(1).broadcast_to([P, DN, P])
                for b in range(TB):
                    pool.wait_ge(decays, b + 1)
                    nc.gpsimd.tensor_tensor(dec[:, b], dec[:, b], low, ALU.mult).then_inc(strict, 1)
                    nc.gpsimd.tensor_tensor(decT[:, b], decT[:, b], up, ALU.mult).then_inc(strict, 1)
                for l in range(6):
                    for b in range(TB):
                        banks.wait_taken(pool, ("kk", b))
                        if l >= 2:
                            banks.wait_full(pool, ("WT", b, l - 2) if l > 2 else ("B0T", b))
                        if l == 2:
                            pool.wait_ge(x0, b + 1)
                        nc.gpsimd.tensor_tensor(lev[:, l % 2, b], mm[:, b],
                                                m.levels[:, l, :].unsqueeze(1).broadcast_to([P, DN, P]),
                                                ALU.mult).then_inc(level_in, 1)

            @block.vector
            def _(dve):
                link = chain(dve, vlink, [0])
                banks.wait_full(dve, "gcol")
                g2 = banks.bank("gcol")[:, 0:32].rearrange("p (s b h) -> p s b h", s=2, b=TB)
                link(nc.vector.tensor_copy(gc[:], g2))
                nc.vector.tensor_tensor(gc[:, 1], gc[:, 1], gc[:, 0], ALU.subtract).then_inc(cols, 1)
                dve.wait_ge(col_exp, 1)
                nc.vector.tensor_tensor(bec[:], m.beta[:], egc[:, 0], ALU.mult).then_inc(banks.taken["dve"], 1)
                for b in range(TB):
                    banks.wait_taken(dve, ("grow", b))
                    link(nc.vector.tensor_tensor(grow[:, b], grow[:, b], bc4(gc[:, 0, b, :]), ALU.subtract))
                    nc.vector.tensor_scalar(dec[:, b], grow[:, b], 0.0, None, ALU.max).then_inc(diffs, 1)
                    nc.vector.tensor_scalar(decT[:, b], grow[:, b], 0.0, None, ALU.min).then_inc(diffs, 1)
                for h in range(DN):
                    v = lambda ap: ap.rearrange("p (b d) -> p b d", d=DH)
                    s = lambda ap: ap[:, :, h].unsqueeze(2).broadcast_to([P, TB, DH])
                    nc.vector.tensor_tensor(v(vb[:, h, :]), v(m.tok[:, 2 * DN + h, :]), s(m.beta), ALU.mult)
                    nc.vector.tensor_tensor(v(kbe[:, h, :]), v(m.tok[:, DN + h, :]), s(bec), ALU.mult)
                    t = nc.vector.tensor_tensor(v(m.kdec[:, h, :]), v(m.tok[:, DN + h, :]), s(egc[:, 1]), ALU.mult)
                t.then_inc(tok_scaled, 1)
                for b in range(TB):
                    dve.wait_ge(strict, 2 * b + 2)
                    link(nc.vector.tensor_tensor(dec[:, b], dec[:, b], bc4(m.beta[:, b, :]), ALU.mult))
                    banks.wait_full(dve, ("kk", b))
                    nc.vector.tensor_tensor(mm[:, b], h4(banks.bank(("kk", b))[:]), dec[:, b],
                                            ALU.mult).then_inc(banks.taken["dve"], 1)
                    banks.wait_full(dve, ("qkT", b))
                    nc.vector.tensor_tensor(m.qkT[:, b], h4(banks.bank(("qkT", b))[:]), decT[:, b],
                                            ALU.mult).then_inc(banks.taken["dve"], 1)
                    nc.vector.tensor_tensor(m.qdT[:, b], m.unitT[:, 0:DN, b * P:(b + 1) * P], m.egrow[:, b], ALU.mult)
                idb = m.ident[:].unsqueeze(1).broadcast_to([P, DN, P])
                for b in range(TB):
                    banks.wait_full(dve, ("B0T", b))
                    nc.vector.tensor_tensor(X[:, b], idb, lev[:, 0, b], ALU.subtract).then_inc(x0, 1)
                    nc.vector.scalar_tensor_tensor(XT[:, b], h4(banks.bank(("B0T", b))[:]), -1.0, idb,
                                                   ALU.mult, ALU.add).then_inc(banks.taken["dve"], 1)
                for l in LV:
                    for b in range(TB):
                        banks.wait_full(dve, ("ZT", b, l))
                        if l < 5:
                            nc.vector.tensor_tensor(X[:, b], X[:, b], h4(banks.bank(("Z", b, l))[:]),
                                                    ALU.subtract).then_inc(banks.taken["dve"], 1)
                        nc.vector.tensor_tensor(XT[:, b], XT[:, b], h4(banks.bank(("ZT", b, l))[:]),
                                                ALU.subtract).then_inc(banks.taken["dve"], 1)
                for b in range(TB):
                    banks.wait_full(dve, ("u", b))
                    nc.vector.tensor_copy(m.u[:, b], h4(banks.bank(("u", b))[:])).then_inc(banks.taken["dve"], 1)


def mixers(nc, m, ps, sem, w_out_in, w_out, sinks, att_out_g, dn_out_g):
    NC = T // CH
    in_ = [sem(f"mixer_small{i}") for i in range(3)]
    ws_done, v_new, s_done, s_new, o_done, o_out = (sem(n) for n in ("ws_done", "v_new", "s_done", "s_new",
                                                                     "o_done", "o_out"))
    zeroed, o_sq, o_ss, o_pow, o_mix = sem("s_zeroed"), sem("o_sq"), sem("o_ss"), sem("o_pow"), sem("z_gate")
    vlink, plink = sem("mix_dve"), sem("mix_pool")
    sc_done, sc_out, negm, prob, den_in, p_done, p_out = (sem(n) for n in (
        "att_scores", "att_scores_out", "att_negmax", "att_probs", "att_sink_exp", "att_pT", "att_pT_out"))
    pv_done, att_o, att_ss, att_rms = (sem(n) for n in ("att_pv", "att_o", "att_ss", "att_rms"))
    bV, bO, bS, bPV = ps[0], ps[1], ps[2], ps[3]
    bA = ps[4:8]

    with ExitStack() as ctx:
        sb = m.mem.local(ctx)
        S = sb("state", [P, 2, DN, P])
        vnew = sb("v_new_t", [P, DN, P])
        ot = sb("o_tok", [P, TB, DNW])
        osq = sb("o_sqr", [P, DNW])
        oss = sb("o_sss", [P, TB, DN])
        dg = sb("dn_gain", [P, DH])
        ag = sb("att_gain", [P, ATT])
        snk = sb("sinks_b", [P, NH])
        sc = sb("att_sc", [P, NH, 2 * P])
        mx = sb("att_mx", [P, TB, NH])
        nm = sb("att_nm", [P, TB, NH])
        sm = sb("att_sm", [P, TB, NH])
        den = sb("att_den", [P, TB, NH])
        pT = sb("att_pTs", [P, 2 * NH, P])
        ao = sb("att_ot", [P, ATT])
        aj = sb("att_junk", [P, ATT])
        ass = sb("att_rss", [P, TB])
        r4 = lambda ap: ap.rearrange("p (h d) -> p h d", h=DN)
        with nc.Block() as block:
            @block.sync
            def _(sp):
                sp.dma_start(snk[:], sinks[0:1, :].broadcast_to([P, NH])).then_inc(in_[0], 16)
                sp.dma_start(ag[:], att_out_g[0:1, :].broadcast_to([P, ATT])).then_inc(in_[1], 16)
                sp.dma_start(dg[:], dn_out_g[0:1, :].broadcast_to([P, DH])).then_inc(in_[2], 16)
                for i in range(2):
                    v = w_out[0].rearrange("(k p) n -> p k n", p=P)
                    sp.dma_start(m.w_raw[i], v[:, :, i * T:(i + 1) * T]).then_inc(w_out_in[i], 16)

            @block.tensor
            def _(pe):
                def scores(b):
                    lo = 0 if b else P
                    if b:
                        pe.wait_ge(p_out, 4 * b)
                    for i in range(4):
                        v = slice(HD * (i // 2), HD * (i // 2) + HD)
                        for e in range(2):
                            g = 2 * (i % 2) + e
                            t = nc.tensor.matmul(bA[i][:, e * 2 * P + lo:(e + 1) * 2 * P],
                                                 m.attqT[v, g, b * P:(b + 1) * P],
                                                 m.attkT[v, (b - 1) * P + lo:(b + 1) * P], start=True, stop=True)
                    t.then_inc(sc_done, 1)

                def p_transposes(b):
                    for i in range(4):
                        pe.wait_ge(prob, NH * b + 2 * i + 2)
                        if i == 0:
                            pe.wait_ge(sc_out, 4 * b + 4)
                        for e in range(2):
                            for half in range(0 if b else 1, 2):
                                t = nc.tensor.transpose(bA[i][:, (2 * e + half) * P:(2 * e + half + 1) * P],
                                                        sc[:, 2 * i + e, half * P:(half + 1) * P], m.ident[:])
                        t.then_inc(p_done, 1)

                def pv(b):
                    pe.wait_ge(p_out, 4 * b + 4)
                    if b:
                        pe.wait_ge(att_o, b)
                    for h in range(NH):
                        kv = h // GRP
                        for half in range(0 if b else 1, 2):
                            t = nc.tensor.matmul(bPV[:, h * HD:(h + 1) * HD], pT[:, 2 * h + half, :],
                                                 m.kva[:, b - 1 + half, KVW + kv * HD:KVW + (kv + 1) * HD],
                                                 start=(half == 0 or b == 0), stop=(half == 1))
                    t.then_inc(pv_done, 1)

                scores(0)
                for c in range(NC):
                    b, q = c // 2, c % 2
                    r = slice(q * CH, (q + 1) * CH)
                    if c == 0:
                        pe.wait_ge(zeroed, 1)
                    else:
                        pe.wait_ge(s_new, DN * c)
                    for h in range(DN):
                        t = nc.tensor.matmul(bV[r, h * P:(h + 1) * P], m.wT[:, b, h, r], S[:, c % 2, h, :],
                                             start=True, stop=True)
                    t.then_inc(ws_done, 1)
                    if q == 0:
                        p_transposes(b)
                    else:
                        pv(b)
                        if b + 1 < TB:
                            scores(b + 1)
                    pe.wait_ge(v_new, c + 1)
                    for h in range(DN):
                        t = nc.tensor.matmul(bS[:, h * P:(h + 1) * P], m.kdec[r, h, b * P:(b + 1) * P],
                                             vnew[r, h, :], start=True, stop=True)
                    t.then_inc(s_done, 1)
                    if c:
                        pe.wait_ge(o_out, c)
                    for h in range(DN):
                        nc.tensor.matmul(bO[r, h * P:(h + 1) * P], m.qdT[:, b, h, r], S[:, c % 2, h, :],
                                         start=True, stop=False)
                        t = nc.tensor.matmul(bO[r, h * P:(h + 1) * P], m.qkT[r, b, h, r], vnew[r, h, :],
                                             start=False, stop=True)
                    t.then_inc(o_done, 1)

            @block.vector
            def _(dve):
                link = chain(dve, vlink, [0])

                def att_max(b):
                    lo = 0 if b else P
                    for i in range(4):
                        dve.wait_ge(sc_done, b + 1)
                        if i == 0 and b:
                            dve.wait_ge(p_done, 4 * b)
                        t = nc.vector.tensor_tensor(
                            sc[:, 2 * i:2 * i + 2, lo:], bA[i][:].rearrange("p (e k) -> p e k", e=2)[:, :, lo:],
                            m.att_mask[:, lo:].unsqueeze(1).broadcast_to([P, 2, 2 * P - lo]), ALU.add)
                        t.then_inc(sc_out, 1)
                    dve.wait_ge(sc_out, 4 * b + 4)
                    link(nc.vector.tensor_reduce(mx[:, b, :], sc[:, :, lo:], AX, ALU.max))
                    if b == 0:
                        dve.wait_ge(in_[0], 16)
                    link(nc.vector.tensor_tensor(mx[:, b, :], mx[:, b, :], snk[:], ALU.max))
                    link(nc.vector.tensor_tensor(sm[:, b, :], snk[:], mx[:, b, :], ALU.subtract))
                    nc.vector.tensor_scalar(nm[:, b, :], mx[:, b, :], -1.0, None, ALU.mult).then_inc(negm, 1)

                def att_out(b):
                    dve.wait_ge(den_in, b + 1)
                    link(nc.vector.tensor_tensor(den[:, b, :], den[:, b, :], sm[:, b, :], ALU.add))
                    link(nc.vector.reciprocal(den[:, b, :], den[:, b, :]))
                    dve.wait_ge(pv_done, b + 1)
                    nc.vector.tensor_tensor(ao[:].rearrange("p (h d) -> p h d", d=HD),
                                            bPV[:].rearrange("p (h d) -> p h d", d=HD),
                                            den[:, b, :].unsqueeze(2).broadcast_to([P, NH, HD]),
                                            ALU.mult).then_inc(att_o, 1)

                def att_norm(b):
                    if b == 0:
                        dve.wait_ge(in_[1], 16)
                    dve.wait_ge(att_rms, b + 1)
                    link(nc.vector.scalar_tensor_tensor(m.mix[:, b, 0:ATT], ao[:], ass[:, b:b + 1], ag[:],
                                                        ALU.mult, ALU.mult))

                def o_sum(b):
                    dve.wait_ge(o_sq, b + 1)
                    nc.vector.tensor_reduce(oss[:, b, :], r4(osq[:]), AX, ALU.add).then_inc(o_ss, 1)

                def o_norm(b):
                    dve.wait_ge(o_pow, b + 1)
                    link(nc.vector.tensor_tensor(r4(ot[:, b, :]), r4(ot[:, b, :]),
                                                 oss[:, b, :].unsqueeze(2).broadcast_to([P, DN, DH]), ALU.mult))
                    nc.vector.tensor_tensor(m.mix[:, b, ATT:], ot[:, b, :], m.z[:, b, :], ALU.mult)

                nc.vector.memset(S[:, 0], 0.0).then_inc(zeroed, 1)
                att_max(0)
                dve.wait_ge(o_mix, 1)
                dve.wait_ge(in_[2], 16)
                for b in range(TB):
                    t = nc.vector.tensor_tensor(r4(m.z[:, b, :]), r4(m.z[:, b, :]),
                                                dg[:].unsqueeze(1).broadcast_to([P, DN, DH]), ALU.mult)
                link(t)
                for c in range(NC):
                    b, q = c // 2, c % 2
                    r = slice(q * CH, (q + 1) * CH)
                    dve.wait_ge(ws_done, c + 1)
                    if c:
                        dve.wait_ge(o_done, c)
                    nc.vector.tensor_tensor(vnew[r], m.u[r, b], r4(bV[:])[r], ALU.subtract).then_inc(v_new, 1)
                    if q == 1:
                        att_out(b)
                        if b + 1 < TB:
                            att_max(b + 1)
                    dve.wait_ge(s_done, c + 1)
                    last = (q + 1) * CH - 1
                    for h in range(DN):
                        nc.vector.scalar_tensor_tensor(S[:, (c + 1) % 2, h, :], S[:, c % 2, h, :],
                                                       m.egrow[:, b, h, last:last + 1],
                                                       bS[:, h * P:(h + 1) * P], ALU.mult, ALU.add).then_inc(s_new, 1)
                    if q == 0 and b:
                        att_norm(b - 1)
                        o_sum(b - 1)
                    elif b:
                        o_norm(b - 1)
                att_norm(TB - 1)
                o_sum(TB - 1)
                o_norm(TB - 1)

            @block.gpsimd
            def _(pool):
                link = chain(pool, plink, [0])
                for b in range(TB):
                    pool.wait_ge(att_ss, b + 1)
                    link(nc.gpsimd.tensor_scalar(ass[:, b:b + 1], ass[:, b:b + 1], 1.0 / ATT, EPS, ALU.mult, ALU.add))
                    nc.gpsimd.tensor_tensor(ass[:, b:b + 1], ass[:, b:b + 1], m.neg_half[:, 0:1],
                                            ALU.pow).then_inc(att_rms, 1)
                    pool.wait_ge(o_ss, b + 1)
                    link(nc.gpsimd.tensor_scalar(oss[:, b, :], oss[:, b, :], 1.0 / DH, EPS, ALU.mult, ALU.add))
                    nc.gpsimd.tensor_tensor(oss[:, b, :], oss[:, b, :], m.neg_half[:, 0:1].broadcast_to([P, DN]),
                                            ALU.pow).then_inc(o_pow, 1)

            @block.scalar
            def _(act):
                def probs(b):
                    lo = 0 if b else P
                    act.wait_ge(negm, b + 1)
                    for h in range(NH):
                        nc.scalar.activation(sc[:, h, lo:], sc[:, h, lo:], ACT.Exp, bias=nm[:, b, h:h + 1],
                                             accum_out=den[:, b, h:h + 1]).then_inc(prob, 1)
                    nc.scalar.activation(sm[:, b, :], sm[:, b, :], ACT.Exp).then_inc(den_in, 1)

                def pT_copies(b):
                    for i in range(4):
                        act.wait_ge(p_done, 4 * b + i + 1)
                        if i == 0 and b:
                            act.wait_ge(pv_done, b)
                        out = pT[:, 4 * i:4 * i + 4, :].rearrange("p (e f) q -> p e f q", e=2)
                        src = bA[i][:].rearrange("p (e f q) -> p e f q", e=2, f=2)
                        lo = 0 if b else 1
                        nc.scalar.activation(out[:, :, lo:], src[:, :, lo:], ACT.Copy).then_inc(p_out, 1)

                def att_square(b):
                    act.wait_ge(att_o, b + 1)
                    nc.scalar.activation(aj[:], ao[:], ACT.Square, accum_out=ass[:, b:b + 1]).then_inc(att_ss, 1)

                nc.scalar.activation(m.z[:], m.z[:], ACT.Silu).then_inc(o_mix, 1)
                for c in range(NC):
                    b, q = c // 2, c % 2
                    r = slice(q * CH, (q + 1) * CH)
                    if q == 0:
                        probs(b)
                        pT_copies(b)
                    act.wait_ge(o_done, c + 1)
                    nc.scalar.activation(ot[r, b, :], bO[r, :], ACT.Copy).then_inc(o_out, 1)
                    if q == 1:
                        att_square(b)
                        act.wait_ge(o_out, c + 1)
                        if b:
                            act.wait_ge(o_ss, b)
                        nc.scalar.activation(osq[:], ot[:, b, :], ACT.Square).then_inc(o_sq, 1)


def output_projection(nc, m, ps, sem, w_out_in, early_u_in, u_t, x, norm_ffn_g, w_q, keys, h_dram):
    done, plink = sem("out_done"), sem("out_pool")
    w_ld = w_out_in + [sem(f"w_q_in{i}") for i in range(2)]
    w_hi, w_lo, mix_hi = sem("w_oq_hi"), sem("w_oq_lo"), sem("mix_hi")
    acc_in, h_spilled, k_in, x_hi = sem("x_again"), sem("h_spilled"), sem("keys_in"), sem("x_hi")
    g_in, squares, scale, normed = sem("ffn_gain_in"), sem("h_squares"), sem("h_scale"), sem("h_normed")
    banks = Banks(ps, done, {"act": sem("out_by_act"), "dve": sem("out_by_dve")})
    halves = [(b, half) for b in range(TB) for half in range(2)]
    tail = [("h", 1, 0), ("h", 1, 1), ("h", 1, 2), ("xT", 0), ("h", 1, 3), ("xT", 1), ("xT", 2), ("xT", 3)]
    for b, half in halves:
        banks.add(("mixT", b, half), "dve")
    for b in range(TB):
        banks.add(("h", 0, b), "dve")
    for g in tail:
        for name in ([g] if g[0] == "h" else [g + (0,), g + (1,)]):
            banks.add(name, "dve")
    for h in range(PH):
        banks.add(("q", h), "dve" if h % 2 else "act")
    for b in range(TB):
        for hh in range(2):
            for p in range(2):
                banks.add(("s", b, p, hh), "dve" if p else "act")
    last = [("h", 0, TB - 1), ("h", 1, TB - 1)]

    def k4(ap):
        return ap.rearrange("p (k t) -> p k t", k=4)

    def part(t, b, half):
        return t[:, 4 * half:4 * half + 4, b * P:(b + 1) * P]

    with ExitStack() as ctx:
        sb = m.mem.local(ctx)
        gain = sb("ffn_gain", [P, D])
        mixh = sb("mixT_hi", [P, KD, T], F32R)
        mixl = sb("mixT_lo", [P, KD, T], F32R)
        wh = sb("w_oq_h", [P, 2, KD, T], F32R)
        wl = sb("w_oq_l", [P, 2, KD, T], F32R)
        ss = sb("h_ss", [P, TB])
        kt = m.mem.over("sub_keys", [P, PH, NK], "ffn_gain")
        w = m.w_raw
        qT = m.mem.over("qT", [P, PH, T], "mixT_hi")
        xn = m.mix
        with nc.Block() as block:
            @block.sync
            def _(sp):
                sp.dma_start(m.acc[:], x[0].rearrange("(b p) d -> p b d", p=P)).then_inc(acc_in, 16)
                for i in range(2):
                    sp.wait_ge(w_lo, i + 1)
                    v = w_q[0].rearrange("(k p) n -> p k n", p=P)
                    sp.dma_start(w[i], v[:, :, i * T:(i + 1) * T]).then_inc(w_ld[2 + i], 16)
                sp.dma_start(gain[:], norm_ffn_g[0:1, :].broadcast_to([P, D])).then_inc(g_in, 16)
                for i in range(2):
                    sp.dma_start(m.u_raw[:, i, :], u_t[NK - EARLY + i]).then_inc(early_u_in[i], 16)
                sp.wait_ge(normed, TB)
                sp.dma_start(kt[:], keys.rearrange("p (h n) -> p h n", h=PH)).then_inc(k_in, 16)
                banks.wait_taken(sp, ("h", 1, TB - 1))
                sp.dma_start(h_dram, m.acc[:]).then_inc(h_spilled, 16)
                sp.wait_ge(h_spilled, 16)

            @block.tensor
            def _(pe):
                def transposes(g, src):
                    banks.wait_free(pe, g)
                    for k in range(4):
                        kk = 4 * g[2] + k
                        t = nc.tensor.transpose(banks.bank(g)[:, k * P:(k + 1) * P],
                                                src[:, g[1], kk * P:(kk + 1) * P], m.ident[:])
                    t.then_inc(done, 1)

                def product(g, lh, ll, rh, rl):
                    banks.wait_free(pe, g)
                    for k in range(KD):
                        nc.tensor.matmul(banks.bank(g)[:], lh(k), rh(k), start=(k == 0), stop=False)
                        nc.tensor.matmul(banks.bank(g)[:], lh(k), rl(k), start=False, stop=False)
                        t = nc.tensor.matmul(banks.bank(g)[:], ll(k), rh(k), start=False, stop=(k == KD - 1))
                    t.then_inc(done, 1)

                def h_product(g):
                    half, b = g[1:]
                    pe.wait_ge(w_lo, half + 1)
                    v = slice(b * P, (b + 1) * P)
                    product(g, lambda k: mixh[:, k, v], lambda k: mixl[:, k, v],
                            lambda k: wh[:, half, k, :], lambda k: wl[:, half, k, :])

                for b, half in halves:
                    transposes(("mixT", b, half), m.mix)
                for b in range(TB):
                    banks.wait_taken(pe, ("mixT", b, 1))
                    h_product(("h", 0, b))
                for g in tail:
                    if g[0] == "h":
                        h_product(g)
                    else:
                        pe.wait_ge(normed, g[1] + 1)
                        for half in range(2):
                            transposes(g + (half,), xn)
                banks.wait_taken(pe, ("xT", TB - 1, 1))
                for h in range(PH):
                    i = h // 4
                    pe.wait_ge(w_lo, 3 + i)
                    v = slice((h % 4) * P, (h % 4 + 1) * P)
                    product(("q", h), lambda k: wh[:, i, k, v], lambda k: wl[:, i, k, v],
                            lambda k: m.xh[:, k, :], lambda k: m.xl[:, k, :])
                banks.wait_taken(pe, ("q", PH - 2))
                banks.wait_taken(pe, ("q", PH - 1))
                pe.wait_ge(k_in, 16)
                for b in range(TB):
                    for hh in range(2):
                        for p in range(2):
                            g = ("s", b, p, hh)
                            banks.wait_free(pe, g)
                            for h in range(4):
                                v = slice(p * HALF, (p + 1) * HALF)
                                t = nc.tensor.matmul(banks.bank(g)[:, h * NK:(h + 1) * NK],
                                                     qT[v, 4 * hh + h, b * P:(b + 1) * P],
                                                     kt[v, 4 * hh + h, :], start=True, stop=True)
                            t.then_inc(done, 1)

            @block.scalar
            def _(act):
                def split_w(i):
                    act.wait_ge(w_ld[i], 16)
                    if i >= 2:
                        banks.wait_full(act, last[i - 2])
                    nc.scalar.activation(wh[:, i % 2], w[i % 2], ACT.Copy).then_inc(w_hi, 1)

                def square(b):
                    banks.wait_taken(act, ("h", 1, b))
                    nc.scalar.activation(xn[:, b, :], m.acc[:, b, :], ACT.Square,
                                         accum_out=ss[:, b:b + 1]).then_inc(squares, 1)

                split_w(0)
                for b, half in halves:
                    g = ("mixT", b, half)
                    banks.wait_full(act, g)
                    nc.scalar.activation(part(mixh, b, half), k4(banks.bank(g)[:]), ACT.Copy).then_inc(mix_hi, 1)
                split_w(1)
                split_w(2)
                for g in tail:
                    if g[0] == "h":
                        square(g[2])
                    else:
                        for half in range(2):
                            banks.wait_full(act, g + (half,))
                            nc.scalar.activation(part(m.xh, g[1], half), k4(banks.bank(g + (half,))[:]),
                                                 ACT.Copy).then_inc(x_hi, 1)
                split_w(3)
                for h in range(0, PH, 2):
                    banks.wait_full(act, ("q", h))
                    nc.scalar.activation(qT[:, h, :], banks.bank(("q", h))[:],
                                         ACT.Copy).then_inc(banks.taken["act"], 1)
                for b in range(TB):
                    for hh in range(2):
                        g = ("s", b, 0, hh)
                        banks.wait_full(act, g)
                        nc.scalar.activation(m.s[:, b, 0, 4 * hh:4 * hh + 4, :],
                                             banks.bank(g)[:].rearrange("p (h n) -> p h n", h=4),
                                             ACT.Copy).then_inc(banks.taken["act"], 1)

            @block.gpsimd
            def _(pool):
                link = chain(pool, plink, [0])
                for b in range(TB):
                    pool.wait_ge(squares, b + 1)
                    link(nc.gpsimd.tensor_scalar(ss[:, b:b + 1], ss[:, b:b + 1], 1.0 / D, EPS, ALU.mult, ALU.add))
                    nc.gpsimd.tensor_tensor(ss[:, b:b + 1], ss[:, b:b + 1], m.neg_half[:, 0:1],
                                            ALU.pow).then_inc(scale, 1)

            @block.vector
            def _(dve):
                def split_w(i):
                    dve.wait_ge(w_hi, i + 1)
                    nc.vector.tensor_tensor(wl[:, i % 2], w[i % 2], wh[:, i % 2].bitcast(F32),
                                            ALU.subtract).then_inc(w_lo, 1)

                def low(t, hi, g, ready):
                    dve.wait_ge(ready, 2 * g[1] + g[2] + 1)
                    nc.vector.tensor_tensor(part(t, g[1], g[2]), k4(banks.bank(g)[:]),
                                            part(hi, g[1], g[2]).bitcast(F32),
                                            ALU.subtract).then_inc(banks.taken["dve"], 1)

                def add_h(g):
                    half, b = g[1:]
                    banks.wait_full(dve, g)
                    v = m.acc[:, b, half * T:(half + 1) * T]
                    nc.vector.tensor_tensor(v, v, banks.bank(g)[:], ALU.add).then_inc(banks.taken["dve"], 1)

                def rows(b):
                    dve.wait_ge(scale, b + 1)
                    nc.vector.scalar_tensor_tensor(xn[:, b, :], m.acc[:, b, :], ss[:, b:b + 1], gain[:],
                                                   ALU.mult, ALU.mult).then_inc(normed, 1)

                split_w(0)
                for b, half in halves:
                    low(mixl, mixh, ("mixT", b, half), mix_hi)
                split_w(1)
                dve.wait_ge(acc_in, 16)
                for b in range(TB):
                    add_h(("h", 0, b))
                split_w(2)
                dve.wait_ge(g_in, 16)
                add_h(tail[0])
                for g in tail[1:]:
                    if g[0] == "h":
                        add_h(g)
                        if g[2] < 3:
                            rows(g[2] - 1)
                    else:
                        if g[1] in (1, 2):
                            rows(g[1] + 1)
                        for half in range(2):
                            low(m.xl, m.xh, g + (half,), x_hi)
                split_w(3)
                for h in range(1, PH, 2):
                    banks.wait_full(dve, ("q", h))
                    nc.vector.tensor_copy(qT[:, h, :], banks.bank(("q", h))[:]).then_inc(banks.taken["dve"], 1)
                for b in range(TB):
                    for hh in range(2):
                        g = ("s", b, 1, hh)
                        banks.wait_full(dve, g)
                        nc.vector.tensor_copy(m.s[:, b, 1, 4 * hh:4 * hh + 4, :],
                                              banks.bank(g)[:].rearrange("p (h n) -> p h n", h=4)
                                              ).then_inc(banks.taken["dve"], 1)


def routing(nc, m, ps, sem, u_in, next_u, u_t, gates, gelus):
    done, vlink = sem("rt_done"), sem("rt_dve")
    subbed, exped, r1_row, masked, r2_ready, r1_ready, iota_made = (sem(n) for n in (
        "rt_subtracted", "rt_exps", "rt_r1_rows", "rt_masked", "rt_r2", "rt_r1", "rt_iota"))
    r1_pool = sem("rt_r1_pool")
    u_hi, u_lo = sem("early_u_hi"), sem("early_u_lo")
    ge_out = sem("early_gelu_out")
    stored = [sem("gates_out0"), sem("gates_out1")]
    banks = Banks(ps, done, {"act": sem("rt_by_act"), "dve": sem("rt_by_dve")})
    JS = 16
    NS = NK // JS
    RING = 12
    ST = 16
    FIRST = 6
    AFTER = [(0, 2, 3, 4, 5)] + [(-1, 0, 1, 2, 3, 4, 5)] * (TB - 1)
    assert FIRST + sum(len(v) for v in AFTER) == EARLY

    def early(b, e):
        if b < 0:
            return range(FIRST)
        n = FIRST + sum(len(v) for v in AFTER[:b]) + sum(i < e for i in AFTER[b])
        return range(n, n + (e in AFTER[b]))

    for n in early(-1, 0):
        banks.add(("up", n), "act")
    for b in range(TB):
        for n in early(b, -1):
            banks.add(("up", n), "act")
        banks.add(("small", b), "dve")
        for e in range(NS):
            for k in range(JS // 4):
                banks.add(("r2T", b, e, k), "act")
            for n in early(b, e):
                banks.add(("up", n), "act")
        for k in range(P // 4):
            banks.add(("G", b, k), "act")

    with ExitStack() as ctx:
        sb = m.mem.local(ctx)
        r2T = sb("r2T", [P, P, NK])
        stage = sb("gate_stage", [P, 2, NK // GJ, ST, GJ])
        r2 = sb("r2", [P, 2, HA, JS])
        e2 = sb("e2", [P, 2, PH, NK])
        cand = sb("sums", [P, PH, NPAIR])
        top = sb("top", [P, 2, PH, TOPK])
        best = sb("best", [P, PH, TOPK])
        theta = sb("theta", [P, 2, PH, TOPK])
        small = sb("rt_small", [P, 2, HA])
        key_row = small[:, 0, :].rearrange("p (h a) -> p h a", h=PH)
        idx = key_row.bitcast(U32)
        e1 = small[:, 1, :].rearrange("p (h a) -> p h a", h=PH)
        smallT = sb("rt_smallT", [P, 2, P])
        zsum = sb("rt_z", [P, PH])
        iota = sb("rt_iota_row", [P, NK])
        r1 = sb("r1", [P, RING, NK])
        u_raw = m.u_raw
        uh = sb("early_u_h", [P, 2, D], F32R)
        ul = sb("early_u_l", [P, 2, D], F32R)
        ge = sb("early_gelu", [P, T])

        def rows(buf, off, r, w):
            return buf[:, :, off:off + r * w].rearrange("p h (r w) -> p h r w", w=w)

        def first(a, r, w):
            return top[:, 0, :, a:a + r].unsqueeze(3).broadcast_to([P, PH, r, w])

        def second(r, w):
            return top[:, 1, :, 0:w].unsqueeze(2).broadcast_to([P, PH, r, w])

        def bc(ap, n):
            return ap.broadcast_to([P, PH, n])

        def u_low(on, n):
            return on.tensor_tensor(ul[:, n % 2, :], u_raw[:, n % 2, :], uh[:, n % 2, :].bitcast(F32), ALU.subtract)

        def wait_ring(eng, b, k):
            n = 32 * b + k - RING // 4
            if n >= 0:
                banks.wait_full(eng, ("G", n // 32, n % 32))

        def one_hot(on, b, t):
            return on.tensor_scalar(r1[:, (P * b + t) % RING, :], iota[:], smallT[:, 0, t:t + 1],
                                    smallT[:, 1, t:t + 1], ALU.is_equal, ALU.mult)

        with nc.Block() as block:
            @block.sync
            def _(sp):
                def load_u(n):
                    sp.wait_ge(u_lo, n - 1)
                    sp.dma_start(u_raw[:, n % 2, :], u_t[NK - EARLY + n]).then_inc(u_in[n % 2], 16)

                for n in range(2, FIRST + 2):
                    load_u(n)
                for b in range(TB):
                    for e in range(-1, NS):
                        for n in early(b, e):
                            if n + 2 < EARLY:
                                load_u(n + 2)
                            else:
                                i = n + 2 - EARLY
                                sp.wait_ge(u_lo, n + 1)
                                sp.dma_start(u_raw[:, i, :], u_t[i]).then_inc(next_u[i], 16)
                    for k in range(P // ST):
                        banks.wait_taken(sp, ("G", b, (k + 1) * ST // 4 - 1))
                        t0 = b * P + k * ST
                        sp.dma_start(gates[:, :, t0:t0 + ST, :].rearrange("g i t j -> i g (t j)"),
                                     stage[:, k % 2].rearrange("p g t j -> p g (t j)")).then_inc(stored[k % 2], 16)
                for half in range(2):
                    sp.wait_ge(stored[half], 16 * (T // ST // 2))
                sp.wait_ge(ge_out, 16 * EARLY)

            @block.gpsimd
            def _(pool):
                nc.gpsimd.iota(iota[:], pattern=[[1, NK]], base=0, channel_multiplier=0,
                               allow_small_or_imprecise_dtypes=True).then_inc(iota_made, 1)
                for n in early(-1, 0):
                    pool.wait_ge(u_hi, n + 1)
                    u_low(nc.gpsimd, n).then_inc(u_lo, 1)
                for b in range(TB):
                    for e in range(NS):
                        pool.wait_ge(masked, NS * b + e + 1)
                        v = r2[:, e % 2].rearrange("p (h a) j -> p h a j", h=PH)
                        nc.gpsimd.tensor_tensor(v, v, e2[:, b % 2, :, e * JS:(e + 1) * JS].unsqueeze(2)
                                                .broadcast_to([P, PH, TOPK, JS]), ALU.mult).then_inc(r2_ready, 1)
                    banks.wait_taken(pool, ("small", b))
                    for k in range(1, P // 4, 2):
                        wait_ring(pool, b, k)
                        one_hot(nc.gpsimd, b, 4 * k + 3).then_inc(r1_pool, 1)

            @block.tensor
            def _(pe):
                def up(n):
                    g = ("up", n)
                    banks.wait_free(pe, g)
                    pe.wait_ge(u_lo, n + 1)
                    q = n % 2
                    for k in range(KD):
                        w = slice(k * P, (k + 1) * P)
                        nc.tensor.matmul(banks.bank(g)[:], uh[:, q, w], m.xh[:, k, :], start=(k == 0), stop=False)
                        nc.tensor.matmul(banks.bank(g)[:], uh[:, q, w], m.xl[:, k, :], start=False, stop=False)
                        t = nc.tensor.matmul(banks.bank(g)[:], ul[:, q, w], m.xh[:, k, :], start=False,
                                             stop=(k == KD - 1))
                    t.then_inc(done, 1)

                for n in early(-1, 0):
                    up(n)
                for b in range(TB):
                    for n in early(b, -1):
                        up(n)
                    banks.wait_free(pe, ("small", b))
                    pe.wait_ge(r1_row, b + 1)
                    for i in range(2):
                        t = nc.tensor.transpose(banks.bank(("small", b))[:, i * P:(i + 1) * P], small[:, i, :],
                                                m.ident[:])
                    t.then_inc(done, 1)
                    for e in range(NS):
                        pe.wait_ge(r2_ready, NS * b + e + 1)
                        for k in range(JS // 4):
                            g = ("r2T", b, e, k)
                            banks.wait_free(pe, g)
                            for i in range(4):
                                t = nc.tensor.transpose(banks.bank(g)[:, i * P:(i + 1) * P],
                                                        r2[:, e % 2, :, 4 * k + i], m.ident[:])
                            t.then_inc(done, 1)
                        for n in early(b, e):
                            up(n)
                    banks.wait_taken(pe, ("r2T", b, NS - 1, JS // 4 - 1))
                    for k in range(P // 4):
                        g = ("G", b, k)
                        banks.wait_free(pe, g)
                        pe.wait_ge(r1_ready, 32 * b + k + 1)
                        if k % 2:
                            pe.wait_ge(r1_pool, 16 * b + k // 2 + 1)
                        for i in range(4):
                            t = nc.tensor.matmul(banks.bank(g)[:, i * NK:(i + 1) * NK],
                                                 r1[:, (P * b + 4 * k + i) % RING, :], r2T[:, 4 * k + i, :],
                                                 start=True, stop=True)
                        t.then_inc(done, 1)

            @block.scalar
            def _(act):
                def split_u(n):
                    act.wait_ge(u_in[n % 2], 16 * (n // 2 + 1))
                    if n >= 2:
                        banks.wait_full(act, ("up", n - 2))
                    nc.scalar.activation(uh[:, n % 2, :], u_raw[:, n % 2, :], ACT.Copy).then_inc(u_hi, 1)

                def gelu(n):
                    banks.wait_full(act, ("up", n))
                    if n:
                        act.wait_ge(ge_out, 16 * n)
                    nc.scalar.activation(ge[:], banks.bank(("up", n))[:],
                                         ACT.Gelu).then_inc(banks.taken["act"], 1)
                    if n + 2 < EARLY:
                        split_u(n + 2)
                    banks.wait_taken(act, ("up", n))
                    act.dma_start(gelus[n], ge[:]).then_inc(ge_out, 16)

                def exps(b):
                    act.wait_ge(subbed, b + 1)
                    nc.scalar.activation(best[:], best[:], ACT.Exp)
                    nc.scalar.activation(e1, e1, ACT.Exp)
                    nc.scalar.activation(e2[:, b % 2], e2[:, b % 2], ACT.Exp).then_inc(exped, 1)

                split_u(0)
                split_u(1)
                for n in early(-1, 0):
                    gelu(n)
                    if n == 2:
                        exps(0)
                for b in range(TB):
                    for n in early(b, -1):
                        gelu(n)
                    for e in range(NS):
                        for k in range(JS // 4):
                            g = ("r2T", b, e, k)
                            banks.wait_full(act, g)
                            if b and e == 0 and k == 0:
                                banks.wait_full(act, ("G", b - 1, P // 4 - 1))
                            j0 = e * JS + 4 * k
                            nc.scalar.activation(r2T[:, :, j0:j0 + 4].rearrange("p t j -> p j t"),
                                                 banks.bank(g)[:].rearrange("p (j t) -> p j t", j=4),
                                                 ACT.Copy).then_inc(banks.taken["act"], 1)
                        for n in early(b, e):
                            gelu(n)
                    if b + 1 < TB:
                        exps(b + 1)
                    for k in range(P // 4):
                        g = ("G", b, k)
                        banks.wait_full(act, g)
                        slot, q = (4 * k // ST) % 2, b * (P // ST) + 4 * k // ST
                        if q >= 2 and 4 * k % ST == 0:
                            act.wait_ge(stored[slot], 16 * (q // 2))
                        t0 = 4 * k % ST
                        nc.scalar.activation(stage[:, slot, :, t0:t0 + 4, :].rearrange("p g t j -> p t g j"),
                                             banks.bank(g)[:].rearrange("p (t g j) -> p t g j", t=4, j=GJ),
                                             ACT.Copy).then_inc(banks.taken["act"], 1)

            @block.vector
            def _(dve):
                link = chain(dve, vlink, [0])

                def prepare(b, part):
                    s1, s2, left = m.s[:, b, 0], m.s[:, b, 1], e2[:, b % 2]
                    th = theta[:, b % 2]
                    if part == 0:
                        for h in range(PH):
                            nc.vector.max(top[:, 0, h, 0:8], s1[:, h, :])
                        for h in range(PH):
                            t = nc.vector.max(top[:, 1, h, 0:8], s2[:, h, :])
                        link(t)
                    elif part == 1:
                        if b >= 2:
                            dve.wait_ge(r2_ready, NS * (b - 1))
                        for h in range(PH):
                            t = nc.vector.max_index(idx[:, h, 0:8], top[:, 0, h, 0:8], s1[:, h, :])
                        link(t)
                        for h in range(PH):
                            nc.vector.match_replace(out=s1[:, h, :], in_to_replace=top[:, 0, h, 0:8],
                                                    in_values=s1[:, h, :], imm_value=-BIG)
                        for h in range(PH):
                            t = nc.vector.match_replace(out=left[:, h, :], in_to_replace=top[:, 1, h, 0:8],
                                                        in_values=s2[:, h, :], imm_value=-BIG)
                        link(t)
                    elif part == 2:
                        for h in range(PH):
                            nc.vector.max(top[:, 0, h, 8:16], s1[:, h, :])
                        for h in range(PH):
                            t = nc.vector.max(top[:, 1, h, 8:16], left[:, h, :])
                        link(t)
                        for h in range(PH):
                            nc.vector.max_index(idx[:, h, 8:16], top[:, 0, h, 8:16], s1[:, h, :])
                    elif part == 3:
                        off = 0
                        for a, r, w in PAIRS:
                            t = nc.vector.tensor_tensor(rows(cand, off, r, w), first(a, r, w), second(r, w), ALU.add)
                            off += r * w
                        link(t)
                        for h in range(PH):
                            t = nc.vector.max(best[:, h, 0:8], cand[:, h, :])
                        link(t)
                        for h in range(PH):
                            t = nc.vector.match_replace(out=cand[:, h, :], in_to_replace=best[:, h, 0:8],
                                                        in_values=cand[:, h, :], imm_value=-BIG)
                        link(t)
                    elif part == 4:
                        for h in range(PH):
                            t = nc.vector.max(best[:, h, 8:16], cand[:, h, :])
                        link(t)
                        for h in range(PH):
                            t = nc.vector.match_replace(out=cand[:, h, :], in_to_replace=best[:, h, 8:16],
                                                        in_values=cand[:, h, :], imm_value=-BIG)
                        link(t)
                    elif part == 5:
                        link(nc.vector.tensor_scalar(cand[:], cand[:], -BIG, BIG, ALU.is_gt, ALU.mult))
                        off = 0
                        for a, r, w in PAIRS:
                            v = rows(cand, off, r, w)
                            t = nc.vector.tensor_tensor(v, v, second(r, w), ALU.add)
                            off += r * w
                        link(t)
                        off = 0
                        for a, r, w in PAIRS:
                            nc.vector.tensor_reduce(th[:, :, a:a + r], rows(cand, off, r, w), AX, ALU.min)
                            off += r * w
                    elif part == 6:
                        nc.vector.tensor_tensor(e1, top[:, 0], bc(top[:, 0, :, 0:1], TOPK), ALU.subtract)
                        nc.vector.tensor_tensor(left, s2, bc(top[:, 1, :, 0:1], NK), ALU.subtract)
                        link(nc.vector.tensor_copy(zsum[:].unsqueeze(2), best[:, :, 0:1]))
                        nc.vector.tensor_copy(key_row, idx)
                        nc.vector.tensor_tensor(best[:], best[:], bc(zsum[:].unsqueeze(2), TOPK),
                                                ALU.subtract).then_inc(subbed, 1)
                    else:
                        dve.wait_ge(exped, b + 1)
                        link(nc.vector.tensor_reduce(zsum[:], best[:], AX, ALU.add))
                        link(nc.vector.reciprocal(zsum[:], zsum[:]))
                        nc.vector.tensor_tensor(e1, e1, bc(zsum[:].unsqueeze(2), TOPK), ALU.mult).then_inc(r1_row, 1)

                def mask(b, e):
                    if NS * b + e >= 2:
                        pb, pe_ = divmod(NS * b + e - 2, NS)
                        banks.wait_full(dve, ("r2T", pb, pe_, JS // 4 - 1))
                    nc.vector.tensor_tensor(r2[:, e % 2].rearrange("p (h a) j -> p h a j", h=PH),
                                            m.s[:, b, 1, :, e * JS:(e + 1) * JS].unsqueeze(2)
                                            .broadcast_to([P, PH, TOPK, JS]),
                                            theta[:, b % 2].unsqueeze(3).broadcast_to([P, PH, TOPK, JS]),
                                            ALU.is_ge).then_inc(masked, 1)

                def split_u(b, e):
                    for n in early(b, e):
                        dve.wait_ge(u_hi, n + 1)
                        u_low(nc.vector, n).then_inc(u_lo, 1)

                for part in range(8):
                    prepare(0, part)
                dve.wait_ge(iota_made, 1)
                mask(0, 0)
                mask(0, 1)
                dve.wait_ge(u_lo, FIRST)
                for b in range(TB):
                    for e in range(-1, 2):
                        split_u(b, e)
                    for e in range(2, NS):
                        if b + 1 < TB and e < 7:
                            prepare(b + 1, e - 2)
                        mask(b, e)
                        split_u(b, e)
                        if e == 2:
                            banks.wait_full(dve, ("small", b))
                            if b:
                                dve.wait_ge(r1_pool, 16 * b)
                            nc.vector.tensor_copy(smallT[:].rearrange("p i t -> p (i t)"),
                                                  banks.bank(("small", b))[:, 0:2 * P]).then_inc(banks.taken["dve"], 1)
                    banks.wait_taken(dve, ("small", b))
                    for k in range(P // 4):
                        if b + 1 < TB:
                            if k == RING // 4:
                                for part in range(5, 7):
                                    prepare(b + 1, part)
                            elif k == 2 * RING // 4:
                                prepare(b + 1, 7)
                                mask(b + 1, 0)
                            elif k == 4 * RING // 4:
                                mask(b + 1, 1)
                        wait_ring(dve, b, k)
                        for i in range(3 if k % 2 else 4):
                            ins = one_hot(nc.vector, b, 4 * k + i)
                        ins.then_inc(r1_ready, 1)


def experts(nc, m, ps, sem, u_in, u_t, v, gates, gelus, h_dram, out):
    NU, NV, NGE = 2, 4, 2
    BODY = 2 * GT
    NM = (NK - EARLY) // BODY
    NT = NK // BODY
    acc_in = sem("acc_in")
    v_in = [sem(f"v_in{i}") for i in range(NV)]
    g_in = sem("gates_in")
    ge_in = [sem(f"gelu_in{i}") for i in range(NGE)]
    u_hi_ready, u_ready, v_hi_ready, v_ready = (sem(n) for n in ("u_hi_ready", "u_ready", "v_hi_ready", "v_ready"))
    up_done, gelu_done, gated, gate_f, gate_hi = (sem(n) for n in ("up_done", "gelu_done", "gated", "gate_f", "gate_hi"))
    down_done, added, out_done = sem("down_done"), sem("added"), sem("out_stored")
    bank_up = ps[0:2]
    bank_down = ps[2:6]
    v_rows = v[0].rearrange("(i j) d -> j i d", j=NK)

    f = lambda ap: ap.bitcast(F32)
    with ExitStack() as ctx:
        sb = m.mem.local(ctx)
        acc = sb("acc_out", [P, TB, D])
        u_raw = m.u_raw
        v_raw = sb("v_raw", [P, NV, D])
        uh = sb("u_hi", [P, 2, D], F32R)
        ul = sb("u_lo", [P, 2, D], F32R)
        vh = sb("v_hi", [P, BODY, D], F32R)
        vl = sb("v_lo", [P, BODY, D], F32R)
        gt = sb("gate_tiles", [P, T, GJ])
        ge = sb("gelu_tile", [P, 2, T])
        af = sb("act_tile", [P, T])
        ah = sb("act_hi", [P, BODY, T], F32R)
        al = sb("act_lo", [P, BODY, T], F32R)
        with nc.Block() as block:
            @block.sync
            def _(sp):
                def load_u(n, slot):
                    sp.dma_start(u_raw[:, slot, :], u_t[bass.ds(n, 1)].rearrange("o p d -> p (o d)")
                                 ).then_inc(u_in[slot], 16)

                def load_v(n, slot):
                    sp.dma_start(v_raw[:, slot, :], v_rows[bass.ds(n, 1)].rearrange("o p d -> p (o d)")
                                 ).then_inc(v_in[slot], 16)

                def load_gates(it):
                    sp.dma_start(gt[:], gates[bass.ds(it, 1)].rearrange("o i t j -> i (o t) j")
                                 ).then_inc(g_in, 16)

                def body(it, u_left=BODY, last=False):
                    for half in range(2):
                        for q in range(GT):
                            jj = half * GT + q
                            n = it * BODY + jj
                            if jj < u_left:
                                sp.wait_ge(u_ready, n + 1)
                                load_u(n + NU, jj % NU)
                        if half and not last:
                            sp.wait_ge(gated, (it + 1) * BODY)
                            load_gates(it + 1)
                        for q in range(GT):
                            jj = half * GT + q
                            if not (last and jj + NV >= BODY):
                                sp.wait_ge(v_ready, it * BODY + jj + 1)
                                load_v(it * BODY + jj + NV, jj % NV)

                def late(it):
                    last = it == NT - 1
                    for half in range(2):
                        for q in range(GT):
                            jj = half * GT + q
                            n = it * BODY + jj
                            sp.wait_ge(gated, n - NGE + 1)
                            sp.dma_start(ge[:, jj % NGE, :], gelus[n - NM * BODY]).then_inc(ge_in[jj % NGE], 16)
                        if half and not last:
                            sp.wait_ge(gated, (it + 1) * BODY)
                            load_gates(it + 1)
                        for q in range(GT):
                            jj = half * GT + q
                            if not (last and jj + NV >= BODY):
                                sp.wait_ge(v_ready, it * BODY + jj + 1)
                                load_v(it * BODY + jj + NV, jj % NV)

                def first_body():
                    for n in range(6):
                        sp.wait_ge(u_ready, n + 1)
                        load_u(n + NU, n % NU)
                        if n == 1:
                            load_gates(0)
                        elif n >= 2:
                            load_v(n - 2, n - 2)
                    sp.dma_start(acc[:], h_dram).then_inc(acc_in, 16)
                    for n in range(GT):
                        sp.wait_ge(v_ready, n + 1)
                        load_v(n + NV, n)
                    for n in range(6, BODY):
                        sp.wait_ge(u_ready, n + 1)
                        load_u(n + NU, n % NU)
                    sp.wait_ge(gated, BODY)
                    load_gates(1)
                    for n in range(GT, BODY):
                        sp.wait_ge(v_ready, n + 1)
                        load_v(n + NV, n % NV)

                first_body()
                with sp.Fori(1, NM - 1) as it:
                    body(it)
                body(NM - 1, u_left=BODY - NU)
                for it in range(NM, NT):
                    late(it)
                sp.wait_ge(added, 8 * NG)
                sp.dma_start(out[0].rearrange("(b p) d -> p b d", p=P), acc[:]).then_inc(out_done, 16)
                sp.wait_ge(out_done, 16)

            @block.tensor
            def _(pe):
                def up(it, jj):
                    n = it * BODY + jj
                    pe.wait_ge(u_ready, n + 1)
                    if not (isinstance(it, int) and it == 0 and jj < 2):
                        pe.wait_ge(gelu_done, n - 1)
                    q, bank = jj % 2, bank_up[jj % 2]
                    for k in range(KD):
                        w = slice(k * P, (k + 1) * P)
                        nc.tensor.matmul(bank[:], uh[:, q, w], m.xh[:, k, :], start=(k == 0), stop=False)
                        nc.tensor.matmul(bank[:], uh[:, q, w], m.xl[:, k, :], start=False, stop=False)
                        t = nc.tensor.matmul(bank[:], ul[:, q, w], m.xh[:, k, :], start=False, stop=(k == KD - 1))
                    t.then_inc(up_done, 1)

                def down(g, half, first):
                    pe.wait_ge(gated, GT * (g + 1))
                    pe.wait_ge(v_ready, GT * (g + 1))
                    for o in range(8):
                        b, dh = o // 2, o % 2
                        if not (first and o < 4):
                            pe.wait_ge(added, 8 * g + o - 3)
                        bank = bank_down[o % 4]
                        for e in range(GT):
                            s = half * GT + e
                            w, c = slice(b * P, (b + 1) * P), slice(dh * T, (dh + 1) * T)
                            nc.tensor.matmul(bank[:], ah[:, s, w], vh[:, s, c], start=(e == 0), stop=False)
                            nc.tensor.matmul(bank[:], ah[:, s, w], vl[:, s, c], start=False, stop=False)
                            t = nc.tensor.matmul(bank[:], al[:, s, w], vh[:, s, c], start=False, stop=(e == GT - 1))
                        t.then_inc(down_done, 1)

                def body(it):
                    for half in range(2):
                        for q in range(GT):
                            up(it, half * GT + q)
                        if half or not isinstance(it, int):
                            down(it * 2 + half - 1, 1 - half, isinstance(it, int))
                body(0)
                with pe.Fori(1, NM) as it:
                    body(it)
                for g in range(2 * NM - 1, NG):
                    down(g, g % 2, False)

            @block.scalar
            def _(act):
                def split_u(it, jj):
                    n = it * BODY + jj
                    act.wait_ge(u_in[jj % NU], 16 * (it * (BODY // NU) + jj // NU + 1))
                    if not (isinstance(it, int) and it == 0 and jj < 2):
                        act.wait_ge(up_done, n - 1)
                    nc.scalar.activation(uh[:, jj % 2, :], u_raw[:, jj % NU, :], ACT.Copy).then_inc(u_hi_ready, 1)

                def split_v(it, half):
                    for q in range(GT):
                        jj = half * GT + q
                        act.wait_ge(v_in[jj % NV], 16 * (it * (BODY // NV) + jj // NV + 1))
                        if not (isinstance(it, int) and it == 0) and q == 0:
                            act.wait_ge(down_done, 8 * (it * 2 + half - 1))
                        nc.scalar.activation(vh[:, jj, :], v_raw[:, jj % NV, :], ACT.Copy).then_inc(v_hi_ready, 1)

                def body(it, last=False):
                    for half in range(2):
                        for q in range(GT):
                            jj = half * GT + q
                            n = it * BODY + jj
                            act.wait_ge(up_done, n + 1)
                            if not (isinstance(it, int) and it == 0 and jj < 2):
                                act.wait_ge(gated, n - 1)
                            nc.scalar.activation(ge[:, jj % 2, :], bank_up[jj % 2][:], ACT.Gelu).then_inc(gelu_done, 1)
                            if jj + 2 < BODY:
                                split_u(it, jj + 2)
                            elif not last:
                                split_u(it + 1, jj + 2 - BODY)
                        split_v(it, half)

                split_u(0, 0)
                split_u(0, 1)
                body(0)
                with act.Fori(1, NM - 1) as it:
                    body(it)
                body(NM - 1, last=True)
                for it in range(NM, NT):
                    for half in range(2):
                        split_v(it, half)

            @block.vector
            def _(dve):
                def split_u(it, jj):
                    n = it * BODY + jj
                    dve.wait_ge(u_hi_ready, n + 1)
                    nc.vector.tensor_tensor(ul[:, jj % 2, :], u_raw[:, jj % NU, :], f(uh[:, jj % 2, :]),
                                            ALU.subtract).then_inc(u_ready, 1)

                def add(g, o):
                    dve.wait_ge(down_done, 8 * g + o + 1)
                    v_ = acc[:, o // 2, (o % 2) * T:(o % 2 + 1) * T]
                    nc.vector.tensor_tensor(v_, v_, bank_down[o % 4][:], ALU.add).then_inc(added, 1)

                def gate(it, jj):
                    n = it * BODY + jj
                    if not (isinstance(it, int) and it == 0 and jj == 0):
                        dve.wait_ge(gated, n)
                    nc.vector.tensor_tensor(af[:], ge[:, jj % 2, :], gt[:, :, jj],
                                            ALU.mult).then_inc(gate_f, 1)
                    dve.wait_ge(gate_f, n + 1)
                    nc.vector.tensor_scalar(ah[:, jj, :], af[:], 1.0, None, ALU.mult
                                            ).then_inc(gate_hi, 1)
                    dve.wait_ge(gate_hi, n + 1)
                    nc.vector.tensor_tensor(al[:, jj, :], af[:], f(ah[:, jj, :]),
                                            ALU.subtract).then_inc(gated, 1)

                def body(it, last=False, late=False):
                    zero = isinstance(it, int) and it == 0
                    for half in range(2):
                        for q in range(GT):
                            jj = half * GT + q
                            n = it * BODY + jj
                            if late:
                                dve.wait_ge(ge_in[jj % NGE], 16 * ((n - NM * BODY) // NGE + 1))
                            else:
                                dve.wait_ge(gelu_done, n + 1)
                            if jj == 0:
                                dve.wait_ge(g_in, 16 * (it + 1))
                            if not zero and q == 0:
                                dve.wait_ge(down_done, 8 * (it * 2 + half - 1))
                            gate(it, jj)
                            if late:
                                pass
                            elif jj + 2 < BODY:
                                split_u(it, jj + 2)
                            elif not last:
                                split_u(it + 1, jj + 2 - BODY)
                        if zero and half:
                            dve.wait_ge(acc_in, 16)
                        for q in range(GT):
                            jj = half * GT + q
                            n = it * BODY + jj
                            dve.wait_ge(v_hi_ready, n + 1)
                            nc.vector.tensor_tensor(vl[:, jj, :], v_raw[:, jj % NV, :], f(vh[:, jj, :]),
                                                    ALU.subtract).then_inc(v_ready, 1)
                            if half or not zero:
                                add(it * 2 + half - 1, 2 * q)
                                add(it * 2 + half - 1, 2 * q + 1)
                split_u(0, 0)
                split_u(0, 1)
                body(0)
                with dve.Fori(1, NM - 1) as it:
                    body(it)
                body(NM - 1, last=True)
                for it in range(NM, NT):
                    body(it, late=True)
                for o in range(8):
                    add(NG - 1, o)


def hybrid_layer(nc, a, out):
    gates = nc.dram_tensor("gates", [NK // GJ, NK, T, GJ], F32, kind="Internal").ap()
    gelus = nc.dram_tensor("early_gelus", [EARLY, P, T], F32, kind="Internal").ap()
    h_dram = nc.dram_tensor("h_spill", [P, TB, D], F32, kind="Internal").ap()
    with ExitStack() as ctx:
        sem = lambda name: ctx.enter_context(nc.semaphore(name))
        ps = [ctx.enter_context(nc.psum_tensor(f"bank{i}", [P, 512], F32)) for i in range(8)]
        mem = Memory(nc)
        m = Tensors()
        m.mem = mem
        m.ident = mem.take("ident", [P, P])
        m.neg_half = mem.take("neg_half", [P, 1])
        m.upper = mem.take("upper", [P, P])
        m.lower = mem.take("lower", [P, P])
        m.chunk_ones = mem.take("chunk_ones", [P, P])
        m.blockdiag = mem.take("blockdiag", [P, 6, P])
        m.levels = mem.take("levels", [P, 6, P])
        m.att_mask = mem.take("att_mask", [P, 2 * P])
        m.kva = mem.take("kva", [P, TB, 2 * KVW])
        m.z = mem.take("z", [P, TB, DNW])
        m.ab = mem.take("ab", [P, TB, 2 * DN])
        m.qa = mem.take("qa", [P, TB, ATT])
        m.g = mem.take("g", [P, TB, DN])
        m.beta = mem.take("beta", [P, TB, DN])
        m.tok = mem.take("tok", [P, CT, T])
        m.unitT = mem.take("unitT", [P, 2 * DN, T])
        m.attqT = mem.take("attqT", [P, GRP, T])
        m.attkT = mem.take("attkT", [P, T])
        input_projection(nc, m, ps, sem, a["x"], a["norm_mix_g"], a["w_in"], a["dn_conv_w"], a["dn_a_log"],
                         a["dn_dt_bias"], a["att_q_norm_g"], a["att_k_norm_g"])
        mem.drop("qa", "ab")
        m.wT = mem.take("wT", [P, TB, DN, P])
        m.u = mem.take("u", [P, TB, DN, P])
        m.qkT = mem.take("qkT", [P, TB, DN, P])
        m.qdT = mem.take("qdT", [P, TB, DN, P])
        m.kdec = mem.take("kdec", [P, DN, T])
        m.egrow = mem.take("egrow", [P, TB, DN, P])
        delta_prepare(nc, m, ps, sem)
        mem.drop("tok", "unitT", "g", "beta", "upper", "lower", "chunk_ones", "blockdiag", "levels")
        m.mix = mem.take("mix", [P, TB, D])
        m.s = mem.take("scores", [P, TB, 2, PH, NK], at_end=True)
        raw = m.s[:].rearrange("p b q h n -> p (b q h n)").rearrange("p (i k n) -> p i k n", i=2, k=KD)
        m.w_raw = [raw[:, 0], raw[:, 1]]
        w_out_in = [sem("w_out_in0"), sem("w_out_in1")]
        mixers(nc, m, ps, sem, w_out_in, a["w_out"], a["att_sinks"], a["att_out_norm_g"], a["dn_out_norm_g"])
        mem.drop("kva", "z", "wT", "u", "qkT", "qdT", "kdec", "egrow", "attqT", "attkT", "att_mask")
        m.acc = mem.take("acc", [P, TB, D])
        m.xh = mem.take("x_hi", [P, KD, T], F32R, at_end=True)
        m.xl = mem.take("x_lo", [P, KD, T], F32R, at_end=True)
        m.u_raw = mem.take("u_raw", [P, 2, D])
        early_u_in, u_in = [[sem(f"{name}{i}") for i in range(2)] for name in ("early_u_in", "u_in")]
        output_projection(nc, m, ps, sem, w_out_in, early_u_in, a["peer_u"], a["x"], a["norm_ffn_g"], a["peer_w_q"], a["peer_sub_keys"], h_dram)
        mem.drop("mix", "acc")
        routing(nc, m, ps, sem, early_u_in, u_in, a["peer_u"], gates, gelus)
        mem.drop("scores")
        experts(nc, m, ps, sem, u_in, a["peer_u"], a["peer_v"], gates, gelus, h_dram, out)


def kernel(**inputs):
    import numpy as np
    import concourse.bacc as bacc
    from concourse.bass_utils import run_bass_kernel_spmd

    a = {name: np.asarray(value) for name, value in inputs.items()}
    a["dn_conv_w"] = a["dn_conv_w"][0].reshape(TAPS, CT, P).transpose(2, 0, 1).reshape(P, TAPS * CT)
    a["peer_sub_keys"] = a["peer_sub_keys"][0].transpose(1, 3, 0, 2).reshape(P, PH * NK)
    a["peer_u"] = a["peer_u"][0].reshape(NK, NK, KD, P).transpose(1, 3, 2, 0).reshape(NK, P, D)
    nc = bacc.Bacc("TRN2", target_bir_lowering=False, num_devices=1)
    arrays, aps = {}, {}
    for name, value in a.items():
        value = np.ascontiguousarray(value)
        arrays["in_" + name] = value
        aps[name] = nc.dram_tensor("in_" + name, value.shape, mybir.dt.from_np(value.dtype),
                                   kind="ExternalInput").ap()
    out = nc.dram_tensor("out_0", (1, T, D), F32, kind="ExternalOutput").ap()
    hybrid_layer(nc, aps, out)
    r = run_bass_kernel_spmd(nc, [arrays], core_ids=[0])
    return r.results[0]["out_0"]
```
